# Optimizing a Trainium2 kernel written in Bass

```python
import math
import jax, jax.numpy as jnp
from jax import lax
import numpy as np

D_MODEL = 1024
BATCH = 1
SEQ = 256
DEPTH = 1

N_META = 16
S5_GROUP = 16
S5_GROUPS = 32
S5_WIDTH = S5_GROUP * S5_GROUPS
S5_STATE = 64
DT_MIN = 0.001
DT_MAX = 0.1
HG_HEADS = 4
HG_HEAD_DIM = 128
HG_WIDTH = HG_HEADS * HG_HEAD_DIM
CHUNK = 64
N_BRANCH = 2
IN_WIDTH = S5_WIDTH + 4 * HG_WIDTH + N_BRANCH * D_MODEL
IN_SPLITS = (S5_WIDTH, S5_WIDTH + HG_WIDTH, S5_WIDTH + 2 * HG_WIDTH,
             S5_WIDTH + 3 * HG_WIDTH, S5_WIDTH + 4 * HG_WIDTH)
N_EXPERTS = 32
TOP_K = 4
D_EXPERT = D_MODEL
SWIGLU_ALPHA = 1.702
SWIGLU_LIMIT = 7.0
MOE_BLOCK = 256
EPS = 1e-6

kernel_name = "hybrid_s5_hgrn2_moe_meta"

def rmsnorm(x, gain):
    x32 = x.astype(jnp.float32)
    y = x32 * lax.rsqrt(jnp.mean(x32 * x32, axis=-1, keepdims=True) + EPS)
    return (y * gain.astype(jnp.float32)).astype(x.dtype)

def s5_mixer(u, lam_re, lam_im, log_dt, b_re, b_im, c_re, c_im, d_skip, w_glu):
    f32 = jnp.float32
    bsz, seq_len, _ = u.shape
    u32 = u.astype(f32).reshape(bsz, seq_len, S5_GROUPS, S5_GROUP)
    lam = lax.complex(lam_re.astype(f32), lam_im.astype(f32))
    dt = jnp.exp(log_dt.astype(f32))[:, None]
    lam_bar = jnp.exp(lam * dt)
    b_mat = lax.complex(b_re.astype(f32), b_im.astype(f32))
    b_bar = ((lam_bar - 1.0) / lam)[:, :, None] * b_mat
    bu = jnp.einsum('gph,blgh->blgp', b_bar, u32.astype(jnp.complex64))
    a = jnp.broadcast_to(lam_bar, bu.shape)

    def combine(left, right):
        a_l, b_l = left
        a_r, b_r = right
        return a_r * a_l, a_r * b_l + b_r

    _, states = lax.associative_scan(combine, (a, bu), axis=1)
    c_mat = lax.complex(c_re.astype(f32), c_im.astype(f32))
    y = jnp.real(jnp.einsum('ghp,blgp->blgh', c_mat, states)) + d_skip.astype(f32) * u32
    y = jax.nn.gelu(y.reshape(bsz, seq_len, S5_WIDTH))
    return y * jax.nn.sigmoid(y @ w_glu.astype(f32))

def hgrn2_mixer(q, fpre, v, g, lb, gn_gain):
    f32 = jnp.float32
    bsz, seq_len, _ = q.shape
    f = lb + (1.0 - lb) * jax.nn.sigmoid(fpre.astype(f32))
    logf = jnp.log(f)
    k = 1.0 - f
    q = jax.nn.silu(q.astype(f32))
    v = v.astype(f32)
    pad = CHUNK - N_META

    def to_chunks(t):
        t = jnp.pad(t, ((0, 0), (pad, 0), (0, 0)))
        n_chunks = t.shape[1] // CHUNK
        t = t.reshape(bsz, n_chunks, CHUNK, HG_HEADS, HG_HEAD_DIM)
        return t.transpose(1, 0, 3, 2, 4)

    qc, kc, vc, lc = to_chunks(q), to_chunks(k), to_chunks(v), to_chunks(logf)
    bc = jnp.cumsum(lc, axis=3)
    causal = jnp.tril(jnp.ones((CHUNK, CHUNK), dtype=bool))[:, :, None]

    def step(state, inp):
        qi, ki, vi, bi = inp
        diff = bi[:, :, :, None, :] - bi[:, :, None, :, :]
        decay = jnp.exp(jnp.where(causal, diff, -jnp.inf))
        scores = jnp.einsum('bhid,bhjd,bhijd->bhij', qi, ki, decay)
        o = scores @ vi + jnp.einsum('bhid,bhde->bhie', qi * jnp.exp(bi), state)
        b_last = bi[:, :, -1:, :]
        state = (jnp.exp(b_last[:, :, 0, :, None]) * state
                 + jnp.einsum('bhjd,bhje->bhde', ki * jnp.exp(b_last - bi), vi))
        return state, o

    s0 = jnp.zeros((bsz, HG_HEADS, HG_HEAD_DIM, HG_HEAD_DIM), f32)
    _, o = lax.scan(step, s0, (qc, kc, vc, bc))
    o = o.transpose(1, 0, 3, 2, 4).reshape(bsz, -1, HG_HEADS, HG_HEAD_DIM)[:, pad:]
    o = o * lax.rsqrt(jnp.mean(o * o, axis=-1, keepdims=True) + EPS)
    o = o.reshape(bsz, seq_len, HG_WIDTH) * gn_gain.astype(f32)
    return o * jax.nn.silu(g.astype(f32))

def moe(xn, w_router, b_router, w_gate_up, b_gate_up, w_down, b_down):
    f32 = jnp.float32
    bsz, seq_len, d = xn.shape
    tokens = xn.reshape(-1, d)
    n_tok = tokens.shape[0]
    logits = (tokens @ w_router + b_router).astype(f32)
    top_logits, top_idx = lax.top_k(logits, TOP_K)
    top_w = jax.nn.softmax(top_logits, axis=-1)

    n_assign = n_tok * TOP_K
    flat_e = top_idx.reshape(-1).astype(jnp.int32)
    flat_tok = jnp.repeat(jnp.arange(n_tok, dtype=jnp.int32), TOP_K)
    flat_w = top_w.reshape(-1)
    order = jnp.argsort(flat_e)
    sorted_e = flat_e[order]
    counts = jnp.bincount(flat_e, length=N_EXPERTS).astype(jnp.int32)
    padded = (counts + MOE_BLOCK - 1) // MOE_BLOCK * MOE_BLOCK
    padded_end = jnp.cumsum(padded)
    padded_start = padded_end - padded
    start = jnp.cumsum(counts) - counts
    rank = jnp.arange(n_assign, dtype=jnp.int32) - start[sorted_e]
    dest = padded_start[sorted_e] + rank
    n_blocks = -(-n_assign // MOE_BLOCK) + N_EXPERTS
    n_rows = n_blocks * MOE_BLOCK
    row_tok = jnp.full((n_rows,), n_tok, dtype=jnp.int32).at[dest].set(flat_tok[order])
    row_w = jnp.zeros((n_rows,), f32).at[dest].set(flat_w[order])
    block_start = jnp.arange(n_blocks, dtype=jnp.int32) * MOE_BLOCK
    block_e = jnp.minimum(jnp.searchsorted(padded_end, block_start, side='right'), N_EXPERTS - 1)
    tokens_pad = jnp.concatenate([tokens, jnp.zeros((1, d), tokens.dtype)], axis=0)
    x_rows = tokens_pad[row_tok].reshape(n_blocks, MOE_BLOCK, d)

    def expert_block(args):
        xb, e = args
        gu = xb @ w_gate_up[e] + b_gate_up[e]
        gate = jnp.minimum(gu[:, ::2], SWIGLU_LIMIT)
        up = jnp.clip(gu[:, 1::2], -SWIGLU_LIMIT, SWIGLU_LIMIT)
        glu = gate * jax.nn.sigmoid(gate * SWIGLU_ALPHA)
        return ((up + 1.0) * glu) @ w_down[e] + b_down[e]

    y_rows = lax.map(expert_block, (x_rows, block_e)).reshape(n_rows, d)
    y = jax.ops.segment_sum(y_rows * row_w[:, None].astype(y_rows.dtype), row_tok,
                            num_segments=n_tok + 1)[:n_tok]
    return y.reshape(bsz, seq_len, d).astype(xn.dtype)

def setup_inputs(seed: int = 0) -> dict:
    key = jax.random.key(seed)
    ks = jax.random.split(key, 32)
    f32 = jnp.float32
    nrm = lambda k, shape, scale: jax.random.normal(k, shape, f32) * scale
    L_ = DEPTH
    x = jax.random.normal(ks[0], (BATCH, SEQ, D_MODEL), f32)
    meta_tokens = nrm(ks[1], (N_META, D_MODEL), 1.0)
    norm1_gain = 1.0 + nrm(ks[2], (L_, D_MODEL), 0.02)
    w_in = nrm(ks[3], (L_, D_MODEL, IN_WIDTH), D_MODEL ** -0.5)
    s5_lambda_re = -0.5 * jnp.exp(nrm(ks[4], (L_, S5_GROUPS, S5_STATE), 0.01))
    s5_lambda_im = (jnp.pi * jnp.arange(S5_STATE, dtype=f32))[None, None, :] + nrm(ks[5], (L_, S5_GROUPS, S5_STATE), 0.01)
    s5_log_dt = jax.random.uniform(ks[6], (L_, S5_GROUPS), f32, math.log(DT_MIN), math.log(DT_MAX))
    s5_b_re = nrm(ks[7], (L_, S5_GROUPS, S5_STATE, S5_GROUP), (2 * S5_GROUP) ** -0.5)
    s5_b_im = nrm(ks[8], (L_, S5_GROUPS, S5_STATE, S5_GROUP), (2 * S5_GROUP) ** -0.5)
    s5_c_re = nrm(ks[9], (L_, S5_GROUPS, S5_GROUP, S5_STATE), (2 * S5_STATE) ** -0.5)
    s5_c_im = nrm(ks[10], (L_, S5_GROUPS, S5_GROUP, S5_STATE), (2 * S5_STATE) ** -0.5)
    s5_d = nrm(ks[11], (L_, S5_GROUPS, S5_GROUP), 1.0)
    s5_w_glu = nrm(ks[12], (L_, S5_WIDTH, S5_WIDTH), S5_WIDTH ** -0.5)
    hgrn_lb_logits = nrm(ks[13], (L_ + 1, HG_WIDTH), 0.1)
    hgrn_norm_gain = 1.0 + nrm(ks[14], (L_, HG_WIDTH), 0.02)
    w_branch_s5 = nrm(ks[15], (L_, S5_WIDTH, D_MODEL), S5_WIDTH ** -0.5)
    w_branch_hgrn = nrm(ks[16], (L_, HG_WIDTH, D_MODEL), HG_WIDTH ** -0.5)
    w_out = nrm(ks[17], (L_, D_MODEL, D_MODEL), D_MODEL ** -0.5)
    norm2_gain = 1.0 + nrm(ks[18], (L_, D_MODEL), 0.02)
    w_router = nrm(ks[19], (L_, D_MODEL, N_EXPERTS), D_MODEL ** -0.5)
    b_router = nrm(ks[20], (L_, N_EXPERTS), 0.01)
    w_gate_up = nrm(ks[21], (L_, N_EXPERTS, D_MODEL, 2 * D_EXPERT), D_MODEL ** -0.5)
    b_gate_up = nrm(ks[22], (L_, N_EXPERTS, 2 * D_EXPERT), 0.01)
    w_down = nrm(ks[23], (L_, N_EXPERTS, D_EXPERT, D_MODEL), D_EXPERT ** -0.5)
    b_down = nrm(ks[24], (L_, N_EXPERTS, D_MODEL), 0.01)
    final_norm_gain = 1.0 + nrm(ks[25], (D_MODEL,), 0.02)
    return {"x": x, "meta_tokens": meta_tokens, "norm1_gain": norm1_gain, "w_in": w_in,
            "s5_lambda_re": s5_lambda_re, "s5_lambda_im": s5_lambda_im, "s5_log_dt": s5_log_dt,
            "s5_b_re": s5_b_re, "s5_b_im": s5_b_im, "s5_c_re": s5_c_re, "s5_c_im": s5_c_im,
            "s5_d": s5_d, "s5_w_glu": s5_w_glu, "hgrn_lb_logits": hgrn_lb_logits,
            "hgrn_norm_gain": hgrn_norm_gain, "w_branch_s5": w_branch_s5, "w_branch_hgrn": w_branch_hgrn,
            "w_out": w_out, "norm2_gain": norm2_gain, "w_router": w_router, "b_router": b_router,
            "w_gate_up": w_gate_up, "b_gate_up": b_gate_up, "w_down": w_down, "b_down": b_down,
            "final_norm_gain": final_norm_gain}

def reference(x, meta_tokens, norm1_gain, w_in, s5_lambda_re, s5_lambda_im, s5_log_dt,
              s5_b_re, s5_b_im, s5_c_re, s5_c_im, s5_d, s5_w_glu, hgrn_lb_logits,
              hgrn_norm_gain, w_branch_s5, w_branch_hgrn, w_out, norm2_gain, w_router, b_router,
              w_gate_up, b_gate_up, w_down, b_down, final_norm_gain):
    f32 = jnp.float32
    bsz = x.shape[0]
    meta = jnp.broadcast_to(meta_tokens[None].astype(x.dtype), (bsz, N_META, D_MODEL))
    h = jnp.concatenate([meta, x], axis=1)
    lower_bounds = jnp.cumsum(jax.nn.softmax(hgrn_lb_logits.astype(f32), axis=0), axis=0)
    for l in range(DEPTH):
        xn = rmsnorm(h, norm1_gain[l])
        proj = xn @ w_in[l]
        u, q, fpre, v, og, gates = jnp.split(proj, IN_SPLITS, axis=-1)
        y_s5 = s5_mixer(u, s5_lambda_re[l], s5_lambda_im[l], s5_log_dt[l], s5_b_re[l], s5_b_im[l],
                        s5_c_re[l], s5_c_im[l], s5_d[l], s5_w_glu[l])
        y_hg = hgrn2_mixer(q, fpre, v, og, lower_bounds[l], hgrn_norm_gain[l])
        gate_s5, gate_hg = jnp.split(jax.nn.sigmoid(gates.astype(f32)), N_BRANCH, axis=-1)
        merged = (gate_s5 * (y_s5 @ w_branch_s5[l].astype(f32))
                  + gate_hg * (y_hg @ w_branch_hgrn[l].astype(f32)))
        h = h + merged.astype(h.dtype) @ w_out[l]
        h = h + moe(rmsnorm(h, norm2_gain[l]), w_router[l], b_router[l], w_gate_up[l],
                    b_gate_up[l], w_down[l], b_down[l])
    y = rmsnorm(h, final_norm_gain)[:, N_META:]
    return y


_drawn_inputs = setup_inputs


def setup_inputs(seed=0):
    import zlib

    import numpy as np

    out = dict(_drawn_inputs(seed))
    spreads = {}
    factors = {'s5_lambda_re': 200.0,
     'hgrn_lb_logits': 3.065,
     'hgrn_norm_gain': 2.841,
     'b_gate_up': 8.0,
     'b_down': 8.0,
     'final_norm_gain': 21.922,
     's5_lambda_im': 27.776,
     's5_log_dt': 31.496,
     's5_b_re': 34.928,
     's5_b_im': 52.752,
     's5_c_re': 27.056,
     's5_c_im': 25.032}
    for name, (base, spread) in spreads.items():
        noise = np.random.default_rng([zlib.crc32(name.encode()), seed]).standard_normal(out[name].shape)
        drawn = base * np.exp(spread * noise) if base else spread * noise
        out[name] = __import__('jax').numpy.asarray(drawn.astype(out[name].dtype))
    for name, factor in factors.items():
        out[name] = (out[name] * factor).astype(out[name].dtype)
    return out
```

```python
from contextlib import ExitStack

import numpy as np
import concourse.bass as bass
from concourse import mybir

F32 = mybir.dt.float32
I32 = mybir.dt.int32
U32 = mybir.dt.uint32
ALU = mybir.AluOpType
ACT = mybir.ActivationFunctionType
AX = mybir.AxisListType.X

P = 128
META, SEQ = 16, 256
TOK = META + SEQ
D = 1024
KD = D // P
W5 = 512
KW = W5 // P
HEADS = 4
STATES = 32 * 64
ST = STATES // P
TT = SEQ // P
E = 32
TOPK = 4
SLOTS = 64
EXTRA = 16
ITEMS = E + EXTRA
PIECES = 12
PC = 2048
EPS = 1e-6
LEVELS = [64, 32, 16, 8, 4, 2, 1]
MAGIC = 1.5 * 2.0 ** 23
TWO_PI = 6.2831850
GELU_C = 2 * 0.7978845608028654

C_ID, C_TRI, C_MASK = 0, P, 2 * P
C_T = C_MASK + len(LEVELS) * 64
C_IE = C_T + TOK
C_IS = C_IE + E
C_GC = C_IS + SLOTS
C_GB = C_GC + 2
C_PI = C_GB + 2
C_ALL = C_PI + 1


def shape_constants():
    c = np.zeros((P, C_ALL), np.float32)
    p = np.arange(P)
    c[:, C_ID:C_ID + P] = np.eye(P)
    c[:, C_TRI:C_TRI + P] = p[:, None] < p[None, :]
    for n, m in enumerate(LEVELS):
        i = np.array([b * 2 * m + m + r for b in range(64 // m) for r in range(m)])
        same = p[:, None] // (2 * m) == i[None, :] // (2 * m)
        left = p[:, None] % (2 * m) < m
        c[:, C_MASK + 64 * n:C_MASK + 64 * (n + 1)] = same & left
    c[:, C_T:C_T + TOK] = np.arange(TOK)
    c[:, C_IE:C_IE + E] = np.arange(E)
    c[:, C_IS:C_IS + SLOTS] = np.arange(SLOTS)
    for g in range(2):
        c[:, C_GC + g] = (p // 16) % 2 == g
        c[:, C_GB + g] = p // 64 == g
    c[:, C_PI] = p
    return c


def build(nc, a, out):
    with ExitStack() as ctx:
        def sb(name, shape, dt=F32):
            return ctx.enter_context(nc.sbuf_tensor(name, shape, dt))

        def sem(name):
            return ctx.enter_context(nc.semaphore(name))

        ring = sb("ring", [P, PIECES, PC])
        cst = sb("cst", [P, C_ALL])
        x = sb("x", [P, TT, D])
        xnT = sb("xnT", [P, KD, TOK])
        uT = sb("uT", [P, KW, TOK])
        v_a = sb("v_a", [P, TT, W5])
        v_m = sb("v_m", [META, W5])
        ogT = sb("ogT", [P, KW, SEQ])
        gates = sb("gates", [P, 2 * KD, SEQ])
        w_mix = sb("w_mix", [P, 10240])
        ones = sb("ones", [P, P])
        prow = sb("prow", [32, P])
        pcol = sb("pcol", [P, 32])
        s5c = sb("s5c", [P, 4, ST])
        blk = sb("blk", [P, 4, 4, P])
        small = sb("small", [P, 64])
        zero_c = sb("zero_c", [P, 4])
        rout = sb("rout", [P, 1400])
        ix = sb("ix", [P, TT, 8], U32)
        idx = sb("idx", [1, ITEMS + 2], I32)

        def at(t, lo, *dims):
            n = int(np.prod(dims))
            v = t[:, lo:lo + n]
            if len(dims) == 1:
                return v
            names = "abcd"[:len(dims)]
            return v.rearrange("p (%s) -> p %s" % (" ".join(names), " ".join(names)),
                               **{k: d for k, d in zip(names, dims)})

        ringf = ring[:, :, :].rearrange("p a b -> p (a b)")
        ident = cst[:, C_ID:C_ID + P]
        tri = cst[:, C_TRI:C_TRI + P]
        steps = cst[:, C_T:C_T + TOK]
        iota_e = cst[:, C_IE:C_IE + E]
        iota_s = cst[:, C_IS:C_IS + SLOTS]
        win = [at(ringf, s * 4096, KD, 512) for s in range(2)]
        qT = at(ringf, 4 * PC, KW, SEQ)
        kT = at(ringf, 4 * PC + 1024, KW, TOK)
        bT = at(ringf, 4 * PC + 2112, KW, TOK)
        xmn = ringf[0:META, 4 * PC:4 * PC + D]
        xm = ringf[0:META, 4 * PC + 1024:4 * PC + 1024 + D]
        s5r = at(ringf[0:ST], 4 * PC + 2112, 8, P)
        s5q = at(ringf[0:ST], 4 * PC + 3136, 3, P)
        B0 = 6 * PC
        NT = TOK
        turns = at(ringf, B0, NT)
        rnd = at(ringf, B0 + NT, NT)
        absf = at(ringf, B0 + 2 * NT, NT)
        frac = [at(ringf, B0 + (3 + i) * NT, NT) for i in range(2)]
        sinT = [at(ringf, B0 + (5 + i) * NT, NT) for i in range(2)]
        cosT = [at(ringf, B0 + (7 + i) * NT, NT) for i in range(2)]
        rot = [at(ringf, B0 + (9 + i) * NT, NT) for i in range(4)]
        zre = at(ringf, B0 + 13 * NT, NT)
        zim = at(ringf, B0 + 14 * NT, NT)
        xre = [at(ringf, B0 + (15 + i) * NT, NT) for i in range(2)]
        xim = [at(ringf, B0 + (17 + i) * NT, NT) for i in range(2)]
        H0 = B0 + 19 * NT
        bre = at(ringf, H0, ST, 16)
        bim = at(ringf, H0 + 256, ST, 16)
        bb = [at(ringf, H0 + 512 + 256 * i, ST, 16) for i in range(4)]
        bz = at(ringf, H0 + 1536, 2, 4, P)
        cn = at(ringf, H0 + 2560, 2, 4, 64)
        cz = at(ringf, H0 + 3072, 2, 4, P)
        xs = at(ringf, H0 + 4096, D)
        xs2 = at(ringf, H0 + 5120, D)
        junk = at(ringf, H0 + 6144, 976)
        M0 = B0
        y5 = at(ringf, M0, KW, SEQ)
        yt = at(ringf, M0 + 1024, KW, SEQ)
        g5 = at(ringf, M0 + 2048, KW, SEQ)
        fT = at(ringf, M0 + 3072, KW, TOK)
        sg = at(ringf, M0 + 4160, KW, SEQ)
        bc = at(ringf, M0 + 5184, 1024)
        kc = at(ringf, M0 + 6208, 1024)
        dec = at(ringf, M0 + 7232, 1024)
        qk = at(ringf, M0 + 8256, 1024)
        stot = at(ringf, M0 + 9280, 8, P)
        tmpl = at(ringf, M0 + 10304, 8, 64)
        qe = at(ringf, M0 + 3072, 1024)
        kh = at(ringf, M0 + 10816, KW, 144)
        eb = at(ringf, M0 + 1024, 1024)
        khT = at(ringf, M0 + 4160, KW, P)
        khTm = ringf[0:META, M0 + 4672:M0 + 4672 + W5]
        st0 = at(ringf, M0 + 5184, KW, P)
        st1 = at(ringf, M0 + 5696, KW, P)
        o2 = at(ringf, M0 + 7232, 1024)
        yh = at(ringf, M0 + 8256, KW, SEQ)
        orn = at(ringf, M0 + 6208, 1024)
        w_out = at(ringf, 0, KD, D)
        mrg = xnT
        w_glu = at(w_mix, 0, KW, W5)
        w_b5 = at(w_mix, 2048, KW, D)
        w_bh = at(w_mix, 6144, KW, D)
        x2 = at(w_mix, 0, TT, D)
        x2T = at(w_mix, 2048, KD, SEQ)
        xgT = at(w_mix, 4096, KD, SLOTS)
        hT = at(w_mix, 4608, KD, SLOTS)
        yT = at(w_mix, 5120, KD, SLOTS)
        gt = at(w_mix, 5632, KD, SLOTS)
        sgm = at(w_mix, 6144, KD, SLOTS)
        up = at(w_mix, 6656, KD, SLOTS)
        ysl = w_mix[0:SLOTS, 7168:7168 + D]
        ctr = w_mix[0:SLOTS, 8192:8192 + SEQ]
        pick = at(w_mix, 8448, TT, SLOTS)
        pickw = at(w_mix, 8576, TT, SLOTS)
        bias = at(w_mix, 8704, ITEMS, 2 * KD)
        wrt = at(w_mix, 9472, KD, E)
        brt = w_mix[0:1, 9728:9728 + E]
        gatesf = gates[:, :, :].rearrange("p a b -> p (a b)")
        bgu = gatesf[0:E, 0:2 * D]
        bdn = gatesf[0:E, 2 * D:3 * D]
        fgain = gatesf[:, 3 * D:4 * D]

        ps = [ctx.enter_context(nc.psum_tensor(f"ps{i}", [P, 512], F32)) for i in range(8)]

        lg, ex, mask, slot, wt = ([rout[:, 64 * j + 32 * t:64 * j + 32 * t + E] for t in range(TT)] for j in range(5))
        mx = [rout[:, 320 + 8 * t:328 + 8 * t] for t in range(TT)]
        nmx = [rout[:, 336 + t:337 + t] for t in range(TT)]
        den = [rout[:, 338 + t:339 + t] for t in range(TT)]
        ixf = [rout[:, 340 + 4 * t:344 + 4 * t] for t in range(TT)]
        cnt, cx, first = (rout[0:E, 348 + j:349 + j] for j in range(3))
        neg = rout[0:E, 352:352 + P]
        oh = rout[0:E, 480:480 + ITEMS]
        ohc = rout[0:E, 528:528 + ITEMS]
        j3 = rout[0:E, 576:624]
        slT = rout[0:E, 640:640 + SEQ]
        wtT = rout[0:E, 896:896 + SEQ]
        islot = at(rout, 1152, TT, ITEMS)
        iwt = at(rout, 1248, TT, ITEMS)
        s = {}
        for n in """consts xload meta rows s5rows bload cload glu_w branch5_w branchh_w out_w expert_rows
                    router_w router_b lastgain win0 win1 out_stored
                    ones_set xs_ready xs_free turned_x xnT_ready turned_m xmT_ready
                    rows_turned cols_ready s5rows_turned s5cols_ready s5r_exp s5r_ang s5r_sin s5r_v
                    bz_ready b_turned b_laid c_turned c_laid
                    proj proj_free bu bu_free ph rounded sines scanned xs5 y_add ysum ydone
                    gelu_in gelu_sig g5_ready glu_mm glu_sig f_sig q_sig og_sig f_ready logf
                    kq_ready decay_in decay_out level_in level_mm level_used diag_mm
                    eb_in eb_out kh_in kh_exp kh_ready kh_turned khT_ready st_mm st0_ready st1_ready stot_ready
                    qe_ready o_mm o2_ready ms_mm yh_ready y5_ready gate_sig br_mm br_free mrg_ready wo_mm
                    h_ready x2_ready x2_turned x2T_ready logit_mm logits_in exped mask_ready
                    rank_mm slot_ready tr_mm cnt_ready start_mm oh_ready item_mm items_ready idx_ready
                    bias_mm bias_ready acc0_mm
                    pick_ready gathered xg_ready gu_mm gate_in gate_sg h_done down_mm yT_ready
                    ct_mm ct_ready yt_mm ysl_ready comb0 comb1 added0 added1 piece_used w_last
                    acol dch ach w_gate w_up w_pickw var_in root_out""".split():
            s[n] = sem(n)
        landed = [sem(f"landed{i}") for i in range(PIECES)]

        x_d = a["x"].rearrange("b (t p) d -> p (b t) d", p=P)
        win_d = a["w_in"].rearrange("l (k p) n -> p (l k) n", p=P)
        gu_d = a["w_gate_up"].rearrange("l e (k p) n -> p (l e k) n", p=P)
        dn_d = a["w_down"].rearrange("l e (k p) n -> p (l e k) n", p=P)
        GROUPS = [0, 2, 1, 3, 4, 5, 6, 7, 8]
        NG = len(GROUPS)

        def expert_piece(q, e, i):
            if i < KD:
                src = gu_d[:, bass.ds(e * KD + i, 1), :]
                dst = ring[:, i:i + 1, :]
            else:
                src = dn_d[:, bass.ds(e * KD + 2 * (i - KD), 2), :]
                dst = ring[:, i, :].rearrange("p (a n) -> p a n", a=2)
            q.dma_start(dst, src).then_inc(landed[i], 16)

        block = ctx.enter_context(nc.Block())

        @block.sync
        def _(sp):
            sp.dma_start(x[:, :, :], x_d).then_inc(s["xload"], 16)
            used = 0
            for n in range(NG):
                if n >= 2:
                    used += 3 if GROUPS[n - 2] == 3 else 4
                    sp.wait_ge(s["proj"], used)
                g = GROUPS[n]
                sp.dma_start(win[n % 2], win_d[:, :, g * 512:(g + 1) * 512]).then_inc(s["win%d" % (n % 2)], 16)
                if n == 2:
                    sp.dma_start(w_glu, a["s5_w_glu"].rearrange("l (k p) n -> p (l k) n", p=P)).then_inc(s["glu_w"], 16)
                if n == 4:
                    sp.dma_start(w_b5, a["w_branch_s5"].rearrange("l (k p) n -> p (l k) n", p=P)).then_inc(s["branch5_w"], 16)
                if n == 5:
                    sp.dma_start(w_bh, a["w_branch_hgrn"].rearrange("l (k p) n -> p (l k) n", p=P)).then_inc(s["branchh_w"], 16)
            sp.wait_ge(s["proj"], 4 * NG - 1)
            sp.dma_start(w_out, a["w_out"].rearrange("l (k p) n -> p (l k) n", p=P)).then_inc(s["out_w"], 16)
            sp.wait_ge(s["br_mm"], 16)
            for i in range(4, PIECES):
                expert_piece(sp, 0, i)
            sp.wait_ge(s["mrg_ready"], 4)
            sp.dma_start(bgu, a["b_gate_up"].rearrange("l e n -> (l e) n")).then_inc(s["expert_rows"], 16)
            sp.dma_start(bdn, a["b_down"].rearrange("l e n -> (l e) n")).then_inc(s["expert_rows"], 16)
            sp.dma_start(fgain, a["final_norm_gain"].rearrange("(o n) -> o n", o=1).to_broadcast([P, D])).then_inc(s["lastgain"], 16)
            sp.dma_start(wrt, a["w_router"].rearrange("l (k p) n -> p (l k) n", p=P)).then_inc(s["router_w"], 16)
            sp.dma_start(brt, a["b_router"]).then_inc(s["router_b"], 16)
            sp.wait_ge(s["wo_mm"], 4)
            for i in range(4):
                expert_piece(sp, 0, i)
            sp.wait_ge(s["idx_ready"], 1)
            n_items = sp.value_load(idx[0:1, ITEMS:ITEMS + 1], min_val=E, max_val=ITEMS - 1)
            with sp.Fori(1, n_items) as w:
                e = sp.value_load(idx[0:1, bass.ds(w, 1)], min_val=0, max_val=E - 1)
                for i in range(PIECES):
                    sp.wait_ge(s["piece_used"], (w - 1) * PIECES + i + 1)
                    expert_piece(sp, e, i)
            sp.wait_ge(s["w_last"], TT)
            for t in range(TT):
                sp.dma_start(out.rearrange("b (t p) d -> p (b t) d", p=P)[:, t, :], x2[:, t, :]).then_inc(s["out_stored"], 16)
            sp.wait_ge(s["out_stored"], 16 * TT)

        @block.gpsimd
        def _(pool):
            nc.gpsimd.memset(ones[:, :], 1.0).then_inc(s["ones_set"], 1)

        @block.scalar
        def _(act):
            n_ach = [0]

            def link(ins):
                n_ach[0] += 1
                ins.then_inc(s["ach"], 1)
                act.wait_ge(s["ach"], n_ach[0])

            def f(o, i, fn, **k):
                return nc.scalar.activation(o, i, fn, **k)

            act.dma_start(cst[:, :], a["shape_consts"]).then_inc(s["consts"], 16)
            act.dma_start(xm[:, :], a["meta_tokens"]).then_inc(s["meta"], 16)
            pr = lambda n, k: a[n].rearrange("l (k p) -> (l k) p", p=P)
            act.dma_start(prow[0:8, :], pr("norm1_gain", 8)).then_inc(s["rows"], 16)
            act.dma_start(prow[8:16, :], pr("norm2_gain", 8)).then_inc(s["rows"], 16)
            act.dma_start(prow[16:24, :], pr("hgrn_lb_logits", 8)).then_inc(s["rows"], 16)
            act.dma_start(prow[24:28, :], pr("hgrn_norm_gain", 4)).then_inc(s["rows"], 16)
            act.dma_start(prow[28:32, :], a["s5_d"].rearrange("l (k g) h -> (l k) (g h)", k=4)).then_inc(s["rows"], 16)
            act.dma_start(s5r[:, 0, :], a["s5_lambda_re"].rearrange("l (i g) p -> (l i) (g p)", g=2)).then_inc(s["s5rows"], 16)
            act.dma_start(s5r[:, 1, :], a["s5_lambda_im"].rearrange("l (i g) p -> (l i) (g p)", g=2)).then_inc(s["s5rows"], 16)
            act.dma_start(small[0:ST, 0:2], a["s5_log_dt"].rearrange("l (i g) -> (l i) g", g=2)).then_inc(s["s5rows"], 16)
            act.dma_start(bre, a["s5_b_re"].rearrange("l (i g) p h -> (g p) (l i) h", g=2)).then_inc(s["bload"], 16)
            act.dma_start(bim, a["s5_b_im"].rearrange("l (i g) p h -> (g p) (l i) h", g=2)).then_inc(s["bload"], 16)
            act.dma_start(cn[:, 0], a["s5_c_re"].rearrange("l (t g) h p -> (g h) (l t) p", t=4)).then_inc(s["cload"], 16)
            act.dma_start(cn[:, 1], a["s5_c_im"].rearrange("l (t g) h p -> (g h) (l t) p", t=4)).then_inc(s["cload"], 16)

            act.wait_ge(s["s5rows"], 48)
            f(small[0:ST, 2:4], small[0:ST, 0:2], ACT.Exp).then_inc(s["s5r_exp"], 1)
            act.wait_ge(s["s5r_v"], 1)
            f(s5r[:, 4, :], s5r[:, 2, :], ACT.Exp).then_inc(s["s5r_exp"], 1)
            act.wait_ge(s["s5r_ang"], 1)
            f(s5r[:, 6, :], s5r[:, 5, :], ACT.Sin, scale=TWO_PI).then_inc(s["s5r_sin"], 1)
            f(s5r[:, 7, :], s5r[:, 5, :], ACT.Sin, scale=TWO_PI / 2).then_inc(s["s5r_sin"], 1)

            def root(n, v):
                act.wait_ge(s["var_in"], n)
                f(v, v, ACT.Sqrt).then_inc(s["root_out"], 1)

            root(1, small[:, 4:6])
            root(2, small[0:META, 8:9])

            def turns_of(i):
                if i >= 1:
                    act.wait_ge(s["rounded"], i)
                f(turns, steps, ACT.Identity, scale=s5c[:, 1, i:i + 1]).then_inc(s["ph"], 1)

            def sines_of(i):
                act.wait_ge(s["rounded"], i + 1)
                if i >= 2:
                    act.wait_ge(s["xs5"], i - 1)
                f(sinT[i % 2], frac[i % 2], ACT.Sin, scale=-TWO_PI)
                if i >= 1:
                    act.wait_ge(s["sines"], i)
                link(f(absf, frac[i % 2], ACT.Abs))
                f(cosT[i % 2], absf, ACT.Sin, scale=-TWO_PI, bias=zero_c[:, 1:2]).then_inc(s["sines"], 1)

            n_proj = [0]

            def proj_copy(dst, rows=P):
                n = n_proj[0]
                n_proj[0] += 1
                act.wait_ge(s["proj"], n + 1)
                f(dst, ps[n % 2][0:rows, 0:dst.free_size()], ACT.Copy).then_inc(s["proj_free"], 1)

            act.wait_ge(s["s5cols_ready"], 1)
            act.wait_ge(s["consts"], 16)
            turns_of(0)
            turns_of(1)
            for m in range(4):
                proj_copy(uT[:, m, :])
            sines_of(0)
            dsts = [kT[:, m, :] for m in range(4)] + [qT[:, m, :] for m in range(4)]
            dsts += [v_a[:, 0, :], v_a[:, 1, :], (v_m[:, :], META)] + [ogT[:, m, :] for m in range(4)]
            dsts += [gates[:, m, :] for m in range(16)]

            def next_proj():
                d = dsts.pop(0)
                proj_copy(*d) if isinstance(d, tuple) else proj_copy(d)

            for i in range(ST):
                if i + 1 < ST:
                    sines_of(i + 1)
                if i + 2 < ST:
                    turns_of(i + 2)
                next_proj()
            act.wait_ge(s["gelu_in"], 1)
            f(yt, yt, ACT.Sigmoid, scale=GELU_C).then_inc(s["gelu_sig"], 1)
            act.wait_ge(s["acol"], 1)
            f(small[:, 20:24], small[:, 16:20], ACT.Sigmoid, scale=-1.0).then_inc(s["acol"], 1)
            f(fT, kT, ACT.Sigmoid).then_inc(s["f_sig"], 1)
            f(sg, qT, ACT.Sigmoid).then_inc(s["q_sig"], 1)
            next_proj()
            next_proj()
            act.wait_ge(s["kq_ready"], 1)
            act.wait_ge(s["glu_mm"], 1)
            for b in range(2):
                last = f(sg[:, 2 * b:2 * b + 2, :], ps[6 + b][:, :].rearrange("p (a n) -> p a n", a=2), ACT.Sigmoid)
            last.then_inc(s["glu_sig"], 1)
            act.wait_ge(s["g5_ready"], 1)
            f(yt, ogT[:, :, :], ACT.Sigmoid).then_inc(s["og_sig"], 1)
            act.wait_ge(s["f_ready"], 1)
            f(bT, fT, ACT.Ln).then_inc(s["logf"], 1)
            next_proj()
            next_proj()
            act.wait_ge(s["kh_in"], 1)
            f(kh, kh, ACT.Exp).then_inc(s["kh_exp"], 1)
            act.wait_ge(s["eb_in"], 1)
            f(eb, bc, ACT.Exp).then_inc(s["eb_out"], 1)
            for n in range(len(LEVELS)):
                act.wait_ge(s["decay_in"], n + 1)
                f(dec, dec, ACT.Exp).then_inc(s["decay_out"], 1)
                next_proj()
            while dsts:
                next_proj()
            act.wait_ge(s["proj_free"], 4 * NG - 1)
            for b in range(4):
                f(gates[:, 4 * b:4 * b + 4, :], gates[:, 4 * b:4 * b + 4, :], ACT.Sigmoid).then_inc(s["gate_sig"], 1)
            root(3, qe)
            root(4, small[:, 32:33])
            root(5, small[:, 33:34])
            act.wait_ge(s["logits_in"], TT)
            for t in range(TT):
                f(ex[t], lg[t], ACT.Exp, bias=nmx[t]).then_inc(s["exped"], 1)
            act.wait_ge(s["idx_ready"], 1)
            n_items = act.value_load(idx[0:1, ITEMS:ITEMS + 1], min_val=E, max_val=ITEMS - 1)

            def combine_parts(w):
                act.wait_ge(s["ct_mm"], w + 1)
                f(ctr, ps[6][0:SLOTS, 0:SEQ], ACT.Copy).then_inc(s["ct_ready"], 1)
                act.wait_ge(s["yt_mm"], w + 1)
                for b in range(2):
                    last = f(ysl[:, 512 * b:512 * b + 512], ps[4 + b][0:SLOTS, :], ACT.Copy)
                last.then_inc(s["ysl_ready"], 1)

            with act.Fori(0, n_items) as w:
                act.wait_ge(s["gate_in"], w + 1)
                f(sgm, gt, ACT.Sigmoid, scale=1.702).then_inc(s["gate_sg"], 1)
                combine_parts(w)
                act.wait_ge(s["piece_used"], (w + 1) * PIECES)
                f(yT, ps[3][:, :].rearrange("p (a n) -> p a n", a=KD), ACT.Copy).then_inc(s["yT_ready"], 1)
            combine_parts(n_items)
            root(6, small[:, 40:41])
            root(7, small[:, 41:42])

        @block.tensor
        def _(pe):
            def mm(o, l, r, start, stop):
                return nc.tensor.matmul(o, l, r, start=start, stop=stop, skip_group_check=True)

            def tr(o, i, n=P):
                return nc.tensor.transpose(o, i, ident[0:n, 0:n])

            pe.wait_ge(s["consts"], 16)
            pe.wait_ge(s["ones_set"], 1)
            pe.wait_ge(s["rows"], 80)
            tr(ps[6][:, 0:32], prow[:, :], 32).then_inc(s["rows_turned"], 1)
            for t in range(TT):
                pe.wait_ge(s["xs_ready"], t + 1)
                for k in range(KD):
                    last = tr(ps[2 * t + k // 4][:, (k % 4) * P:(k % 4 + 1) * P], (xs, xs2)[t][:, k * P:(k + 1) * P])
                last.then_inc(s["turned_x"], 1)
            pe.wait_ge(s["xs_ready"], 3)
            for k in range(KD):
                last = tr(ps[5][:, k * META:(k + 1) * META], xmn[:, k * P:(k + 1) * P], META)
            last.then_inc(s["turned_m"], 1)
            pe.wait_ge(s["s5r_v"], 2)
            for j, row in enumerate((4, 5, 2, 3)):
                last = tr(ps[7][:, j * ST:(j + 1) * ST], s5r[:, row, :], ST)
            last.then_inc(s["s5rows_turned"], 1)

            n_proj = [0]

            def proj_tile(n, m):
                g = GROUPS[n]
                if m == 0:
                    pe.wait_ge(s["win%d" % (n % 2)], 16 * (n // 2 + 1))
                q = n_proj[0]
                n_proj[0] += 1
                if q >= 2:
                    pe.wait_ge(s["proj_free"], q - 1)
                for k in range(KD):
                    if g == 3:
                        lo, hi = ((META, META + P), (META + P, TOK), (0, META))[m]
                        last = mm(ps[q % 2][0:hi - lo, :], xnT[:, k, lo:hi], win[n % 2][:, k, :], k == 0, k == KD - 1)
                    else:
                        lo = 0 if g in (0, 2) else META
                        last = mm(ps[q % 2][:, 0:TOK - lo], win[n % 2][:, k, m * P:(m + 1) * P], xnT[:, k, lo:TOK],
                                  k == 0, k == KD - 1)
                last.then_inc(s["proj"], 1)

            def bu(i):
                if i >= 2:
                    pe.wait_ge(s["bu_free"], i - 1)
                r = 32 * (i % 4)
                for c in range(2):
                    last = mm(ps[2 + 2 * (i % 2) + c][:, 0:TOK], blk[r:r + 32, c, i // 4, :], uT[r:r + 32, i // 4, :], True, True)
                last.then_inc(s["bu"], 1)

            def y_of(i):
                pe.wait_ge(s["xs5"], i + 1)
                r, t = 32 * (i % 4), i // 4
                o = ps[6 + t // 2][r:r + 32, (t % 2) * SEQ:(t % 2 + 1) * SEQ]
                mm(o, blk[:, 2, t, r:r + 32], xre[i % 2][:, META:TOK], True, False)
                mm(o, blk[:, 3, t, r:r + 32], xim[i % 2][:, META:TOK], False, True).then_inc(s["ysum"], 1)

            pe.wait_ge(s["xnT_ready"], 1)
            for m in range(4):
                proj_tile(0, m)
            pe.wait_ge(s["bz_ready"], 1)
            for c in range(2):
                for t in range(4):
                    last = tr(ps[2 + c][:, t * P:(t + 1) * P], bz[:, c, t, :])
            last.then_inc(s["b_turned"], 1)
            for c in range(2):
                for t in range(4):
                    last = tr(ps[4 + c][:, t * P:(t + 1) * P], cz[:, c, t, :])
            last.then_inc(s["c_turned"], 1)
            tiles = [(n, m) for n in range(1, NG) for m in range(3 if GROUPS[n] == 3 else 4)]
            pe.wait_ge(s["b_laid"], 1)
            pe.wait_ge(s["proj_free"], 4)
            bu(0)
            pe.wait_ge(s["c_laid"], 1)
            bu(1)
            for i in range(ST):
                proj_tile(*tiles.pop(0))
                if i + 2 < ST:
                    bu(i + 2)
                y_of(i)
            for _ in range(2):
                proj_tile(*tiles.pop(0))
            pe.wait_ge(s["glu_w"], 16)
            pe.wait_ge(s["g5_ready"], 1)
            for m in range(KW):
                for k in range(KW):
                    last = mm(ps[6 + m // 2][:, (m % 2) * SEQ:(m % 2 + 1) * SEQ], w_glu[:, k, m * P:(m + 1) * P], g5[:, k, :],
                              k == 0 and m % 2 == 0, k == KW - 1)
            last.then_inc(s["glu_mm"], 1)
            for _ in range(3):
                proj_tile(*tiles.pop(0))
            pe.wait_ge(s["kh_ready"], 1)
            pe.wait_ge(s["glu_sig"], 1)
            for h in range(HEADS):
                tr(ps[6][0:META, h * P:(h + 1) * P], kh[:, h, 0:META])
                last = tr(ps[7][:, h * P:(h + 1) * P], kh[:, h, META:META + P])
            last.then_inc(s["kh_turned"], 1)
            pe.wait_ge(s["kq_ready"], 2)
            for j in range(8):
                last = mm(ps[4 + j // 4][:, (j % 4) * P:(j % 4 + 1) * P], kc[:, j * P:(j + 1) * P],
                          qT.rearrange("p a b -> p (a b)")[:, j * P:(j + 1) * P], j % 4 == 0, j % 4 == 3)
            last.then_inc(s["diag_mm"], 1)
            for n, m in enumerate(LEVELS):
                pe.wait_ge(s["level_in"], n + 1)
                if n >= 2:
                    pe.wait_ge(s["level_used"], n - 1)
                for j in range(8):
                    col = qk[:, j * P:(j + 1) * P]
                    right = col.rearrange("p (b m) -> p b m", m=2 * m)[:, :, m:2 * m]
                    last = mm(ps[2 + n % 2][:, j * 64:(j + 1) * 64], col, right, j == 0, j == 7)
                last.then_inc(s["level_mm"], 1)
                proj_tile(*tiles.pop(0))
                if n == 2:
                    pe.wait_ge(s["khT_ready"], 1)
                    for h in range(HEADS):
                        hs = slice(h * P, (h + 1) * P)
                        mm(ps[6][:, hs], khTm[:, hs], v_m[:, hs], h == 0, h == 3)
                        last = mm(ps[7][:, hs], khT[:, h, :], v_a[:, 0, hs], h == 0, h == 3)
                    last.then_inc(s["st_mm"], 1)
            while tiles:
                proj_tile(*tiles.pop(0))
            pe.wait_ge(s["qe_ready"], 1)
            pe.wait_ge(s["st1_ready"], 1)
            pe.wait_ge(s["stot_ready"], 1)
            for h in range(HEADS):
                for c in range(TT):
                    j = 2 * h + c
                    o = ps[4 + j // 4][:, (j % 4) * P:(j % 4 + 1) * P]
                    mm(o, (st0, st1)[c][:, h, :], qe[:, j * P:(j + 1) * P], j % 4 == 0, False)
                    last = mm(o, v_a[:, c, h * P:(h + 1) * P], stot[:, j, :], False, j % 4 == 3)
            last.then_inc(s["o_mm"], 1)
            pe.wait_ge(s["o2_ready"], 1)
            for b in range(2):
                last = mm(ps[6 + b][:, :], ones[:, :], o2[:, 512 * b:512 * b + 512], True, True)
            last.then_inc(s["ms_mm"], 1)
            pe.wait_ge(s["branch5_w"], 16)
            pe.wait_ge(s["branchh_w"], 16)
            pe.wait_ge(s["y5_ready"], 1)
            pe.wait_ge(s["proj_free"], 35)
            pe.wait_ge(s["level_used"], 7)
            for b in range(4):
                for br, (w, y) in enumerate(((w_b5, y5), (w_bh, yh))):
                    if b >= 2:
                        pe.wait_ge(s["br_free"], 2 * (b - 2) + br + 1)
                    if b == 0 and br == 1:
                        pe.wait_ge(s["yh_ready"], 1)
                    for j in range(2):
                        m = 2 * b + j
                        for k in range(KW):
                            last = mm(ps[2 * (b % 2) + br][:, j * SEQ:(j + 1) * SEQ], w[:, k, m * P:(m + 1) * P], y[:, k, :],
                                      k == 0 and j == 0, k == KW - 1)
                        last.then_inc(s["br_mm"], 1)
            pe.wait_ge(s["out_w"], 16)
            pe.wait_ge(s["mrg_ready"], 4)
            for t in range(TT):
                for b in range(2):
                    for k in range(KD):
                        last = mm(ps[4 + 2 * t + b][:, :], mrg[:, k, t * P:(t + 1) * P], w_out[:, k, 512 * b:512 * b + 512],
                                  k == 0, k == KD - 1)
                    last.then_inc(s["wo_mm"], 1)
            for t in range(TT):
                pe.wait_ge(s["x2_ready"], t + 1)
                for k in range(KD):
                    last = tr(ps[2 * t + k // 4][:, (k % 4) * P:(k % 4 + 1) * P], x2[:, t, k * P:(k + 1) * P])
                last.then_inc(s["x2_turned"], 1)
            pe.wait_ge(s["router_w"], 16)
            pe.wait_ge(s["router_b"], 16)
            for t in range(TT):
                pe.wait_ge(s["x2T_ready"], t + 1)
                for k in range(KD):
                    mm(ps[4 + t][:, 0:E], x2T[:, k, t * P:(t + 1) * P], wrt[:, k, :], k == 0, False)
                mm(ps[4 + t][:, 0:E], ones[0:1, :], brt, False, True).then_inc(s["logit_mm"], 1)
            pe.wait_ge(s["mask_ready"], TT)
            mm(ps[0][:, 0:E], tri, mask[0], True, True)
            mm(ps[1][:, 0:E], tri, mask[1], True, False)
            mm(ps[1][:, 0:E], ones[:, :], mask[0], False, True)
            for t in range(TT):
                last = mm(ps[2][0:E, 0:1], mask[t], ones[:, 0:1], t == 0, t == TT - 1)
            last.then_inc(s["rank_mm"], 1)
            pe.wait_ge(s["slot_ready"], TT)
            for t in range(TT):
                tr(ps[3][0:E, t * P:(t + 1) * P], slot[t])
                last = tr(ps[3][0:E, (2 + t) * P:(3 + t) * P], wt[t])
            last.then_inc(s["tr_mm"], 1)
            pe.wait_ge(s["cnt_ready"], 1)
            mm(ps[2][0:E, 1:2], tri[0:E, 0:E], cx, True, True)
            mm(ps[2][0:1, 2:3], ones[0:E, 0:1], cx, True, True).then_inc(s["start_mm"], 1)
            pe.wait_ge(s["oh_ready"], 1)
            for t in range(TT):
                o = ps[4 + t]
                mm(o[:, 0:ITEMS], slT[:, t * P:(t + 1) * P], oh, True, False)
                mm(o[:, 0:ITEMS], neg, ohc, False, True)
                mm(o[:, 64:64 + ITEMS], wtT[:, t * P:(t + 1) * P], oh, True, True)
            mm(ps[6][0:1, 0:ITEMS], cst[0:E, C_PI:C_PI + 1], oh, True, True).then_inc(s["item_mm"], 1)
            pe.wait_ge(s["expert_rows"], 32)
            bg = bgu.rearrange("e (m p g) -> e g m p", p=P, g=2)
            for g in range(2):
                for m in range(KD):
                    last = mm(ps[g][:, m * ITEMS:(m + 1) * ITEMS], bg[:, g, m, :], oh, m == 0, m == KD - 1)
            last.then_inc(s["bias_mm"], 1)
            pe.wait_ge(s["items_ready"], 1)
            for t in range(TT):
                for b in range(2):
                    if t == 1 and b == 0:
                        pe.wait_ge(s["bias_ready"], 1)
                    o = (ps[4], ps[5], ps[0], ps[1])[2 * t + b]
                    last = mm(o[:, :], wtT[:, t * P:(t + 1) * P], bdn[:, 512 * b:512 * b + 512], True, True)
            last.then_inc(s["acc0_mm"], 1)

            def gather(w):
                pe.wait_ge(s["pick_ready"], w + 1)
                if not isinstance(w, int):
                    pe.wait_ge(s["xg_ready"], w)
                for k in range(KD):
                    for t in range(TT):
                        last = mm(ps[2][:, k * SLOTS:(k + 1) * SLOTS], x2[:, t, k * P:(k + 1) * P], pick[:, t, :],
                                  k == 0 and t == 0, t == TT - 1)
                last.then_inc(s["gathered"], 1)

            def turn_last(w1):
                pe.wait_ge(s["consts"], 16)
                pe.wait_ge(s["added0"], w1)
                pe.wait_ge(s["w_pickw"], w1)
                for t in range(TT):
                    last = tr(ps[6][0:SLOTS, t * P:(t + 1) * P], pickw[:, t, :])
                last.then_inc(s["ct_mm"], 1)
                pe.wait_ge(s["consts"], 16)
                pe.wait_ge(s["yT_ready"], w1)
                pe.wait_ge(s["added1"], w1)
                for k in range(KD):
                    last = tr(ps[4 + k // 4][0:SLOTS, (k % 4) * P:(k % 4 + 1) * P], yT[:, k, :])
                last.then_inc(s["yt_mm"], 1)

            def add_last(w):
                pe.wait_ge(s["ct_ready"], w + 1)
                pe.wait_ge(s["ysl_ready"], w + 1)
                for t, sm in ((0, "comb0"), (1, "comb1")):
                    for b in range(2):
                        last = mm(ps[(6, 4)[t] + b][:, :], ctr[:, t * P:(t + 1) * P], ysl[:, 512 * b:512 * b + 512], True, True)
                    last.then_inc(s[sm], 1)

            pe.wait_ge(s["idx_ready"], 1)
            gather(0)
            n_items = pe.value_load(idx[0:1, ITEMS:ITEMS + 1], min_val=E, max_val=ITEMS - 1)
            n_plus = pe.value_load(idx[0:1, ITEMS + 1:ITEMS + 2], min_val=E + 1, max_val=ITEMS)
            with pe.Fori(0, n_items) as w:
                pe.wait_ge(s["xg_ready"], w + 1)
                pe.wait_ge(s["h_done"], w + 1)
                for k in range(KD):
                    pe.wait_ge(landed[k], 16 * (w + 1))
                    wv = ring[:, k, :].rearrange("p (m q g) -> p g m q", q=P, g=2)
                    for g in range(2):
                        for m in range(KD):
                            last = mm(ps[g][:, m * SLOTS:(m + 1) * SLOTS], wv[:, g, m, :], xgT[:, k, :],
                                      k == 0 and m == 0, k == KD - 1)
                    last.then_inc(s["piece_used"], 1)
                turn_last(pe.snap(w + 1))
                gather(w + 1)
                add_last(w)
                pe.wait_ge(s["h_done"], w + 2)
                for k in range(KD):
                    if k % 2 == 0:
                        pe.wait_ge(landed[KD + k // 2], 16 * (w + 1))
                    wv = ring[:, KD + k // 2, (k % 2) * D:(k % 2 + 1) * D]
                    for m in range(KD):
                        last = mm(ps[3][:, m * SLOTS:(m + 1) * SLOTS], wv[:, m * P:(m + 1) * P], hT[:, k, :],
                                  k == 0 and m == 0, k == KD - 1)
                    if k % 2 == 1:
                        last.then_inc(s["piece_used"], 1)
            turn_last(n_plus)
            add_last(n_items)

        @block.vector
        def _(dve):
            n_dch = [0]
            V = nc.vector

            def link(ins):
                n_dch[0] += 1
                ins.then_inc(s["dch"], 1)
                dve.wait_ge(s["dch"], n_dch[0])

            def tt(o, i0, i1, op):
                return V.tensor_tensor(out=o, in0=i0, in1=i1, op=op)

            def ts(o, i, s1, s2, op0, op1=None):
                return V.tensor_scalar(o, i, s1, s2, op0, op1) if op1 is not None else V.tensor_scalar(o, i, s1, None, op0)

            def stt(o, i0, sc, i1, op0, op1):
                return V.scalar_tensor_tensor(out=o, in0=i0, scalar=sc, in1=i1, op0=op0, op1=op1)

            def wide(col, n):
                return col.unsqueeze(2).to_broadcast([col.shape[0], col.shape[1], n])

            MU, AD, SU = ALU.mult, ALU.add, ALU.subtract
            V.memset(zero_c[:, 0:1], 0.0)
            link(V.memset(zero_c[:, 1:2], float(np.float32(np.pi / 2))))
            R = lambda j: s5r[:, j, :]
            R2 = lambda j: s5r[:, j, :].rearrange("p (g n) -> p g n", g=2)
            dt2 = wide(small[0:ST, 2:4], 64)
            dve.wait_ge(s["s5r_exp"], 1)
            tt(R2(2), R2(0), dt2, MU).then_inc(s["s5r_v"], 1)
            link(tt(R2(3), R2(1), dt2, MU))
            link(ts(R(6), R(3), float(1 / (2 * np.pi)), MAGIC, MU, AD))
            link(ts(R(6), R(6), MAGIC, None, SU))
            c1 = 6.28125
            c2 = float(np.float32(2 * np.pi - c1) // 2 ** -19 * 2 ** -19)
            c3 = float(2 * np.pi - c1 - c2)
            for c in (c1, c2, c3):
                link(stt(R(3), R(6), -c, R(3), MU, AD))
            link(ts(R(5), R(3), float(1 / (2 * np.pi)), 0.5, MU, ALU.min))
            ts(R(5), R(5), -0.5, None, ALU.max).then_inc(s["s5r_ang"], 1)
            dve.wait_ge(s["s5r_exp"], 2)
            dve.wait_ge(s["s5r_sin"], 2)
            link(tt(R(7), R(7), R(7), MU))
            link(tt(R(7), R(7), R(4), MU))
            link(stt(R(7), R(7), -2.0, R(4), MU, AD))
            link(ts(R(7), R(7), -1.0, None, AD))
            link(tt(R(6), R(6), R(4), MU))
            q1, q2, q3 = s5q[:, 0, :], s5q[:, 1, :], s5q[:, 2, :]
            tt(q1, R(0), R(0), MU)
            link(tt(q2, R(1), R(1), MU))
            link(tt(q1, q1, q2, AD))
            link(V.reciprocal(q1, q1))
            tt(q2, R(7), R(0), MU)
            link(tt(q3, R(6), R(1), MU))
            link(tt(q2, q2, q3, AD))
            link(tt(R(2), q2, q1, MU))
            tt(q2, R(6), R(0), MU)
            link(tt(q3, R(7), R(1), MU))
            link(tt(q2, q2, q3, SU))
            tt(R(3), q2, q1, MU).then_inc(s["s5r_v"], 1)

            dve.wait_ge(s["xload"], 16)
            for t in range(TT):
                last = V.tensor_tensor_reduce((xs, xs2)[t], x[:, t, :], x[:, t, :], 1.0, 0.0, MU, AD, small[:, 4 + t:5 + t])
            link(last)
            ts(small[:, 4:6], small[:, 4:6], 1.0 / D, EPS, MU, AD).then_inc(s["var_in"], 1)
            dve.wait_ge(s["meta"], 16)
            link(V.tensor_tensor_reduce(xmn, xm[:, :], xm[:, :], 1.0, 0.0, MU, AD, small[0:META, 8:9]))
            ts(small[0:META, 8:9], small[0:META, 8:9], 1.0 / D, EPS, MU, AD).then_inc(s["var_in"], 1)
            dve.wait_ge(s["root_out"], 1)
            link(V.reciprocal(small[:, 6:8], small[:, 4:6]))
            for t in range(TT):
                ts((xs, xs2)[t], x[:, t, :], small[:, 6 + t:7 + t], None, MU).then_inc(s["xs_ready"], 1)
            dve.wait_ge(s["root_out"], 2)
            link(V.reciprocal(small[0:META, 9:10], small[0:META, 8:9]))
            ts(xmn, xm[:, :], small[0:META, 9:10], None, MU).then_inc(s["xs_ready"], 1)
            dve.wait_ge(s["rows_turned"], 1)
            link(V.tensor_copy(pcol[:, :], ps[6][:, 0:32]))
            gain1, gain2 = pcol[:, 0:8], pcol[:, 8:16]
            for t in range(TT):
                dve.wait_ge(s["turned_x"], t + 1)
                for b in range(2):
                    tt(xnT[:, 4 * b:4 * b + 4, META + t * P:META + (t + 1) * P],
                       ps[2 * t + b][:, :].rearrange("p (a n) -> p a n", a=4), wide(gain1[:, 4 * b:4 * b + 4], P), MU)
            dve.wait_ge(s["turned_m"], 1)
            tt(xnT[:, :, 0:META], ps[5][:, 0:KD * META].rearrange("p (a n) -> p a n", a=KD), wide(gain1, META), MU)\
                .then_inc(s["xnT_ready"], 1)
            dve.wait_ge(s["s5rows_turned"], 1)
            V.tensor_copy(s5c[:, :, :], ps[7][:, 0:4 * ST].rearrange("p (a n) -> p a n", a=4)).then_inc(s["s5cols_ready"], 1)
            dve.wait_ge(s["s5cols_ready"], 1)
            dve.wait_ge(s["bload"], 32)
            dve.wait_ge(s["consts"], 16)
            cr, ci = wide(s5c[:, 2, :], 16), wide(s5c[:, 3, :], 16)
            tt(bb[0], bre, cr, MU)
            tt(bb[1], bim, ci, MU)
            tt(bb[2], bre, ci, MU)
            link(tt(bb[3], bim, cr, MU))
            tt(bb[0], bb[0], bb[1], SU)
            link(tt(bb[2], bb[2], bb[3], AD))
            for c in range(2):
                for g in range(2):
                    o = bz[:, c, :, :].rearrange("p t (i g h) -> p (t i) g h", i=4, g=2)[:, :, g, :]
                    last = ts(o, bb[2 * c], cst[:, C_GB + g:C_GB + g + 1], None, MU)
            dve.wait_ge(s["cload"], 32)
            for c in range(2):
                for g in range(2):
                    last = ts(cz[:, c, :, g * 64:(g + 1) * 64], cn[:, c], cst[:, C_GC + g:C_GC + g + 1], (1.0, -1.0)[c], MU, MU)
            last.then_inc(s["bz_ready"], 1)

            def fraction(i):
                dve.wait_ge(s["ph"], i + 1)
                if i >= 2:
                    dve.wait_ge(s["sines"], i - 1)
                link(ts(rnd, turns, MAGIC, None, AD))
                stt(frac[i % 2], rnd, MAGIC, turns, SU, SU).then_inc(s["rounded"], 1)

            fraction(0)
            dve.wait_ge(s["b_turned"], 1)
            for c in range(2):
                last = V.tensor_copy(blk[:, c, :, :], ps[2 + c][:, :].rearrange("p (a n) -> p a n", a=4))
            last.then_inc(s["b_laid"], 1)
            dve.wait_ge(s["c_turned"], 1)
            for c in range(2):
                last = V.tensor_copy(blk[:, 2 + c, :, :], ps[4 + c][:, :].rearrange("p (a n) -> p a n", a=4))
            last.then_inc(s["c_laid"], 1)
            fraction(1)
            for i in range(ST):
                re, im = ps[2 + 2 * (i % 2)][:, 0:TOK], ps[3 + 2 * (i % 2)][:, 0:TOK]
                sn, co = sinT[i % 2], cosT[i % 2]
                if i >= 1:
                    dve.wait_ge(s["xs5"], i)
                dve.wait_ge(s["bu"], i + 1)
                dve.wait_ge(s["sines"], i + 1)
                tt(rot[0], re, co, MU)
                tt(rot[1], im, sn, MU)
                tt(rot[2], im, co, MU)
                link(tt(rot[3], re, sn, MU))
                tt(rot[0], rot[0], rot[1], AD).then_inc(s["bu_free"], 1)
                link(tt(rot[2], rot[2], rot[3], SU))
                r = s5c[:, 0, i:i + 1].to_broadcast([P, TOK])
                V.tensor_tensor_scan(zre, r, rot[0], 0.0, MU, AD)
                link(V.tensor_tensor_scan(zim, r, rot[2], 0.0, MU, AD))
                z = slice(META, TOK)
                if i >= 2:
                    dve.wait_ge(s["ysum"], i - 1)
                tt(rot[0][:, z], zre[:, z], co[:, z], MU)
                tt(rot[1][:, z], zim[:, z], sn[:, z], MU)
                tt(rot[2][:, z], zre[:, z], sn[:, z], MU)
                link(tt(rot[3][:, z], zim[:, z], co[:, z], MU))
                tt(xre[i % 2][:, z], rot[0][:, z], rot[1][:, z], SU)
                tt(xim[i % 2][:, z], rot[2][:, z], rot[3][:, z], AD).then_inc(s["xs5"], 1)
                if i + 2 < ST:
                    fraction(i + 2)
            dve.wait_ge(s["ysum"], ST)
            for t in range(KW):
                last = stt(y5[:, t, :], uT[:, t, META:TOK], pcol[:, 28 + t:29 + t],
                           ps[6 + t // 2][:, (t % 2) * SEQ:(t % 2 + 1) * SEQ], MU, AD)
            link(last)
            link(tt(yt, y5, y5, MU))
            link(ts(yt, yt, 0.044715, 1.0, MU, AD))
            tt(yt, yt, y5, MU).then_inc(s["gelu_in"], 1)
            tt(small[:, 16:20], pcol[:, 20:24], pcol[:, 16:20], SU).then_inc(s["acol"], 1)
            dve.wait_ge(s["gelu_sig"], 1)
            tt(g5, y5, yt, MU).then_inc(s["g5_ready"], 1)
            dve.wait_ge(s["q_sig"], 1)
            tt(qT, qT, sg, MU).then_inc(s["kq_ready"], 1)
            dve.wait_ge(s["acol"], 2)
            link(ts(small[:, 24:28], small[:, 20:24], -1.0, 1.0, MU, AD))
            dve.wait_ge(s["f_sig"], 1)
            for h in range(HEADS):
                last = ts(fT[:, h, :], fT[:, h, :], small[:, 24 + h:25 + h], small[:, 20 + h:21 + h], MU, AD)
            last.then_inc(s["f_ready"], 1)
            dve.wait_ge(s["f_ready"], 1)
            link(ts(kT, fT, -1.0, 1.0, MU, AD))
            dve.wait_ge(s["glu_sig"], 1)
            tt(y5, g5, sg, MU).then_inc(s["y5_ready"], 1)
            V.tensor_copy(kc.rearrange("p (a n) -> p a n", a=KW), kT[:, :, META:TOK]).then_inc(s["kq_ready"], 1)
            dve.wait_ge(s["og_sig"], 1)
            for h in range(HEADS):
                link(stt(ogT[:, h, :], ogT[:, h, :], pcol[:, 24 + h:25 + h], yt[:, h, :], MU, MU))
            dve.wait_ge(s["logf"], 1)
            chunk = ((0, META), (META, META + P), (META + P, TOK))
            one = ones[:, 0:1]
            dve.wait_ge(s["ones_set"], 1)
            for h in range(HEADS):
                for lo, hi in chunk:
                    last = V.tensor_tensor_scan(bT[:, h, lo:hi], one.to_broadcast([P, hi - lo]), bT[:, h, lo:hi], 0.0, MU, AD)
            link(last)
            for lo, hi in chunk[:2]:
                last = tt(kh[:, :, lo:hi], bT[:, :, hi - 1:hi].to_broadcast([P, HEADS, hi - lo]), bT[:, :, lo:hi], SU)
            last.then_inc(s["kh_in"], 1)
            V.tensor_copy(bc.rearrange("p (a n) -> p a n", a=KW), bT[:, :, META:TOK]).then_inc(s["eb_in"], 1)

            def level_decay(n):
                m = LEVELS[n]
                if n >= 1:
                    dve.wait_ge(s["level_in"], n)
                b = bc.rearrange("p (c m) -> p c m", m=2 * m)
                d = dec.rearrange("p (c m) -> p c m", m=2 * m)
                mid = b[:, :, m - 1:m].to_broadcast([P, 1024 // (2 * m), m])
                tt(d[:, :, 0:m], mid, b[:, :, 0:m], SU)
                tt(d[:, :, m:2 * m], b[:, :, m:2 * m], mid, SU).then_inc(s["decay_in"], 1)

            dve.wait_ge(s["eb_in"], 1)
            level_decay(0)
            dve.wait_ge(s["kh_exp"], 1)
            tt(kh, kh, kT[:, :, 0:META + P], MU).then_inc(s["kh_ready"], 1)
            dve.wait_ge(s["eb_out"], 1)
            tt(qe, eb, qT.rearrange("p a b -> p (a b)"), MU).then_inc(s["qe_ready"], 1)
            dve.wait_ge(s["diag_mm"], 1)
            for b in range(2):
                last = tt(stot[:, 4 * b:4 * b + 4, :], ps[4 + b][:, :].rearrange("p (a n) -> p a n", a=4),
                          ident.unsqueeze(1).to_broadcast([P, 4, P]), MU)
            link(last)
            qf = qT.rearrange("p a b -> p (a b)")
            stf = stot.rearrange("p a b -> p (a b)")

            def level_sum(n):
                m = LEVELS[n]
                dve.wait_ge(s["level_mm"], n + 1)
                mk = cst[:, C_MASK + 64 * n:C_MASK + 64 * (n + 1)].unsqueeze(1).to_broadcast([P, 8, 64])
                ins = tt(tmpl, ps[2 + n % 2][:, :].rearrange("p (a n) -> p a n", a=8), mk, MU)
                ins.then_inc(s["level_used"], 1)
                dve.wait_ge(s["level_used"], n + 1)
                so = stf.rearrange("p (c m) -> p c m", m=2 * m)[:, :, m:2 * m]
                ins = tt(so, so, tmpl.rearrange("p a b -> p (a b)").rearrange("p (c m) -> p c m", m=m), AD)
                if n == len(LEVELS) - 1:
                    ins.then_inc(s["stot_ready"], 1)
                else:
                    link(ins)

            for n, m in enumerate(LEVELS):
                dve.wait_ge(s["decay_out"], n + 1)
                if n >= 1:
                    dve.wait_ge(s["level_mm"], n)
                g3 = lambda t: t.rearrange("p (c m) -> p c m", m=2 * m)
                tt(g3(qk)[:, :, 0:m], g3(dec)[:, :, 0:m], g3(kc)[:, :, 0:m], MU)
                tt(g3(qk)[:, :, m:2 * m], g3(dec)[:, :, m:2 * m], g3(qf)[:, :, m:2 * m], MU).then_inc(s["level_in"], 1)
                if n + 1 < len(LEVELS):
                    level_decay(n + 1)
                if n == 1:
                    dve.wait_ge(s["kh_turned"], 1)
                    V.tensor_copy(khTm, ps[6][0:META, :])
                    V.tensor_copy(khT, ps[7][:, :].rearrange("p (a n) -> p a n", a=4)).then_inc(s["khT_ready"], 1)
                if n >= 1:
                    level_sum(n - 1)
            level_sum(len(LEVELS) - 1)
            dve.wait_ge(s["st_mm"], 1)
            link(V.tensor_copy(st0, ps[6][:, :].rearrange("p (a n) -> p a n", a=4)))
            for h in range(HEADS):
                last = stt(st1[:, h, :], st0[:, h, :], eb[:, h * SEQ + P - 1:h * SEQ + P], ps[7][:, h * P:(h + 1) * P], MU, AD)
            last.then_inc(s["st1_ready"], 1)
            dve.wait_ge(s["o_mm"], 1)
            for b in range(2):
                last = V.tensor_copy(orn[:, 512 * b:512 * b + 512], ps[4 + b][:, :])
            link(last)
            tt(o2, orn, orn, MU).then_inc(s["o2_ready"], 1)
            dve.wait_ge(s["ms_mm"], 1)
            for b in range(2):
                last = ts(qe[:, 512 * b:512 * b + 512], ps[6 + b][:, :], 1.0 / P, EPS, MU, AD)
            last.then_inc(s["var_in"], 1)
            dve.wait_ge(s["root_out"], 3)
            link(V.reciprocal(qe, qe))
            link(tt(orn, orn, qe, MU))
            tt(yh, orn.rearrange("p (a n) -> p a n", a=KW), ogT[:, :, :], MU).then_inc(s["yh_ready"], 1)
            dve.wait_ge(s["gate_sig"], 4)
            for b in range(4):
                for br in range(2):
                    dve.wait_ge(s["br_mm"], 4 * b + 2 * br + 2)
                    ins = tt((mrg[:, 2 * b:2 * b + 2, 0:SEQ], gates[:, KD + 2 * b:KD + 2 * b + 2, :])[br],
                             ps[2 * (b % 2) + br][:, :].rearrange("p (a n) -> p a n", a=2),
                             gates[:, br * KD + 2 * b:br * KD + 2 * b + 2, :], MU)
                    ins.then_inc(s["br_free"], 1)
                dve.wait_ge(s["br_free"], 2 * b + 2)
                tt(mrg[:, 2 * b:2 * b + 2, 0:SEQ], mrg[:, 2 * b:2 * b + 2, 0:SEQ], gates[:, KD + 2 * b:KD + 2 * b + 2, :], AD)\
                    .then_inc(s["mrg_ready"], 1)
            for t in range(TT):
                for b in range(2):
                    dve.wait_ge(s["wo_mm"], 2 * t + b + 1)
                    last = tt(x[:, t, 512 * b:512 * b + 512], ps[4 + 2 * t + b][:, :], x[:, t, 512 * b:512 * b + 512], AD)
                link(last)
                link(V.tensor_tensor_reduce(x2[:, t, :], x[:, t, :], x[:, t, :], 1.0, 0.0, MU, AD, small[:, 32 + t:33 + t]))
                ts(small[:, 32 + t:33 + t], small[:, 32 + t:33 + t], 1.0 / D, EPS, MU, AD).then_inc(s["var_in"], 1)
                dve.wait_ge(s["root_out"], 4 + t)
                link(V.reciprocal(small[:, 34 + t:35 + t], small[:, 32 + t:33 + t]))
                ts(x2[:, t, :], x[:, t, :], small[:, 34 + t:35 + t], None, MU).then_inc(s["x2_ready"], 1)
            for t in range(TT):
                dve.wait_ge(s["x2_turned"], t + 1)
                for b in range(2):
                    last = tt(x2T[:, 4 * b:4 * b + 4, t * P:(t + 1) * P], ps[2 * t + b][:, :].rearrange("p (a n) -> p a n", a=4),
                              wide(gain2[:, 4 * b:4 * b + 4], P), MU)
                last.then_inc(s["x2T_ready"], 1)
            for t in range(TT):
                dve.wait_ge(s["logit_mm"], t + 1)
                link(V.tensor_copy(lg[t], ps[4 + t][:, 0:E]))
                link(V.max(mx[t], lg[t]))
                ts(nmx[t], mx[t][:, 0:1], -1.0, None, MU).then_inc(s["logits_in"], 1)
                link(V.max_index(ix[:, t, :], mx[t], lg[t]))
                link(V.tensor_copy(ixf[t], ix[:, t, 0:TOPK]))
                link(ts(mask[t], iota_e, ixf[t][:, 0:1], None, ALU.is_equal))
                for k in range(1, TOPK):
                    ins = stt(mask[t], iota_e, ixf[t][:, k:k + 1], mask[t], ALU.is_equal, AD)
                    if k < TOPK - 1:
                        link(ins)
                ins.then_inc(s["mask_ready"], 1)
            dve.wait_ge(s["mask_ready"], TT)
            dve.wait_ge(s["exped"], TT)
            dve.wait_ge(s["rank_mm"], 1)
            for t in range(TT):
                link(tt(ex[t], ex[t], mask[t], MU))
                link(V.tensor_reduce(den[t], ex[t], AX, AD))
                link(V.reciprocal(den[t], den[t]))
                ts(wt[t], ex[t], den[t], None, MU)
                link(stt(slot[t], mask[t], 4096.0, ps[t][:, 0:E], MU, AD))
                ts(slot[t], slot[t], -4096.0, None, AD).then_inc(s["slot_ready"], 1)
            link(V.tensor_copy(cnt, ps[2][0:E, 0:1]))
            link(ts(cx, cnt, float(SLOTS), None, ALU.is_gt))
            for j in (2, 3):
                ins = stt(cx, cnt, float(SLOTS * j), cx, ALU.is_gt, AD)
                if j == 2:
                    link(ins)
            ins.then_inc(s["cnt_ready"], 1)
            V.memset(neg, -float(SLOTS))
            V.memset(ohc[:, 0:E], 0.0)
            V.tensor_copy(oh[:, 0:E], ident[0:E, 0:E])
            dve.wait_ge(s["start_mm"], 1)
            link(V.tensor_copy(first, ps[2][0:E, 1:2]))
            js, ja, jb = j3[:, 0:EXTRA], j3[:, 16:32], j3[:, 32:48]
            link(ts(js, iota_e[0:E, 0:EXTRA], first, None, SU))
            ts(ja, js, 0.0, None, ALU.is_ge)
            link(ts(jb, js, cx, None, ALU.is_lt))
            link(tt(oh[:, E:ITEMS], ja, jb, MU))
            link(ts(js, js, 1.0, None, AD))
            tt(ohc[:, E:ITEMS], js, oh[:, E:ITEMS], MU)
            dve.wait_ge(s["tr_mm"], 1)
            V.tensor_copy(slT, ps[3][0:E, 0:SEQ])
            V.tensor_copy(wtT, ps[3][0:E, SEQ:2 * SEQ]).then_inc(s["oh_ready"], 1)
            dve.wait_ge(s["item_mm"], 1)
            V.tensor_copy(idx[0:1, 0:ITEMS], ps[6][0:1, 0:ITEMS]).then_inc(s["added0"], 1)
            ts(idx[0:1, ITEMS + 1:ITEMS + 2], ps[2][0:1, 2:3], float(E + 1), None, AD)
            ts(idx[0:1, ITEMS:ITEMS + 1], ps[2][0:1, 2:3], float(E), None, AD).then_inc(s["idx_ready"], 1)
            for t in range(TT):
                V.tensor_copy(islot[:, t, :], ps[4 + t][:, 0:ITEMS])
                last = V.tensor_copy(iwt[:, t, :], ps[4 + t][:, 64:64 + ITEMS])
            last.then_inc(s["items_ready"], 1)
            dve.wait_ge(s["bias_mm"], 1)
            for g in range(2):
                o = bias[:, :, g * KD:(g + 1) * KD].rearrange("p w m -> p m w")
                last = V.tensor_copy(o, ps[g][:, 0:KD * ITEMS].rearrange("p (m w) -> p m w", m=KD))
            last.then_inc(s["bias_ready"], 1)
            dve.wait_ge(s["items_ready"], 1)
            V.memset(yT, 0.0).then_inc(s["yT_ready"], 1)
            V.memset(pickw, 0.0).then_inc(s["w_pickw"], 1)
            dve.wait_ge(s["acc0_mm"], 1)
            for t in range(TT):
                for b in range(2):
                    o = (ps[4], ps[5], ps[0], ps[1])[2 * t + b]
                    last = tt(x[:, t, 512 * b:512 * b + 512], o[:, :], x[:, t, 512 * b:512 * b + 512], AD)
                last.then_inc(s[("added1", "h_done")[t]], 1)

            def picks(w):
                for t in range(TT):
                    last = ts(pick[:, t, :], iota_s, islot[:, t, bass.ds(w, 1)], None, ALU.is_equal)
                return last

            def take_gathered(w):
                dve.wait_ge(s["gathered"], w + 1)
                tt(xgT, ps[2][:, :].rearrange("p (a n) -> p a n", a=KD), wide(gain2, SLOTS), MU).then_inc(s["xg_ready"], 1)

            def add_item(w):
                for t, sm in ((0, "0"), (1, "1")):
                    dve.wait_ge(s["comb" + sm], w + 1)
                    for b in range(2):
                        last = tt(x[:, t, 512 * b:512 * b + 512], ps[(6, 4)[t] + b][:, :], x[:, t, 512 * b:512 * b + 512], AD)
                    last.then_inc(s["added" + sm], 1)

            picks(0).then_inc(s["pick_ready"], 1)
            n_items = dve.value_load(idx[0:1, ITEMS:ITEMS + 1], min_val=E, max_val=ITEMS - 1)
            take_gathered(0)
            with dve.Fori(0, n_items) as w:
                picks(w + 1).then_inc(s["pick_ready"], 1)
                dve.wait_ge(s["piece_used"], w * PIECES + KD)
                bw = lambda g: bias[:, bass.ds(w, 1), g * KD:(g + 1) * KD].rearrange("p o m -> p (o m)")
                pg = [ps[g][:, :].rearrange("p (a n) -> p a n", a=KD) for g in range(2)]
                tt(gt, pg[0], wide(bw(0), SLOTS), AD).then_inc(s["w_gate"], 1)
                dve.wait_ge(s["w_gate"], 3 * w + 1)
                ts(gt, gt, 7.0, None, ALU.min).then_inc(s["gate_in"], 1)
                tt(up, pg[1], wide(bw(1), SLOTS), AD).then_inc(s["w_gate"], 1)
                dve.wait_ge(s["w_gate"], 3 * w + 2)
                dve.wait_ge(s["gate_in"], w + 1)
                ts(up, up, 7.0, -7.0, ALU.min, ALU.max).then_inc(s["w_gate"], 1)
                dve.wait_ge(s["w_gate"], 3 * w + 3)
                f1 = lambda t: t.rearrange("p a b -> p (a b)")
                stt(f1(up), f1(up), 1.0, f1(gt), AD, MU).then_inc(s["w_up"], 1)
                dve.wait_ge(s["w_up"], w + 1)
                dve.wait_ge(s["gate_sg"], w + 1)
                tt(hT, up, sgm, MU).then_inc(s["h_done"], 1)
                dve.wait_ge(s["ct_mm"], w + 1)
                for t in range(TT):
                    last = ts(pickw[:, t, :], iota_s, islot[:, t, bass.ds(w, 1)], iwt[:, t, bass.ds(w, 1)], ALU.is_equal, MU)
                last.then_inc(s["w_pickw"], 1)
                take_gathered(w + 1)
                add_item(w)
            add_item(n_items)
            dve.wait_ge(s["added1"], n_items + 2)
            dve.wait_ge(s["lastgain"], 16)
            for t in range(TT):
                link(V.tensor_tensor_reduce(x2[:, t, :], x[:, t, :], x[:, t, :], 1.0, 0.0, MU, AD, small[:, 40 + t:41 + t]))
                ts(small[:, 40 + t:41 + t], small[:, 40 + t:41 + t], 1.0 / D, EPS, MU, AD).then_inc(s["var_in"], 1)
                dve.wait_ge(s["root_out"], 6 + t)
                link(V.reciprocal(small[:, 42 + t:43 + t], small[:, 40 + t:41 + t]))
                stt(x2[:, t, :], x[:, t, :], small[:, 42 + t:43 + t], fgain, MU, MU).then_inc(s["w_last"], 1)


_INS = ["x", "meta_tokens", "norm1_gain", "w_in", "s5_lambda_re", "s5_lambda_im", "s5_log_dt", "s5_b_re",
        "s5_b_im", "s5_c_re", "s5_c_im", "s5_d", "s5_w_glu", "hgrn_lb_logits", "hgrn_norm_gain", "w_branch_s5",
        "w_branch_hgrn", "w_out", "norm2_gain", "w_router", "b_router", "w_gate_up", "b_gate_up", "w_down",
        "b_down", "final_norm_gain"]


def kernel(**inputs):
    import concourse.bacc as bacc
    from concourse.bass_utils import run_bass_kernel_spmd

    nc = bacc.Bacc("TRN2", target_bir_lowering=False, num_devices=1)
    arrays = {n: np.ascontiguousarray(inputs[n]) for n in _INS}
    arrays["shape_consts"] = shape_constants()
    feeds, views = {}, {}
    for n, v in arrays.items():
        feeds[f"in_{n}"] = v
        views[n] = nc.dram_tensor(f"in_{n}", v.shape, mybir.dt.from_np(v.dtype), kind="ExternalInput").ap()
    out = nc.dram_tensor("out_0", (1, SEQ, D), F32, kind="ExternalOutput").ap()
    build(nc, views, out)
    r = run_bass_kernel_spmd(nc, [feeds], core_ids=[0])
    return r.results[0]["out_0"]
```

```python
from contextlib import ExitStack

import numpy as np
import concourse.bass as bass
from concourse import mybir

F32 = mybir.dt.float32
I32 = mybir.dt.int32
U32 = mybir.dt.uint32
ALU = mybir.AluOpType
ACT = mybir.ActivationFunctionType
AX = mybir.AxisListType.X

P = 128
META, SEQ = 16, 256
TOK = META + SEQ
D = 1024
KD = D // P
W5 = 512
KW = W5 // P
HEADS = 4
STATES = 32 * 64
ST = STATES // P
TT = SEQ // P
E = 32
TOPK = 4
SLOTS = 64
EXTRA = 16
ITEMS = E + EXTRA
PIECES = 12
PC = 2048
EPS = 1e-6
LIMIT = 7.0
LEVELS = [64, 32, 16, 8, 4, 2, 1]
MAGIC = 1.5 * 2.0 ** 23
TWO_PI = 6.2831850
GELU_C = 2 * 0.7978845608028654

C_ID, C_TRI, C_MASK = 0, P, 2 * P
C_T = C_MASK + len(LEVELS) * 64
C_IE = C_T + TOK
C_IS = C_IE + E
C_GC = C_IS + SLOTS
C_GB = C_GC + 2
C_PI = C_GB + 2
C_ALL = C_PI + 1


def shape_constants():
    c = np.zeros((P, C_ALL), np.float32)
    p = np.arange(P)
    c[:, C_ID:C_ID + P] = np.eye(P)
    c[:, C_TRI:C_TRI + P] = p[:, None] < p[None, :]
    for n, m in enumerate(LEVELS):
        i = np.array([b * 2 * m + m + r for b in range(64 // m) for r in range(m)])
        same = p[:, None] // (2 * m) == i[None, :] // (2 * m)
        left = p[:, None] % (2 * m) < m
        c[:, C_MASK + 64 * n:C_MASK + 64 * (n + 1)] = same & left
    c[:, C_T:C_T + TOK] = np.arange(TOK)
    c[:, C_IE:C_IE + E] = np.arange(E)
    c[:, C_IS:C_IS + SLOTS] = np.arange(SLOTS)
    for g in range(2):
        c[:, C_GC + g] = (p // 16) % 2 == g
        c[:, C_GB + g] = p // 64 == g
    c[:, C_PI] = p
    return c


def build(nc, a, out):
    with ExitStack() as ctx:
        def sb(name, shape, dt=F32):
            return ctx.enter_context(nc.sbuf_tensor(name, shape, dt))

        def sem(name):
            return ctx.enter_context(nc.semaphore(name))

        ring = sb("ring", [P, PIECES, PC])
        cst = sb("cst", [P, C_ALL])
        x = sb("x", [P, TT, D])
        xnT = sb("xnT", [P, KD, TOK])
        uT = sb("uT", [P, KW, TOK])
        v_a = sb("v_a", [P, TT, W5])
        v_m = sb("v_m", [META, W5])
        ogT = sb("ogT", [P, KW, SEQ])
        gates = sb("gates", [P, 2 * KD, SEQ])
        w_mix = sb("w_mix", [P, 10240])
        ones = sb("ones", [P, P])
        prow = sb("prow", [32, P])
        pcol = sb("pcol", [P, 32])
        s5c = sb("s5c", [P, 4, ST])
        blk = sb("blk", [P, 4, 4, P])
        small = sb("small", [P, 64])
        rms = small[:, 48:64]
        zero_c = sb("zero_c", [P, 4])
        rout = sb("rout", [P, 1400])
        ix = sb("ix", [P, TT, 8], U32)
        idx = sb("idx", [1, ITEMS + 2], I32)

        def at(t, lo, *dims):
            n = int(np.prod(dims))
            v = t[:, lo:lo + n]
            if len(dims) == 1:
                return v
            names = "abcd"[:len(dims)]
            return v.rearrange("p (%s) -> p %s" % (" ".join(names), " ".join(names)),
                               **{k: d for k, d in zip(names, dims)})

        ringf = ring[:, :, :].rearrange("p a b -> p (a b)")
        ident = cst[:, C_ID:C_ID + P]
        tri = cst[:, C_TRI:C_TRI + P]
        steps = cst[:, C_T:C_T + TOK]
        iota_e = cst[:, C_IE:C_IE + E]
        iota_s = cst[:, C_IS:C_IS + SLOTS]
        win = [at(ringf, s * 4096, KD, 512) for s in range(2)]
        qT = at(ringf, 4 * PC, KW, SEQ)
        kT = at(ringf, 4 * PC + 1024, KW, TOK)
        bT = at(ringf, 4 * PC + 2112, KW, TOK)
        xmn = ringf[0:META, 4 * PC:4 * PC + D]
        xm = ringf[0:META, 4 * PC + 1024:4 * PC + 1024 + D]
        s5r = at(ringf[0:ST], 4 * PC + 2112, 8, P)
        s5q = at(ringf[0:ST], 4 * PC + 3136, 3, P)
        B0 = 6 * PC
        NT = TOK
        turns = at(ringf, B0, NT)
        rnd = at(ringf, B0 + NT, NT)
        absf = at(ringf, B0 + 2 * NT, NT)
        frac = [at(ringf, B0 + (3 + i) * NT, NT) for i in range(2)]
        sinT = [at(ringf, B0 + (5 + i) * NT, NT) for i in range(2)]
        cosT = [at(ringf, B0 + (7 + i) * NT, NT) for i in range(2)]
        rot = [at(ringf, B0 + (9 + i) * NT, NT) for i in range(4)]
        zre = at(ringf, B0 + 13 * NT, NT)
        zim = at(ringf, B0 + 14 * NT, NT)
        xre = [at(ringf, B0 + (15 + i) * NT, NT) for i in range(2)]
        xim = [at(ringf, B0 + (17 + i) * NT, NT) for i in range(2)]
        H0 = B0 + 19 * NT
        bre = at(ringf, H0, ST, 16)
        bim = at(ringf, H0 + 256, ST, 16)
        bb = [at(ringf, H0 + 512 + 256 * i, ST, 16) for i in range(4)]
        bz = at(ringf, H0 + 1536, 2, 4, P)
        cn = at(ringf, H0 + 2560, 2, 4, 64)
        cz = at(ringf, H0 + 3072, 2, 4, P)
        xs = at(ringf, H0 + 4096, D)
        xs2 = at(ringf, H0 + 5120, D)
        junk = at(ringf, H0 + 6144, 976)
        M0 = B0
        y5 = at(ringf, M0, KW, SEQ)
        yt = at(ringf, M0 + 1024, KW, SEQ)
        g5 = at(ringf, M0 + 2048, KW, SEQ)
        fT = at(ringf, M0 + 3072, KW, TOK)
        sg = at(ringf, M0 + 4160, KW, SEQ)
        bc = at(ringf, M0 + 5184, 1024)
        kc = at(ringf, M0 + 6208, 1024)
        dec = at(ringf, M0 + 7232, 1024)
        qk = at(ringf, M0 + 8256, 1024)
        stot = at(ringf, M0 + 9280, 8, P)
        tmpl = at(ringf, M0 + 10304, 8, 64)
        qe = at(ringf, M0 + 3072, 1024)
        kh = at(ringf, M0 + 10816, KW, 144)
        eb = at(ringf, M0 + 1024, 1024)
        khT = at(ringf, M0 + 4160, KW, P)
        khTm = ringf[0:META, M0 + 4672:M0 + 4672 + W5]
        st0 = at(ringf, M0 + 5184, KW, P)
        st1 = at(ringf, M0 + 5696, KW, P)
        o2 = at(ringf, M0 + 7232, 1024)
        yh = at(ringf, M0 + 8256, KW, SEQ)
        orn = at(ringf, M0 + 6208, 1024)
        w_out = at(ringf, 0, KD, D)
        mrg = xnT
        w_glu = at(w_mix, 0, KW, W5)
        w_b5 = at(w_mix, 2048, KW, D)
        w_bh = at(w_mix, 6144, KW, D)
        x2 = at(w_mix, 0, TT, D)
        x2T = at(w_mix, 2048, KD, SEQ)
        xgT = at(w_mix, 4096, KD, SLOTS)
        hT = at(w_mix, 4608, 4, 2, SLOTS)
        gt = at(w_mix, 5120, 512)
        sgm = at(w_mix, 5632, 512)
        up = at(w_mix, 6144, 512)
        ysl = at(w_mix, 6656, 512)
        ctr = at(w_mix, 7168, SEQ)
        pick = at(w_mix, 7424, TT, SLOTS)
        pickw = at(w_mix, 7552, TT, 2, SLOTS)
        ohb = at(w_mix, 7808, SLOTS)
        wrt = at(w_mix, 9472, KD, E)
        brt = w_mix[0:1, 9728:9728 + E]
        gatesf = gates[:, :, :].rearrange("p a b -> p (a b)")
        bgu = gatesf[:, 0:2 * D]
        bdn = gatesf[:, 2 * D:3 * D]
        fgain = gatesf[:, 3 * D:4 * D]

        ps = [ctx.enter_context(nc.psum_tensor(f"ps{i}", [P, 512], F32)) for i in range(8)]

        lg, ex, mask, slot, wt = ([rout[:, 64 * j + 32 * t:64 * j + 32 * t + E] for t in range(TT)] for j in range(5))
        mx = [rout[:, 320 + 8 * t:328 + 8 * t] for t in range(TT)]
        nmx = [rout[:, 336 + t:337 + t] for t in range(TT)]
        den = [rout[:, 338 + t:339 + t] for t in range(TT)]
        ixf = [rout[:, 340 + 4 * t:344 + 4 * t] for t in range(TT)]
        cnt, cx, first = (rout[0:E, 348 + j:349 + j] for j in range(3))
        neg = rout[0:E, 352:352 + P]
        oh = rout[0:E, 480:480 + ITEMS]
        ohc = rout[0:E, 528:528 + ITEMS]
        j3 = rout[0:E, 576:624]
        slT = rout[0:E, 640:640 + SEQ]
        wtT = rout[0:E, 896:896 + SEQ]
        islot = at(rout, 1152, TT, ITEMS)
        iwt = at(rout, 1248, TT, ITEMS)
        s = {}
        for n in """consts xload0 xload1 meta rows s5rows bload cload glu_w branch5_w branchh_w out_w expert_rows
                    router_w router_b lastgain win0 win1 out_stored
                    ones_set xs_ready xs_free turned_x xnT_ready turned_m xmT_ready
                    rows_turned cols_ready s5rows_turned s5cols_ready s5r_exp s5r_ang s5r_sin s5r_v
                    bz_ready b_turned b_laid c_turned c_laid
                    proj proj_free bu bu_free ph rounded sines scanned xs5 y_add ysum ydone
                    gelu_in gelu_sig g5_ready glu_mm glu_sig f_sig q_sig og_sig f_ready logf
                    kq_ready decay_in decay_out level_in level_mm level_used diag_mm
                    eb_in eb_out kh_in kh_exp kh_ready kh_turned khT_ready st_mm st0_ready st1_ready stot_ready
                    qe_ready o_mm o2_ready ms_mm yh_ready y5_ready gate_sig br_mm br_free mrg_ready wo_mm
                    h_ready x2_ready x2_turned x2T_ready logit_mm logits_in exped mask_ready
                    rank_mm slot_ready tr_mm cnt_ready start_mm oh_ready item_mm items_ready idx_ready
                    rms_out ohb_used diag_ready inv_mm
                    pick_ready gathered xg_ready gate_in gate_sg h_done yT_ready
                    ct_mm ct_ready ysl_ready comb0 comb1 added0 added1 piece_used w_last
                    acol dch ach w_gate w_up pad_zero ohb_ready h_turned hT_ready  w_pickw var_in root_out""".split():
            s[n] = sem(n)
        landed = [sem(f"landed{i}") for i in range(PIECES)]

        x_d = a["x"].rearrange("b (t p) d -> p (b t) d", p=P)
        win_d = a["w_in"].rearrange("l (k p) n -> p (l k) n", p=P)
        gu_d = a["w_gate_up"].rearrange("l e (k p) n -> p (l e k) n", p=P)
        dn_d = a["w_down"].rearrange("l e (k p) n -> p (l e k) n", p=P)
        GROUPS = [0, 2, 1, 3, 4, 5, 6, 7, 8]
        NG = len(GROUPS)

        def expert_piece(q, e, i):
            if i < KD:
                src = gu_d[:, bass.ds(e * KD + i, 1), :]
                dst = ring[:, i:i + 1, :]
            else:
                src = dn_d[:, bass.ds(e * KD + 2 * (i - KD), 2), :]
                dst = ring[:, i, :].rearrange("p (a n) -> p a n", a=2)
            q.dma_start(dst, src).then_inc(landed[i], 16)

        block = ctx.enter_context(nc.Block())

        @block.sync
        def _(sp):
            for t in range(TT):
                sp.dma_start(x[:, t, :], x_d[:, t, :]).then_inc(s["xload%d" % t], 16)
            sp.dma_start(xm[:, :], a["meta_tokens"]).then_inc(s["meta"], 16)
            pr = lambda n, k: a[n].rearrange("l (k p) -> (l k) p", p=P)
            sp.dma_start(prow[0:8, :], pr("norm1_gain", 8)).then_inc(s["rows"], 16)
            sp.dma_start(prow[8:16, :], pr("norm2_gain", 8)).then_inc(s["rows"], 16)
            sp.dma_start(prow[16:24, :], pr("hgrn_lb_logits", 8)).then_inc(s["rows"], 16)
            sp.dma_start(prow[24:28, :], pr("hgrn_norm_gain", 4)).then_inc(s["rows"], 16)
            sp.dma_start(prow[28:32, :], a["s5_d"].rearrange("l (k g) h -> (l k) (g h)", k=4)).then_inc(s["rows"], 16)
            used = 0
            for n in range(NG):
                if n >= 2:
                    used += 3 if GROUPS[n - 2] == 3 else 4
                    sp.wait_ge(s["proj"], used)
                g = GROUPS[n]
                sp.dma_start(win[n % 2], win_d[:, :, g * 512:(g + 1) * 512]).then_inc(s["win%d" % (n % 2)], 16)
                if n == 2:
                    sp.dma_start(w_glu, a["s5_w_glu"].rearrange("l (k p) n -> p (l k) n", p=P)).then_inc(s["glu_w"], 16)
                if n == 4:
                    sp.dma_start(w_b5, a["w_branch_s5"].rearrange("l (k p) n -> p (l k) n", p=P)).then_inc(s["branch5_w"], 16)
                if n == 5:
                    sp.dma_start(w_bh, a["w_branch_hgrn"].rearrange("l (k p) n -> p (l k) n", p=P)).then_inc(s["branchh_w"], 16)
            sp.wait_ge(s["proj"], 4 * NG - 1)
            sp.dma_start(w_out, a["w_out"].rearrange("l (k p) n -> p (l k) n", p=P)).then_inc(s["out_w"], 16)
            sp.wait_ge(s["br_mm"], 16)
            sp.dma_start(wrt, a["w_router"].rearrange("l (k p) n -> p (l k) n", p=P)).then_inc(s["router_w"], 16)
            sp.dma_start(brt, a["b_router"]).then_inc(s["router_b"], 16)
            for i in range(4, PIECES):
                expert_piece(sp, 0, i)
            sp.wait_ge(s["mrg_ready"], 4)
            sp.dma_start(bgu[0:E, :], a["b_gate_up"].rearrange("l e n -> (l e) n")).then_inc(s["expert_rows"], 16)
            sp.dma_start(bdn[0:E, :], a["b_down"].rearrange("l e n -> (l e) n")).then_inc(s["expert_rows"], 16)
            sp.dma_start(fgain, a["final_norm_gain"].rearrange("(o n) -> o n", o=1).to_broadcast([P, D])).then_inc(s["lastgain"], 16)
            sp.wait_ge(s["wo_mm"], 4)
            for i in range(4):
                expert_piece(sp, 0, i)
            sp.wait_ge(s["idx_ready"], 1)
            n_items = sp.value_load(idx[0:1, ITEMS:ITEMS + 1], min_val=E, max_val=ITEMS - 1)
            with sp.Fori(1, n_items) as w:
                e = sp.value_load(idx[0:1, bass.ds(w, 1)], min_val=0, max_val=E - 1)
                for i in range(PIECES):
                    sp.wait_ge(s["piece_used"], (w - 1) * PIECES + i + 1)
                    expert_piece(sp, e, i)
            for t in range(TT):
                sp.wait_ge(s["w_last"], t + 1)
                sp.dma_start(out.rearrange("b (t p) d -> p (b t) d", p=P)[:, t, :], x2[:, t, :]).then_inc(s["out_stored"], 16)
            sp.wait_ge(s["out_stored"], 16 * TT)

        @block.gpsimd
        def _(pool):
            nc.gpsimd.memset(ones[:, :], 1.0).then_inc(s["ones_set"], 1)
            pool.wait_ge(s["mrg_ready"], 4)
            for q in range(1, 4):
                nc.gpsimd.memset(ohb[32 * q:32 * q + 32, :], 0.0)
                nc.gpsimd.memset(bgu[32 * q:32 * q + 32, :], 0.0)
                last = nc.gpsimd.memset(bdn[32 * q:32 * q + 32, :], 0.0)
            last.then_inc(s["pad_zero"], 1)

        @block.scalar
        def _(act):
            n_ach = [0]

            def link(ins):
                n_ach[0] += 1
                ins.then_inc(s["ach"], 1)
                act.wait_ge(s["ach"], n_ach[0])

            def f(o, i, fn, **k):
                return nc.scalar.activation(o, i, fn, **k)

            act.dma_start(cst[:, :], a["shape_consts"]).then_inc(s["consts"], 16)
            act.dma_start(s5r[:, 0, :], a["s5_lambda_re"].rearrange("l (i g) p -> (l i) (g p)", g=2)).then_inc(s["s5rows"], 16)
            act.dma_start(s5r[:, 1, :], a["s5_lambda_im"].rearrange("l (i g) p -> (l i) (g p)", g=2)).then_inc(s["s5rows"], 16)
            act.dma_start(small[0:ST, 0:2], a["s5_log_dt"].rearrange("l (i g) -> (l i) g", g=2)).then_inc(s["s5rows"], 16)
            act.dma_start(bre, a["s5_b_re"].rearrange("l (i g) p h -> (g p) (l i) h", g=2)).then_inc(s["bload"], 16)
            act.dma_start(bim, a["s5_b_im"].rearrange("l (i g) p h -> (g p) (l i) h", g=2)).then_inc(s["bload"], 16)
            act.dma_start(cn[:, 0], a["s5_c_re"].rearrange("l (t g) h p -> (g h) (l t) p", t=4)).then_inc(s["cload"], 16)
            act.dma_start(cn[:, 1], a["s5_c_im"].rearrange("l (t g) h p -> (g h) (l t) p", t=4)).then_inc(s["cload"], 16)

            def root(n, v):
                act.wait_ge(s["var_in"], n)
                f(v, v, ACT.Sqrt).then_inc(s["root_out"], 1)

            for t in range(TT):
                root(1 + t, small[:, 4 + t:5 + t])
            root(3, small[0:META, 8:9])
            act.wait_ge(s["s5rows"], 48)
            f(small[0:ST, 2:4], small[0:ST, 0:2], ACT.Exp).then_inc(s["s5r_exp"], 1)
            act.wait_ge(s["s5r_v"], 1)
            f(s5r[:, 4, :], s5r[:, 2, :], ACT.Exp).then_inc(s["s5r_exp"], 1)
            act.wait_ge(s["s5r_ang"], 1)
            f(s5r[:, 6, :], s5r[:, 5, :], ACT.Sin, scale=TWO_PI).then_inc(s["s5r_sin"], 1)
            f(s5r[:, 7, :], s5r[:, 5, :], ACT.Sin, scale=TWO_PI / 2).then_inc(s["s5r_sin"], 1)

            def turns_of(i):
                if i >= 1:
                    act.wait_ge(s["rounded"], i)
                f(turns, steps, ACT.Identity, scale=s5c[:, 1, i:i + 1]).then_inc(s["ph"], 1)

            def sines_of(i):
                act.wait_ge(s["rounded"], i + 1)
                if i >= 2:
                    act.wait_ge(s["xs5"], i - 1)
                f(sinT[i % 2], frac[i % 2], ACT.Sin, scale=-TWO_PI)
                if i >= 1:
                    act.wait_ge(s["sines"], i)
                link(f(absf, frac[i % 2], ACT.Abs))
                f(cosT[i % 2], absf, ACT.Sin, scale=-TWO_PI, bias=zero_c[:, 1:2]).then_inc(s["sines"], 1)

            n_proj = [0]

            def proj_copy(dst, rows=P):
                n = n_proj[0]
                n_proj[0] += 1
                act.wait_ge(s["proj"], n + 1)
                f(dst, ps[n % 2][0:rows, 0:dst.free_size()], ACT.Copy).then_inc(s["proj_free"], 1)

            for m in range(3):
                proj_copy(uT[:, m, :])
            act.wait_ge(s["s5cols_ready"], 1)
            act.wait_ge(s["consts"], 16)
            turns_of(0)
            turns_of(1)
            sines_of(0)
            proj_copy(uT[:, 3, :])
            dsts = [kT[:, m, :] for m in range(4)] + [qT[:, m, :] for m in range(4)]
            dsts += [v_a[:, 0, :], v_a[:, 1, :], (v_m[:, :], META)] + [ogT[:, m, :] for m in range(4)]
            dsts += [gates[:, m, :] for m in range(16)]

            def next_proj():
                d = dsts.pop(0)
                proj_copy(*d) if isinstance(d, tuple) else proj_copy(d)

            for i in range(ST):
                if i + 1 < ST:
                    sines_of(i + 1)
                if i + 2 < ST:
                    turns_of(i + 2)
                next_proj()
            act.wait_ge(s["gelu_in"], 1)
            f(yt, yt, ACT.Sigmoid, scale=GELU_C).then_inc(s["gelu_sig"], 1)
            act.wait_ge(s["acol"], 1)
            f(small[:, 20:24], small[:, 16:20], ACT.Sigmoid, scale=-1.0).then_inc(s["acol"], 1)
            f(fT, kT, ACT.Sigmoid).then_inc(s["f_sig"], 1)
            f(sg, qT, ACT.Sigmoid).then_inc(s["q_sig"], 1)
            next_proj()
            next_proj()
            act.wait_ge(s["kq_ready"], 1)
            act.wait_ge(s["glu_mm"], 1)
            for b in range(2):
                last = f(sg[:, 2 * b:2 * b + 2, :], ps[6 + b][:, :].rearrange("p (a n) -> p a n", a=2), ACT.Sigmoid)
            last.then_inc(s["glu_sig"], 1)
            act.wait_ge(s["g5_ready"], 1)
            f(yt, ogT[:, :, :], ACT.Sigmoid).then_inc(s["og_sig"], 1)
            act.wait_ge(s["f_ready"], 1)
            f(bT, fT, ACT.Ln).then_inc(s["logf"], 1)
            next_proj()
            next_proj()
            act.wait_ge(s["kh_in"], 1)
            f(kh, kh, ACT.Exp).then_inc(s["kh_exp"], 1)
            act.wait_ge(s["eb_in"], 1)
            f(eb, bc, ACT.Exp).then_inc(s["eb_out"], 1)
            for n in range(len(LEVELS)):
                act.wait_ge(s["decay_in"], n + 1)
                f(dec, dec, ACT.Exp).then_inc(s["decay_out"], 1)
                next_proj()
            while dsts:
                next_proj()
            act.wait_ge(s["proj_free"], 4 * NG - 1)
            def gate_sigmoids(b):
                f(gates[:, 4 * b:4 * b + 4, :], gates[:, 4 * b:4 * b + 4, :], ACT.Sigmoid).then_inc(s["gate_sig"], 1)

            gate_sigmoids(0)
            gate_sigmoids(1)
            act.wait_ge(s["o_mm"], 1)
            for b in range(2):
                f(o2[:, 512 * b:512 * b + 512], ps[4 + b][:, :], ACT.Square).then_inc(s["o2_ready"], 1)
            act.wait_ge(s["ms_mm"], 1)
            f(rms[:, 0:8], ps[7][:, 0:8], ACT.Sqrt, scale=1.0 / P, bias=zero_c[:, 2:3]).then_inc(s["rms_out"], 1)
            gate_sigmoids(2)
            gate_sigmoids(3)
            root(4, small[:, 32:33])
            root(5, small[:, 33:34])
            act.wait_ge(s["logits_in"], TT)
            for t in range(TT):
                f(ex[t], lg[t], ACT.Exp, bias=nmx[t]).then_inc(s["exped"], 1)
            act.wait_ge(s["idx_ready"], 1)
            n_items = act.value_load(idx[0:1, ITEMS:ITEMS + 1], min_val=E, max_val=ITEMS - 1)

            def combine_parts(w):
                act.wait_ge(s["ct_mm"], w + 1)
                f(ctr, ps[5][:, 0:SEQ], ACT.Copy).then_inc(s["ct_ready"], 1)

            with act.Fori(0, n_items) as w:
                combine_parts(w)
                act.wait_ge(s["gate_in"], w + 1)
                f(sgm, gt, ACT.Sigmoid, scale=1.702).then_inc(s["gate_sg"], 1)
                act.wait_ge(s["piece_used"], (w + 1) * PIECES)
                f(ysl, ps[4][:, :], ACT.Copy).then_inc(s["ysl_ready"], 1)
            combine_parts(n_items)
            root(6, small[:, 40:41])
            root(7, small[:, 41:42])

        @block.tensor
        def _(pe):
            def mm(o, l, r, start, stop):
                return nc.tensor.matmul(o, l, r, start=start, stop=stop, skip_group_check=True)

            def tr(o, i, n=P):
                return nc.tensor.transpose(o, i, ident[0:n, 0:n])

            pe.wait_ge(s["consts"], 16)
            pe.wait_ge(s["ones_set"], 1)
            pe.wait_ge(s["rows"], 80)
            tr(ps[6][:, 0:32], prow[:, :], 32).then_inc(s["rows_turned"], 1)
            for t in range(TT):
                pe.wait_ge(s["xs_ready"], t + 1)
                for k in range(KD):
                    last = tr(ps[2 * t + k // 4][:, (k % 4) * P:(k % 4 + 1) * P], (xs, xs2)[t][:, k * P:(k + 1) * P])
                last.then_inc(s["turned_x"], 1)
            pe.wait_ge(s["xs_ready"], 3)
            for k in range(KD):
                last = tr(ps[5][:, k * META:(k + 1) * META], xmn[:, k * P:(k + 1) * P], META)
            last.then_inc(s["turned_m"], 1)
            n_proj = [0]

            def proj_tile(n, m):
                g = GROUPS[n]
                if m == 0:
                    pe.wait_ge(s["win%d" % (n % 2)], 16 * (n // 2 + 1))
                q = n_proj[0]
                n_proj[0] += 1
                if q >= 2:
                    pe.wait_ge(s["proj_free"], q - 1)
                for k in range(KD):
                    if g == 3:
                        lo, hi = ((META, META + P), (META + P, TOK), (0, META))[m]
                        last = mm(ps[q % 2][0:hi - lo, :], xnT[:, k, lo:hi], win[n % 2][:, k, :], k == 0, k == KD - 1)
                    else:
                        lo = 0 if g in (0, 2) else META
                        last = mm(ps[q % 2][:, 0:TOK - lo], win[n % 2][:, k, m * P:(m + 1) * P], xnT[:, k, lo:TOK],
                                  k == 0, k == KD - 1)
                last.then_inc(s["proj"], 1)

            def bu(i):
                if i >= 2:
                    pe.wait_ge(s["bu_free"], i - 1)
                r = 32 * (i % 4)
                for c in range(2):
                    last = mm(ps[2 + 2 * (i % 2) + c][:, 0:TOK], blk[r:r + 32, c, i // 4, :], uT[r:r + 32, i // 4, :], True, True)
                last.then_inc(s["bu"], 1)

            def y_of(i):
                pe.wait_ge(s["xs5"], i + 1)
                r, t = 32 * (i % 4), i // 4
                o = ps[6 + t // 2][r:r + 32, (t % 2) * SEQ:(t % 2 + 1) * SEQ]
                mm(o, blk[:, 2, t, r:r + 32], xre[i % 2][:, META:TOK], True, False)
                mm(o, blk[:, 3, t, r:r + 32], xim[i % 2][:, META:TOK], False, True).then_inc(s["ysum"], 1)

            pe.wait_ge(s["xnT_ready"], 1)
            for m in range(3):
                proj_tile(0, m)
            pe.wait_ge(s["s5r_v"], 2)
            for j, row in enumerate((4, 5, 2, 3)):
                last = tr(ps[7][:, j * ST:(j + 1) * ST], s5r[:, row, :], ST)
            last.then_inc(s["s5rows_turned"], 1)
            proj_tile(0, 3)
            pe.wait_ge(s["bz_ready"], 1)
            for c in range(2):
                for t in range(4):
                    last = tr(ps[2 + c][:, t * P:(t + 1) * P], bz[:, c, t, :])
            last.then_inc(s["b_turned"], 1)
            for c in range(2):
                for t in range(4):
                    last = tr(ps[4 + c][:, t * P:(t + 1) * P], cz[:, c, t, :])
            last.then_inc(s["c_turned"], 1)
            tiles = [(n, m) for n in range(1, NG) for m in range(3 if GROUPS[n] == 3 else 4)]
            pe.wait_ge(s["b_laid"], 1)
            pe.wait_ge(s["proj_free"], 4)
            bu(0)
            pe.wait_ge(s["c_laid"], 1)
            bu(1)
            for i in range(ST):
                proj_tile(*tiles.pop(0))
                if i + 2 < ST:
                    bu(i + 2)
                y_of(i)
            for _ in range(2):
                proj_tile(*tiles.pop(0))
            pe.wait_ge(s["glu_w"], 16)
            pe.wait_ge(s["g5_ready"], 1)
            for m in range(KW):
                for k in range(KW):
                    last = mm(ps[6 + m // 2][:, (m % 2) * SEQ:(m % 2 + 1) * SEQ], w_glu[:, k, m * P:(m + 1) * P], g5[:, k, :],
                              k == 0 and m % 2 == 0, k == KW - 1)
            last.then_inc(s["glu_mm"], 1)
            for _ in range(3):
                proj_tile(*tiles.pop(0))
            pe.wait_ge(s["kh_ready"], 1)
            pe.wait_ge(s["glu_sig"], 1)
            for h in range(HEADS):
                tr(ps[6][0:META, h * P:(h + 1) * P], kh[:, h, 0:META])
                last = tr(ps[7][:, h * P:(h + 1) * P], kh[:, h, META:META + P])
            last.then_inc(s["kh_turned"], 1)
            pe.wait_ge(s["kq_ready"], 2)
            for j in range(8):
                last = mm(ps[4 + j // 4][:, (j % 4) * P:(j % 4 + 1) * P], kc[:, j * P:(j + 1) * P],
                          qT.rearrange("p a b -> p (a b)")[:, j * P:(j + 1) * P], j % 4 == 0, j % 4 == 3)
            last.then_inc(s["diag_mm"], 1)
            for n, m in enumerate(LEVELS):
                pe.wait_ge(s["level_in"], n + 1)
                if n >= 2:
                    pe.wait_ge(s["level_used"], n - 1)
                for j in range(8):
                    col = qk[:, j * P:(j + 1) * P]
                    right = col.rearrange("p (b m) -> p b m", m=2 * m)[:, :, m:2 * m]
                    last = mm(ps[2 + n % 2][:, j * 64:(j + 1) * 64], col, right, j == 0, j == 7)
                last.then_inc(s["level_mm"], 1)
                proj_tile(*tiles.pop(0))
                if n == 2:
                    pe.wait_ge(s["khT_ready"], 1)
                    for h in range(HEADS):
                        hs = slice(h * P, (h + 1) * P)
                        mm(ps[6][:, hs], khTm[:, hs], v_m[:, hs], h == 0, h == 3)
                        last = mm(ps[7][:, hs], khT[:, h, :], v_a[:, 0, hs], h == 0, h == 3)
                    last.then_inc(s["st_mm"], 1)
            while tiles:
                proj_tile(*tiles.pop(0))
            pe.wait_ge(s["qe_ready"], 1)
            pe.wait_ge(s["st1_ready"], 1)
            pe.wait_ge(s["stot_ready"], 1)
            for h in range(HEADS):
                for c in range(TT):
                    j = 2 * h + c
                    o = ps[4 + j // 4][:, (j % 4) * P:(j % 4 + 1) * P]
                    mm(o, (st0, st1)[c][:, h, :], qe[:, j * P:(j + 1) * P], j % 4 == 0, False)
                    last = mm(o, v_a[:, c, h * P:(h + 1) * P], stot[:, j, :], False, j % 4 == 3)
            last.then_inc(s["o_mm"], 1)
            def branch(br, b):
                w, y = ((w_b5, y5), (w_bh, yh))[br]
                for j in range(2):
                    m = 2 * b + j
                    for k in range(KW):
                        last = mm(ps[4 * br + b][:, j * SEQ:(j + 1) * SEQ], w[:, k, m * P:(m + 1) * P], y[:, k, :],
                                  k == 0 and j == 0, k == KW - 1)
                    last.then_inc(s["br_mm"], 1)

            pe.wait_ge(s["branch5_w"], 16)
            pe.wait_ge(s["y5_ready"], 1)
            pe.wait_ge(s["proj_free"], 4 * NG - 1)
            pe.wait_ge(s["level_used"], 7)
            branch(0, 0)
            pe.wait_ge(s["o2_ready"], 2)
            for j in range(8):
                last = mm(ps[7][:, j:j + 1], o2[:, j * P:(j + 1) * P], ones[:, 0:1], j == 0, j == 7)
            last.then_inc(s["ms_mm"], 1)
            branch(0, 1)
            pe.wait_ge(s["diag_ready"], 1)
            for b in range(2):
                last = mm(ps[6 + b][:, :], ones[:, :], qe[:, 512 * b:512 * b + 512], True, True)
            last.then_inc(s["inv_mm"], 1)
            branch(0, 2)
            branch(0, 3)
            pe.wait_ge(s["branchh_w"], 16)
            pe.wait_ge(s["yh_ready"], 2)
            for b in range(4):
                branch(1, b)
            pe.wait_ge(s["out_w"], 16)
            for t in range(TT):
                for b in range(2):
                    for k in range(KD):
                        if t == 0 and b == 0 and k % 2 == 0:
                            pe.wait_ge(s["mrg_ready"], k // 2 + 1)
                        last = mm(ps[2 * t + b][:, :], mrg[:, k, t * P:(t + 1) * P], w_out[:, k, 512 * b:512 * b + 512],
                                  k == 0, k == KD - 1)
                    last.then_inc(s["wo_mm"], 1)
            for t in range(TT):
                pe.wait_ge(s["x2_ready"], t + 1)
                for k in range(KD):
                    last = tr(ps[4 + 2 * t + k // 4][:, (k % 4) * P:(k % 4 + 1) * P], x2[:, t, k * P:(k + 1) * P])
                last.then_inc(s["x2_turned"], 1)
            pe.wait_ge(s["router_w"], 16)
            pe.wait_ge(s["router_b"], 16)
            pe.wait_ge(s["x2T_ready"], TT)
            for k in range(KD):
                for t in range(TT):
                    mm(ps[t][:, 0:E], x2T[:, k, t * P:(t + 1) * P], wrt[:, k, :], k == 0, False)
            for t in range(TT):
                mm(ps[t][:, 0:E], ones[0:1, :], brt, False, True).then_inc(s["logit_mm"], 1)
            pe.wait_ge(s["mask_ready"], 1)
            mm(ps[0][:, 0:E], tri, mask[0], True, True)
            mm(ps[1][:, 0:E], tri, mask[1], True, False)
            mm(ps[1][:, 0:E], ones[:, :], mask[0], False, True)
            for t in range(TT):
                last = mm(ps[2][0:E, 0:1], mask[t], ones[:, 0:1], t == 0, t == TT - 1)
            last.then_inc(s["rank_mm"], 1)
            pe.wait_ge(s["slot_ready"], 1)
            for t in range(TT):
                tr(ps[3][0:E, t * P:(t + 1) * P], slot[t])
                last = tr(ps[3][0:E, (2 + t) * P:(3 + t) * P], wt[t])
            last.then_inc(s["tr_mm"], 1)
            pe.wait_ge(s["cnt_ready"], 1)
            mm(ps[2][0:E, 1:2], tri[0:E, 0:E], cx, True, True)
            mm(ps[2][0:1, 2:3], ones[0:E, 0:1], cx, True, True).then_inc(s["start_mm"], 1)
            pe.wait_ge(s["oh_ready"], 1)
            for t in range(TT):
                o = ps[4 + t]
                mm(o[:, 0:ITEMS], slT[:, t * P:(t + 1) * P], oh, True, False)
                mm(o[:, 0:ITEMS], neg, ohc, False, True)
                mm(o[:, 64:64 + ITEMS], wtT[:, t * P:(t + 1) * P], oh, True, True)
            mm(ps[6][0:1, 0:ITEMS], cst[0:E, C_PI:C_PI + 1], oh, True, True).then_inc(s["item_mm"], 1)
            pe.wait_ge(s["expert_rows"], 32)

            def gather(w):
                pe.wait_ge(s["pick_ready"], w + 1)
                if not isinstance(w, int):
                    pe.wait_ge(s["xg_ready"], w)
                for k in range(KD):
                    for t in range(TT):
                        last = mm(ps[2][:, k * SLOTS:(k + 1) * SLOTS], x2[:, t, k * P:(k + 1) * P], pick[:, t, :],
                                  k == 0 and t == 0, t == TT - 1)
                last.then_inc(s["gathered"], 1)

            def turn_last(w1):
                pe.wait_ge(s["w_pickw"], w1)
                pe.wait_ge(s["added1"], w1)
                for t in range(TT):
                    last = tr(ps[5][:, t * P:(t + 1) * P], pickw[:, t, :, :].rearrange("p a b -> p (a b)"))
                last.then_inc(s["ct_mm"], 1)

            def add_last(w):
                pe.wait_ge(s["ct_ready"], w + 1)
                pe.wait_ge(s["ysl_ready"], w + 1)
                pe.wait_ge(s["added0"], w + 1)
                for t, sm in ((0, "comb0"), (1, "comb1")):
                    for b in range(2):
                        hs = slice(SLOTS * b, SLOTS * (b + 1))
                        last = mm(ps[(6, 4)[t] + b][:, :], ctr[hs, t * P:(t + 1) * P], ysl[hs, :], True, True)
                    last.then_inc(s[sm], 1)

            pe.wait_ge(s["idx_ready"], 1)
            gather(0)
            n_items = pe.value_load(idx[0:1, ITEMS:ITEMS + 1], min_val=E, max_val=ITEMS - 1)
            n_plus = pe.value_load(idx[0:1, ITEMS + 1:ITEMS + 2], min_val=E + 1, max_val=ITEMS)
            with pe.Fori(0, n_items) as w:
                turn_last(pe.snap(w + 1))
                pe.wait_ge(s["xg_ready"], w + 1)
                pe.wait_ge(s["h_done"], w + 1)
                pe.wait_ge(s["ohb_ready"], w + 1)
                for k in range(-1, KD):
                    if k >= 0:
                        pe.wait_ge(landed[k], 16 * (w + 1))
                    lhs, wk = (ohb, bgu) if k < 0 else (xgT[:, k, :], ring[:, k, :])
                    wv = wk.rearrange("p (h f g) -> p g h f", h=2, g=2)
                    for g in range(2):
                        for h in range(2):
                            last = mm(ps[g][SLOTS * h:SLOTS * (h + 1), :], lhs, wv[:, g, h, :], k < 0, k == KD - 1)
                    if k >= 0:
                        last.then_inc(s["piece_used"], 1)
                add_last(w)
                pe.wait_ge(s["h_done"], w + 2)
                for c in range(4):
                    last = tr(ps[3][:, c * P:(c + 1) * P], up[:, c * P:(c + 1) * P])
                last.then_inc(s["h_turned"], 1)
                gather(w + 1)
                pe.wait_ge(s["hT_ready"], w + 1)
                pe.wait_ge(s["added1"], w + 2)
                for h in range(2):
                    last = mm(ps[4][SLOTS * h:SLOTS * (h + 1), :], ohb, bdn[:, 512 * h:512 * h + 512], True, False)
                last.then_inc(s["ohb_used"], 1)
                for k in range(KD):
                    if k % 2 == 0:
                        pe.wait_ge(landed[KD + k // 2], 16 * (w + 1))
                    wv = ring[:, KD + k // 2, (k % 2) * D:(k % 2 + 1) * D]
                    for h in range(2):
                        last = mm(ps[4][SLOTS * h:SLOTS * (h + 1), :], hT[:, k % 4, k // 4, :], wv[:, 512 * h:512 * h + 512],
                                  False, k == KD - 1)
                    if k % 2 == 1:
                        last.then_inc(s["piece_used"], 1)
            turn_last(n_plus)
            add_last(n_items)

        @block.vector
        def _(dve):
            n_dch = [0]
            V = nc.vector

            def link(ins):
                n_dch[0] += 1
                ins.then_inc(s["dch"], 1)
                dve.wait_ge(s["dch"], n_dch[0])

            def tt(o, i0, i1, op):
                return V.tensor_tensor(out=o, in0=i0, in1=i1, op=op)

            def ts(o, i, s1, s2, op0, op1=None):
                return V.tensor_scalar(o, i, s1, s2, op0, op1) if op1 is not None else V.tensor_scalar(o, i, s1, None, op0)

            def stt(o, i0, sc, i1, op0, op1):
                return V.scalar_tensor_tensor(out=o, in0=i0, scalar=sc, in1=i1, op0=op0, op1=op1)

            def wide(col, n):
                return col.unsqueeze(2).to_broadcast([col.shape[0], col.shape[1], n])

            MU, AD, SU = ALU.mult, ALU.add, ALU.subtract
            V.memset(zero_c[:, 0:1], 0.0)
            V.memset(zero_c[:, 2:3], EPS)
            link(V.memset(zero_c[:, 1:2], float(np.float32(np.pi / 2))))
            for t in range(TT):
                dve.wait_ge(s["xload%d" % t], 16)
                link(V.tensor_tensor_reduce((xs, xs2)[t], x[:, t, :], x[:, t, :], 1.0, 0.0, MU, AD, small[:, 4 + t:5 + t]))
                ts(small[:, 4 + t:5 + t], small[:, 4 + t:5 + t], 1.0 / D, EPS, MU, AD).then_inc(s["var_in"], 1)
            for t in range(TT):
                dve.wait_ge(s["root_out"], t + 1)
                link(V.reciprocal(small[:, 6 + t:7 + t], small[:, 4 + t:5 + t]))
                ts((xs, xs2)[t], x[:, t, :], small[:, 6 + t:7 + t], None, MU).then_inc(s["xs_ready"], 1)
            dve.wait_ge(s["meta"], 16)
            link(V.tensor_tensor_reduce(xmn, xm[:, :], xm[:, :], 1.0, 0.0, MU, AD, small[0:META, 8:9]))
            ts(small[0:META, 8:9], small[0:META, 8:9], 1.0 / D, EPS, MU, AD).then_inc(s["var_in"], 1)
            dve.wait_ge(s["root_out"], 3)
            link(V.reciprocal(small[0:META, 9:10], small[0:META, 8:9]))
            ts(xmn, xm[:, :], small[0:META, 9:10], None, MU).then_inc(s["xs_ready"], 1)
            dve.wait_ge(s["rows_turned"], 1)
            link(V.tensor_copy(pcol[:, :], ps[6][:, 0:32]))
            gain1, gain2 = pcol[:, 0:8], pcol[:, 8:16]
            for t in range(TT):
                dve.wait_ge(s["turned_x"], t + 1)
                for b in range(2):
                    tt(xnT[:, 4 * b:4 * b + 4, META + t * P:META + (t + 1) * P],
                       ps[2 * t + b][:, :].rearrange("p (a n) -> p a n", a=4), wide(gain1[:, 4 * b:4 * b + 4], P), MU)
            dve.wait_ge(s["turned_m"], 1)
            tt(xnT[:, :, 0:META], ps[5][:, 0:KD * META].rearrange("p (a n) -> p a n", a=KD), wide(gain1, META), MU)\
                .then_inc(s["xnT_ready"], 1)
            R = lambda j: s5r[:, j, :]
            R2 = lambda j: s5r[:, j, :].rearrange("p (g n) -> p g n", g=2)
            dt2 = wide(small[0:ST, 2:4], 64)
            dve.wait_ge(s["s5r_exp"], 1)
            tt(R2(2), R2(0), dt2, MU).then_inc(s["s5r_v"], 1)
            link(tt(R2(3), R2(1), dt2, MU))
            link(ts(R(6), R(3), float(1 / (2 * np.pi)), MAGIC, MU, AD))
            link(ts(R(6), R(6), MAGIC, None, SU))
            c1 = 6.28125
            c2 = float(np.float32(2 * np.pi - c1) // 2 ** -19 * 2 ** -19)
            c3 = float(2 * np.pi - c1 - c2)
            for c in (c1, c2, c3):
                link(stt(R(3), R(6), -c, R(3), MU, AD))
            link(ts(R(5), R(3), float(1 / (2 * np.pi)), 0.5, MU, ALU.min))
            ts(R(5), R(5), -0.5, None, ALU.max).then_inc(s["s5r_ang"], 1)
            dve.wait_ge(s["s5r_exp"], 2)
            dve.wait_ge(s["s5r_sin"], 2)
            link(tt(R(7), R(7), R(7), MU))
            link(tt(R(7), R(7), R(4), MU))
            link(stt(R(7), R(7), -2.0, R(4), MU, AD))
            link(ts(R(7), R(7), -1.0, None, AD))
            link(tt(R(6), R(6), R(4), MU))
            q1, q2, q3 = s5q[:, 0, :], s5q[:, 1, :], s5q[:, 2, :]
            tt(q1, R(0), R(0), MU)
            link(tt(q2, R(1), R(1), MU))
            link(tt(q1, q1, q2, AD))
            link(V.reciprocal(q1, q1))
            tt(q2, R(7), R(0), MU)
            link(tt(q3, R(6), R(1), MU))
            link(tt(q2, q2, q3, AD))
            link(tt(R(2), q2, q1, MU))
            tt(q2, R(6), R(0), MU)
            link(tt(q3, R(7), R(1), MU))
            link(tt(q2, q2, q3, SU))
            tt(R(3), q2, q1, MU).then_inc(s["s5r_v"], 1)

            dve.wait_ge(s["s5rows_turned"], 1)
            V.tensor_copy(s5c[:, :, :], ps[7][:, 0:4 * ST].rearrange("p (a n) -> p a n", a=4)).then_inc(s["s5cols_ready"], 1)
            dve.wait_ge(s["s5cols_ready"], 1)
            dve.wait_ge(s["bload"], 32)
            dve.wait_ge(s["consts"], 16)
            cr, ci = wide(s5c[:, 2, :], 16), wide(s5c[:, 3, :], 16)
            tt(bb[0], bre, cr, MU)
            tt(bb[1], bim, ci, MU)
            tt(bb[2], bre, ci, MU)
            link(tt(bb[3], bim, cr, MU))
            tt(bb[0], bb[0], bb[1], SU)
            link(tt(bb[2], bb[2], bb[3], AD))
            for c in range(2):
                for g in range(2):
                    o = bz[:, c, :, :].rearrange("p t (i g h) -> p (t i) g h", i=4, g=2)[:, :, g, :]
                    last = ts(o, bb[2 * c], cst[:, C_GB + g:C_GB + g + 1], None, MU)
            dve.wait_ge(s["cload"], 32)
            for c in range(2):
                for g in range(2):
                    last = ts(cz[:, c, :, g * 64:(g + 1) * 64], cn[:, c], cst[:, C_GC + g:C_GC + g + 1], (1.0, -1.0)[c], MU, MU)
            last.then_inc(s["bz_ready"], 1)

            def fraction(i):
                dve.wait_ge(s["ph"], i + 1)
                if i >= 2:
                    dve.wait_ge(s["sines"], i - 1)
                link(ts(rnd, turns, MAGIC, None, AD))
                stt(frac[i % 2], rnd, MAGIC, turns, SU, SU).then_inc(s["rounded"], 1)

            fraction(0)
            dve.wait_ge(s["b_turned"], 1)
            for c in range(2):
                last = V.tensor_copy(blk[:, c, :, :], ps[2 + c][:, :].rearrange("p (a n) -> p a n", a=4))
            last.then_inc(s["b_laid"], 1)
            dve.wait_ge(s["c_turned"], 1)
            for c in range(2):
                last = V.tensor_copy(blk[:, 2 + c, :, :], ps[4 + c][:, :].rearrange("p (a n) -> p a n", a=4))
            last.then_inc(s["c_laid"], 1)
            fraction(1)
            for i in range(ST):
                re, im = ps[2 + 2 * (i % 2)][:, 0:TOK], ps[3 + 2 * (i % 2)][:, 0:TOK]
                sn, co = sinT[i % 2], cosT[i % 2]
                if i >= 1:
                    dve.wait_ge(s["xs5"], i)
                dve.wait_ge(s["bu"], i + 1)
                dve.wait_ge(s["sines"], i + 1)
                tt(rot[0], re, co, MU)
                tt(rot[1], im, sn, MU)
                tt(rot[2], im, co, MU)
                link(tt(rot[3], re, sn, MU))
                tt(rot[0], rot[0], rot[1], AD).then_inc(s["bu_free"], 1)
                link(tt(rot[2], rot[2], rot[3], SU))
                r = s5c[:, 0, i:i + 1].to_broadcast([P, TOK])
                V.tensor_tensor_scan(zre, r, rot[0], 0.0, MU, AD)
                link(V.tensor_tensor_scan(zim, r, rot[2], 0.0, MU, AD))
                z = slice(META, TOK)
                if i >= 2:
                    dve.wait_ge(s["ysum"], i - 1)
                tt(rot[0][:, z], zre[:, z], co[:, z], MU)
                tt(rot[1][:, z], zim[:, z], sn[:, z], MU)
                tt(rot[2][:, z], zre[:, z], sn[:, z], MU)
                link(tt(rot[3][:, z], zim[:, z], co[:, z], MU))
                tt(xre[i % 2][:, z], rot[0][:, z], rot[1][:, z], SU)
                tt(xim[i % 2][:, z], rot[2][:, z], rot[3][:, z], AD).then_inc(s["xs5"], 1)
                if i + 2 < ST:
                    fraction(i + 2)
            dve.wait_ge(s["ysum"], ST)
            for t in range(KW):
                last = stt(y5[:, t, :], uT[:, t, META:TOK], pcol[:, 28 + t:29 + t],
                           ps[6 + t // 2][:, (t % 2) * SEQ:(t % 2 + 1) * SEQ], MU, AD)
            link(last)
            link(tt(yt, y5, y5, MU))
            link(ts(yt, yt, 0.044715, 1.0, MU, AD))
            tt(yt, yt, y5, MU).then_inc(s["gelu_in"], 1)
            tt(small[:, 16:20], pcol[:, 20:24], pcol[:, 16:20], SU).then_inc(s["acol"], 1)
            dve.wait_ge(s["gelu_sig"], 1)
            tt(g5, y5, yt, MU).then_inc(s["g5_ready"], 1)
            dve.wait_ge(s["q_sig"], 1)
            tt(qT, qT, sg, MU).then_inc(s["kq_ready"], 1)
            dve.wait_ge(s["acol"], 2)
            link(ts(small[:, 24:28], small[:, 20:24], -1.0, 1.0, MU, AD))
            dve.wait_ge(s["f_sig"], 1)
            for h in range(HEADS):
                last = ts(fT[:, h, :], fT[:, h, :], small[:, 24 + h:25 + h], small[:, 20 + h:21 + h], MU, AD)
            last.then_inc(s["f_ready"], 1)
            dve.wait_ge(s["f_ready"], 1)
            link(ts(kT, fT, -1.0, 1.0, MU, AD))
            dve.wait_ge(s["glu_sig"], 1)
            tt(y5, g5, sg, MU).then_inc(s["y5_ready"], 1)
            V.tensor_copy(kc.rearrange("p (a n) -> p a n", a=KW), kT[:, :, META:TOK]).then_inc(s["kq_ready"], 1)
            dve.wait_ge(s["og_sig"], 1)
            for h in range(HEADS):
                link(stt(ogT[:, h, :], ogT[:, h, :], pcol[:, 24 + h:25 + h], yt[:, h, :], MU, MU))
            dve.wait_ge(s["logf"], 1)
            chunk = ((0, META), (META, META + P), (META + P, TOK))
            one = ones[:, 0:1]
            dve.wait_ge(s["ones_set"], 1)
            for h in range(HEADS):
                for lo, hi in chunk:
                    last = V.tensor_tensor_scan(bT[:, h, lo:hi], one.to_broadcast([P, hi - lo]), bT[:, h, lo:hi], 0.0, MU, AD)
            link(last)
            for lo, hi in chunk[:2]:
                last = tt(kh[:, :, lo:hi], bT[:, :, hi - 1:hi].to_broadcast([P, HEADS, hi - lo]), bT[:, :, lo:hi], SU)
            last.then_inc(s["kh_in"], 1)
            V.tensor_copy(bc.rearrange("p (a n) -> p a n", a=KW), bT[:, :, META:TOK]).then_inc(s["eb_in"], 1)

            def level_decay(n):
                m = LEVELS[n]
                if n >= 1:
                    dve.wait_ge(s["level_in"], n)
                b = bc.rearrange("p (c m) -> p c m", m=2 * m)
                d = dec.rearrange("p (c m) -> p c m", m=2 * m)
                mid = b[:, :, m - 1:m].to_broadcast([P, 1024 // (2 * m), m])
                tt(d[:, :, 0:m], mid, b[:, :, 0:m], SU)
                tt(d[:, :, m:2 * m], b[:, :, m:2 * m], mid, SU).then_inc(s["decay_in"], 1)

            dve.wait_ge(s["eb_in"], 1)
            level_decay(0)
            dve.wait_ge(s["kh_exp"], 1)
            tt(kh, kh, kT[:, :, 0:META + P], MU).then_inc(s["kh_ready"], 1)
            dve.wait_ge(s["eb_out"], 1)
            tt(qe, eb, qT.rearrange("p a b -> p (a b)"), MU).then_inc(s["qe_ready"], 1)
            dve.wait_ge(s["diag_mm"], 1)
            for b in range(2):
                last = tt(stot[:, 4 * b:4 * b + 4, :], ps[4 + b][:, :].rearrange("p (a n) -> p a n", a=4),
                          ident.unsqueeze(1).to_broadcast([P, 4, P]), MU)
            link(last)
            qf = qT.rearrange("p a b -> p (a b)")
            stf = stot.rearrange("p a b -> p (a b)")

            def level_sum(n):
                m = LEVELS[n]
                dve.wait_ge(s["level_mm"], n + 1)
                mk = cst[:, C_MASK + 64 * n:C_MASK + 64 * (n + 1)].unsqueeze(1).to_broadcast([P, 8, 64])
                ins = tt(tmpl, ps[2 + n % 2][:, :].rearrange("p (a n) -> p a n", a=8), mk, MU)
                ins.then_inc(s["level_used"], 1)
                dve.wait_ge(s["level_used"], n + 1)
                so = stf.rearrange("p (c m) -> p c m", m=2 * m)[:, :, m:2 * m]
                ins = tt(so, so, tmpl.rearrange("p a b -> p (a b)").rearrange("p (c m) -> p c m", m=m), AD)
                if n == len(LEVELS) - 1:
                    ins.then_inc(s["stot_ready"], 1)
                else:
                    link(ins)

            for n, m in enumerate(LEVELS):
                dve.wait_ge(s["decay_out"], n + 1)
                if n >= 1:
                    dve.wait_ge(s["level_mm"], n)
                g3 = lambda t: t.rearrange("p (c m) -> p c m", m=2 * m)
                tt(g3(qk)[:, :, 0:m], g3(dec)[:, :, 0:m], g3(kc)[:, :, 0:m], MU)
                tt(g3(qk)[:, :, m:2 * m], g3(dec)[:, :, m:2 * m], g3(qf)[:, :, m:2 * m], MU).then_inc(s["level_in"], 1)
                if n + 1 < len(LEVELS):
                    level_decay(n + 1)
                if n == 1:
                    dve.wait_ge(s["kh_turned"], 1)
                    V.tensor_copy(khTm, ps[6][0:META, :])
                    V.tensor_copy(khT, ps[7][:, :].rearrange("p (a n) -> p a n", a=4)).then_inc(s["khT_ready"], 1)
                if n >= 1:
                    level_sum(n - 1)
            level_sum(len(LEVELS) - 1)
            dve.wait_ge(s["st_mm"], 1)
            link(V.tensor_copy(st0, ps[6][:, :].rearrange("p (a n) -> p a n", a=4)))
            for h in range(HEADS):
                last = stt(st1[:, h, :], st0[:, h, :], eb[:, h * SEQ + P - 1:h * SEQ + P], ps[7][:, h * P:(h + 1) * P], MU, AD)
            last.then_inc(s["st1_ready"], 1)
            for b in range(2):
                dve.wait_ge(s["o2_ready"], b + 1)
                tt(orn[:, 512 * b:512 * b + 512], ps[4 + b][:, :], ogT[:, 2 * b:2 * b + 2, :].rearrange("p a b -> p (a b)"), MU)
            def merge(br, b):
                dve.wait_ge(s["gate_sig"], 2 * br + 2)
                dve.wait_ge(s["br_mm"], 8 * br + 2 * b + 2)
                return tt((mrg[:, 2 * b:2 * b + 2, 0:SEQ], gates[:, KD + 2 * b:KD + 2 * b + 2, :])[br],
                          ps[4 * br + b][:, :].rearrange("p (a n) -> p a n", a=2),
                          gates[:, br * KD + 2 * b:br * KD + 2 * b + 2, :], MU)

            link(merge(0, 0))
            dve.wait_ge(s["rms_out"], 1)
            link(V.reciprocal(rms[:, 8:16], rms[:, 0:8]))
            tt(qe.rearrange("p (a n) -> p a n", a=8), wide(rms[:, 8:16], P), ident.unsqueeze(1).to_broadcast([P, 8, P]), MU)\
                .then_inc(s["diag_ready"], 1)
            merge(0, 1)
            dve.wait_ge(s["inv_mm"], 1)
            for b in range(2):
                tt(yh[:, 2 * b:2 * b + 2, :], orn[:, 512 * b:512 * b + 512].rearrange("p (a n) -> p a n", a=2),
                   ps[6 + b][:, :].rearrange("p (a n) -> p a n", a=2), MU).then_inc(s["yh_ready"], 1)
            for b in range(2, 4):
                merge(0, b)
            for b in range(4):
                link(merge(1, b))
                tt(mrg[:, 2 * b:2 * b + 2, 0:SEQ], mrg[:, 2 * b:2 * b + 2, 0:SEQ], gates[:, KD + 2 * b:KD + 2 * b + 2, :], AD)\
                    .then_inc(s["mrg_ready"], 1)
            for t in range(TT):
                for b in range(2):
                    dve.wait_ge(s["wo_mm"], 2 * t + b + 1)
                    last = tt(x[:, t, 512 * b:512 * b + 512], ps[2 * t + b][:, :], x[:, t, 512 * b:512 * b + 512], AD)
                link(last)
                link(V.tensor_tensor_reduce(x2[:, t, :], x[:, t, :], x[:, t, :], 1.0, 0.0, MU, AD, small[:, 32 + t:33 + t]))
                ts(small[:, 32 + t:33 + t], small[:, 32 + t:33 + t], 1.0 / D, EPS, MU, AD).then_inc(s["var_in"], 1)
                dve.wait_ge(s["root_out"], 4 + t)
                link(V.reciprocal(small[:, 34 + t:35 + t], small[:, 32 + t:33 + t]))
                ts(x2[:, t, :], x[:, t, :], small[:, 34 + t:35 + t], None, MU).then_inc(s["x2_ready"], 1)
            for t in range(TT):
                dve.wait_ge(s["x2_turned"], t + 1)
                for b in range(2):
                    last = tt(x2T[:, 4 * b:4 * b + 4, t * P:(t + 1) * P], ps[4 + 2 * t + b][:, :].rearrange("p (a n) -> p a n", a=4),
                              wide(gain2[:, 4 * b:4 * b + 4], P), MU)
                last.then_inc(s["x2T_ready"], 1)
            both = range(TT)
            dve.wait_ge(s["logit_mm"], TT)
            link([V.tensor_copy(lg[t], ps[t][:, 0:E]) for t in both][-1])
            link([V.max(mx[t], lg[t]) for t in both][-1])
            for t in both:
                ts(nmx[t], mx[t][:, 0:1], -1.0, None, MU).then_inc(s["logits_in"], 1)
            link([V.max_index(ix[:, t, :], mx[t], lg[t]) for t in both][-1])
            link([V.tensor_copy(ixf[t], ix[:, t, 0:TOPK]) for t in both][-1])
            link([ts(mask[t], iota_e, ixf[t][:, 0:1], None, ALU.is_equal) for t in both][-1])
            for k in range(1, TOPK):
                last = [stt(mask[t], iota_e, ixf[t][:, k:k + 1], mask[t], ALU.is_equal, AD) for t in both][-1]
                if k < TOPK - 1:
                    link(last)
            last.then_inc(s["mask_ready"], 1)
            dve.wait_ge(s["mask_ready"], 1)
            dve.wait_ge(s["exped"], TT)
            link([tt(ex[t], ex[t], mask[t], MU) for t in both][-1])
            link([V.tensor_reduce(den[t], ex[t], AX, AD) for t in both][-1])
            link([V.reciprocal(den[t], den[t]) for t in both][-1])
            for t in both:
                ts(wt[t], ex[t], den[t], None, MU)
            dve.wait_ge(s["rank_mm"], 1)
            link([stt(slot[t], mask[t], 4096.0, ps[t][:, 0:E], MU, AD) for t in both][-1])
            for t in both:
                last = ts(slot[t], slot[t], -4096.0, None, AD)
            last.then_inc(s["slot_ready"], 1)
            link(V.tensor_copy(cnt, ps[2][0:E, 0:1]))
            link(ts(cx, cnt, float(SLOTS), None, ALU.is_gt))
            for j in (2, 3):
                ins = stt(cx, cnt, float(SLOTS * j), cx, ALU.is_gt, AD)
                if j == 2:
                    link(ins)
            ins.then_inc(s["cnt_ready"], 1)
            V.memset(neg, -float(SLOTS))
            V.memset(ohc[:, 0:E], 0.0)
            V.tensor_copy(oh[:, 0:E], ident[0:E, 0:E])
            dve.wait_ge(s["start_mm"], 1)
            link(V.tensor_copy(first, ps[2][0:E, 1:2]))
            js, ja, jb = j3[:, 0:EXTRA], j3[:, 16:32], j3[:, 32:48]
            link(ts(js, iota_e[0:E, 0:EXTRA], first, None, SU))
            ts(ja, js, 0.0, None, ALU.is_ge)
            link(ts(jb, js, cx, None, ALU.is_lt))
            link(tt(oh[:, E:ITEMS], ja, jb, MU))
            link(ts(js, js, 1.0, None, AD))
            tt(ohc[:, E:ITEMS], js, oh[:, E:ITEMS], MU)
            dve.wait_ge(s["tr_mm"], 1)
            V.tensor_copy(slT, ps[3][0:E, 0:SEQ])
            V.tensor_copy(wtT, ps[3][0:E, SEQ:2 * SEQ]).then_inc(s["oh_ready"], 1)
            dve.wait_ge(s["item_mm"], 1)
            V.tensor_copy(idx[0:1, 0:ITEMS], ps[6][0:1, 0:ITEMS]).then_inc(s["added0"], 1)
            ts(idx[0:1, ITEMS + 1:ITEMS + 2], ps[2][0:1, 2:3], float(E + 1), None, AD)
            ts(idx[0:1, ITEMS:ITEMS + 1], ps[2][0:1, 2:3], float(E), None, AD).then_inc(s["idx_ready"], 1)
            for t in range(TT):
                V.tensor_copy(islot[:, t, :], ps[4 + t][:, 0:ITEMS])
                V.tensor_copy(iwt[:, t, :], ps[4 + t][:, 64:64 + ITEMS]).then_inc(s[("h_done", "added1")[t]], 1)
            dve.wait_ge(s["added1"], 1)

            def picks(w):
                for t in range(TT):
                    last = ts(pick[:, t, :], iota_s, islot[:, t, bass.ds(w, 1)], None, ALU.is_equal)
                return last

            def take_gathered(w):
                dve.wait_ge(s["gathered"], w + 1)
                tt(xgT, ps[2][:, :].rearrange("p (a n) -> p a n", a=KD), wide(gain2, SLOTS), MU).then_inc(s["xg_ready"], 1)

            def add_item(w, t):
                dve.wait_ge(s[("comb0", "comb1")[t]], w + 1)
                for b in range(2):
                    last = tt(x[:, t, 512 * b:512 * b + 512], ps[(6, 4)[t] + b][:, :], x[:, t, 512 * b:512 * b + 512], AD)
                last.then_inc(s[("added0", "added1")[t]], 1)

            def expert_of(w):
                return V.tensor_copy(ohb[0:E, :], oh[:, bass.ds(w, 1)].to_broadcast([E, SLOTS]))

            picks(0).then_inc(s["pick_ready"], 1)
            V.memset(ysl, 0.0).then_inc(s["ysl_ready"], 1)
            V.memset(pickw, 0.0).then_inc(s["w_pickw"], 1)
            dve.wait_ge(s["pad_zero"], 1)
            expert_of(0).then_inc(s["ohb_ready"], 1)
            n_items = dve.value_load(idx[0:1, ITEMS:ITEMS + 1], min_val=E, max_val=ITEMS - 1)
            take_gathered(0)
            with dve.Fori(0, n_items) as w:
                picks(w + 1).then_inc(s["pick_ready"], 1)
                dve.wait_ge(s["piece_used"], w * PIECES + KD)
                ts(gt, ps[0][:, :], LIMIT, None, ALU.min).then_inc(s["gate_in"], 1)
                ts(up, ps[1][:, :], LIMIT, -LIMIT, ALU.min, ALU.max).then_inc(s["w_gate"], 1)
                dve.wait_ge(s["w_gate"], w + 1)
                stt(up, up, 1.0, gt, AD, MU).then_inc(s["w_up"], 1)
                dve.wait_ge(s["w_up"], w + 1)
                dve.wait_ge(s["gate_sg"], w + 1)
                tt(up, up, sgm, MU).then_inc(s["h_done"], 1)
                add_item(w, 0)
                dve.wait_ge(s["h_turned"], w + 1)
                V.tensor_copy(hT, ps[3][:, :].rearrange("p (a b c) -> p a b c", a=4, b=2)).then_inc(s["hT_ready"], 1)
                add_item(w, 1)
                dve.wait_ge(s["ct_mm"], w + 1)
                for t in range(TT):
                    for h in range(2):
                        last = ts(pickw[:, t, h, :], iota_s, islot[:, t, bass.ds(w, 1)], iwt[:, t, bass.ds(w, 1)],
                                  ALU.is_equal, MU)
                last.then_inc(s["w_pickw"], 1)
                take_gathered(w + 1)
                dve.wait_ge(s["ohb_used"], w + 1)
                expert_of(w + 1).then_inc(s["ohb_ready"], 1)
            add_item(n_items, 0)
            add_item(n_items, 1)
            dve.wait_ge(s["added1"], n_items + 2)
            dve.wait_ge(s["lastgain"], 16)
            for t in range(TT):
                link(V.tensor_tensor_reduce(x2[:, t, :], x[:, t, :], x[:, t, :], 1.0, 0.0, MU, AD, small[:, 40 + t:41 + t]))
                ts(small[:, 40 + t:41 + t], small[:, 40 + t:41 + t], 1.0 / D, EPS, MU, AD).then_inc(s["var_in"], 1)
                dve.wait_ge(s["root_out"], 6 + t)
                link(V.reciprocal(small[:, 42 + t:43 + t], small[:, 40 + t:41 + t]))
                stt(x2[:, t, :], x[:, t, :], small[:, 42 + t:43 + t], fgain, MU, MU).then_inc(s["w_last"], 1)


_INS = ["x", "meta_tokens", "norm1_gain", "w_in", "s5_lambda_re", "s5_lambda_im", "s5_log_dt", "s5_b_re",
        "s5_b_im", "s5_c_re", "s5_c_im", "s5_d", "s5_w_glu", "hgrn_lb_logits", "hgrn_norm_gain", "w_branch_s5",
        "w_branch_hgrn", "w_out", "norm2_gain", "w_router", "b_router", "w_gate_up", "b_gate_up", "w_down",
        "b_down", "final_norm_gain"]


def kernel(**inputs):
    import concourse.bacc as bacc
    from concourse.bass_utils import run_bass_kernel_spmd

    nc = bacc.Bacc("TRN2", target_bir_lowering=False, num_devices=1)
    arrays = {n: np.ascontiguousarray(inputs[n]) for n in _INS}
    arrays["shape_consts"] = shape_constants()
    feeds, views = {}, {}
    for n, v in arrays.items():
        feeds[f"in_{n}"] = v
        views[n] = nc.dram_tensor(f"in_{n}", v.shape, mybir.dt.from_np(v.dtype), kind="ExternalInput").ap()
    out = nc.dram_tensor("out_0", (1, SEQ, D), F32, kind="ExternalOutput").ap()
    build(nc, views, out)
    r = run_bass_kernel_spmd(nc, [feeds], core_ids=[0])
    return r.results[0]["out_0"]
```

```python
from contextlib import ExitStack

import numpy as np
import concourse.bass as bass
from concourse import mybir

F32 = mybir.dt.float32
I32 = mybir.dt.int32
U32 = mybir.dt.uint32
ALU = mybir.AluOpType
ACT = mybir.ActivationFunctionType
AX = mybir.AxisListType.X

P = 128
META, SEQ = 16, 256
TOK = META + SEQ
D = 1024
KD = D // P
W5 = 512
KW = W5 // P
HEADS = 4
STATES = 32 * 64
ST = STATES // P
TT = SEQ // P
E = 32
TOPK = 4
LATE = 5
SLOTS = 64
EXTRA = 16
ITEMS = E + EXTRA
PIECES = 12
DOWN = PIECES - KD
PC = 2048
EPS = 1e-6
LIMIT = 7.0
LEVELS = [64, 32, 16, 8, 4, 2, 1]
MAGIC = 1.5 * 2.0 ** 23
TWO_PI = 6.2831850
GELU_C = 2 * 0.7978845608028654

C_ID, C_TRI, C_MASK = 0, P, 2 * P
C_T = C_MASK + len(LEVELS) * 64
C_IE = C_T + TOK
C_IS = C_IE + E
C_GC = C_IS + SLOTS
C_GB = C_GC + 2
C_PI = C_GB + 2
C_SEL = C_PI + 1
C_ALL = C_SEL + META


def shape_constants():
    c = np.zeros((P, C_ALL), np.float32)
    p = np.arange(P)
    c[:, C_ID:C_ID + P] = np.eye(P)
    c[:, C_TRI:C_TRI + P] = p[:, None] < p[None, :]
    for n, m in enumerate(LEVELS):
        i = np.array([b * 2 * m + m + r for b in range(64 // m) for r in range(m)])
        same = p[:, None] // (2 * m) == i[None, :] // (2 * m)
        left = p[:, None] % (2 * m) < m
        c[:, C_MASK + 64 * n:C_MASK + 64 * (n + 1)] = same & left
    c[:, C_T:C_T + TOK] = np.arange(TOK)
    c[:, C_IE:C_IE + E] = np.arange(E)
    c[:, C_IS:C_IS + SLOTS] = np.arange(SLOTS)
    for g in range(2):
        c[:, C_GC + g] = (p // 16) % 2 == g
        c[:, C_GB + g] = p // 64 == g
    c[:, C_PI] = p
    c[:, C_SEL:C_SEL + META] = p[:, None] % 32 == np.arange(META)
    return c


def build(nc, a, out):
    with ExitStack() as ctx:
        def sb(name, shape, dt=F32):
            return ctx.enter_context(nc.sbuf_tensor(name, shape, dt))

        def sem(name):
            return ctx.enter_context(nc.semaphore(name))

        ring = sb("ring", [P, PIECES + DOWN, PC])
        cst = sb("cst", [P, C_ALL])
        x = sb("x", [P, TT, D])
        gates = sb("gates", [P, 2 * KD, SEQ])
        w_mix = sb("w_mix", [P, 10240])
        ones = sb("ones", [P, P])
        prow = sb("prow", [32, P])
        pcol = sb("pcol", [P, 32])
        s5c = sb("s5c", [P, 4, ST])
        small = sb("small", [P, 64])
        rms = small[:, 48:64]
        zero_c = sb("zero_c", [P, 4])
        rout = sb("rout", [P, 1400])
        ix = sb("ix", [P, TT, 8], U32)
        idx = sb("idx", [1, ITEMS + 4], I32)

        def at(t, lo, *dims):
            n = int(np.prod(dims))
            v = t[:, lo:lo + n]
            if len(dims) == 1:
                return v
            names = "abcd"[:len(dims)]
            return v.rearrange("p (%s) -> p %s" % (" ".join(names), " ".join(names)),
                               **{k: d for k, d in zip(names, dims)})

        ringf = ring[:, :, :].rearrange("p a b -> p (a b)")
        ident = cst[:, C_ID:C_ID + P]
        tri = cst[:, C_TRI:C_TRI + P]
        steps = cst[:, C_T:C_T + TOK]
        iota_e = cst[:, C_IE:C_IE + E]
        iota_s = cst[:, C_IS:C_IS + SLOTS]
        L0 = PIECES * PC
        xnT = at(ringf, L0, KD, TOK)
        uT = at(ringf, L0 + 2176, KW, TOK)
        v_a = at(ringf, L0 + 3264, TT, W5)
        v_m = ringf[0:META, L0 + 4288:L0 + 4288 + W5]
        ogT = at(ringf, L0 + 4800, KW, SEQ)
        blk = at(ringf, L0 + 5824, 4, 4, P)
        win = [at(ringf, s * 4096, KD, 512) for s in range(2)]
        qT = at(ringf, 4 * PC, KW, SEQ)
        kT = at(ringf, 4 * PC + 1024, KW, TOK)
        bT = at(ringf, 4 * PC + 2112, KW, TOK)
        xmn = ringf[0:META, 4 * PC:4 * PC + D]
        xm = ringf[0:META, 4 * PC + 1024:4 * PC + 1024 + D]
        s5r = at(ringf[0:ST], 4 * PC + 2112, 8, P)
        s5q = at(ringf[0:ST], 4 * PC + 3136, 3, P)
        B0 = 6 * PC
        NT = TOK
        turns = at(ringf, B0, NT)
        rnd = at(ringf, B0 + NT, NT)
        absf = at(ringf, B0 + 2 * NT, NT)
        frac = [at(ringf, B0 + (3 + i) * NT, NT) for i in range(2)]
        sinT = [at(ringf, B0 + (5 + i) * NT, NT) for i in range(2)]
        cosT = [at(ringf, B0 + (7 + i) * NT, NT) for i in range(2)]
        rot = [at(ringf, B0 + (9 + i) * NT, NT) for i in range(4)]
        zre = at(ringf, B0 + 13 * NT, NT)
        zim = at(ringf, B0 + 14 * NT, NT)
        xre = [at(ringf, B0 + (15 + i) * NT, NT) for i in range(2)]
        xim = [at(ringf, B0 + (17 + i) * NT, NT) for i in range(2)]
        H0 = B0 + 19 * NT
        bre = at(ringf, H0, ST, 16)
        bim = at(ringf, H0 + 256, ST, 16)
        bb = [at(ringf, H0 + 512 + 256 * i, ST, 16) for i in range(4)]
        bz = at(ringf, H0 + 1536, 2, 4, P)
        cn = at(ringf, H0 + 2560, 2, 4, 64)
        cz = at(ringf, H0 + 3072, 2, 4, P)
        xs = at(ringf, H0 + 4096, D)
        xs2 = at(ringf, H0 + 5120, D)
        v_parts = xs[:, 0:W5]
        pool_rot = [at(ringf, H0 + 6144 + i * NT, NT) for i in range(2)]
        M0 = B0
        y5 = at(ringf, M0, KW, SEQ)
        yt = at(ringf, M0 + 1024, KW, SEQ)
        g5 = at(ringf, M0 + 2048, KW, SEQ)
        fT = at(ringf, M0 + 3072, KW, TOK)
        sg = at(ringf, M0 + 4160, KW, SEQ)
        bc = at(ringf, M0 + 5184, 1024)
        kc = at(ringf, M0 + 6208, 1024)
        dec = at(ringf, M0 + 7232, 1024)
        qk = at(ringf, M0 + 8256, 1024)
        stot = at(ringf, M0 + 9280, 8, P)
        tmpl = at(ringf, M0 + 10304, 8, 64)
        qe = at(ringf, M0 + 3072, 1024)
        dgs = at(ringf, M0 + 1024, 1024)
        kh = at(ringf, M0 + 10816, KW, 144)
        eb = at(ringf, M0 + 1024, 1024)
        khT = at(ringf, M0 + 4160, KW, P)
        khTm = ringf[0:META, M0 + 4672:M0 + 4672 + W5]
        st0 = at(ringf, M0 + 5184, KW, P)
        st1 = at(ringf, M0 + 5696, KW, P)
        o2 = at(ringf, M0 + 7232, 1024)
        yh = at(ringf, M0 + 8256, KW, SEQ)
        orn = at(ringf, M0 + 6208, 1024)
        w_out = at(ringf, 0, KD, D)
        mrg = at(ringf, L0, KD, SEQ)
        w_glu = at(w_mix, 0, KW, W5)
        w_b5 = at(w_mix, 2048, KW, D)
        w_bh = at(w_mix, 6144, KW, D)
        x2 = at(w_mix, 0, TT, D)
        sumT = at(w_mix, 2048, KD, SEQ)
        xgT = at(w_mix, 4096, KD, SLOTS)
        hT = at(w_mix, 4608, 4, 2, SLOTS)
        gt = at(w_mix, 5120, 512)
        sgm = at(w_mix, 5632, 512)
        up = at(w_mix, 6144, 512)
        ysl = at(w_mix, 6656, 512)
        ctr = at(w_mix, 7168, SEQ)
        pick = at(w_mix, 7424, TT, SLOTS)
        pickw = at(w_mix, 7552, TT, 2, SLOTS)
        ohb = at(w_mix, 7808, SLOTS)
        wrt = at(w_mix, 9472, KD, E)
        brt = w_mix[:, 9728:9728 + E]
        lgq = at(w_mix, 9760, TT, P)
        gatesf = gates[:, :, :].rearrange("p a b -> p (a b)")
        bgu = gatesf[:, 0:2 * D]
        bdn = gatesf[:, 2 * D:3 * D]
        fgain = gatesf[:, 3 * D:4 * D]

        ps = [ctx.enter_context(nc.psum_tensor(f"ps{i}", [P, 512], F32)) for i in range(8)]

        lg, ex, mask = ([rout[:, 64 * j + 32 * t:64 * j + 32 * t + E] for t in range(TT)] for j in range(3))
        mx = [rout[:, 320 + 8 * t:328 + 8 * t] for t in range(TT)]
        nmx = [rout[:, 336 + t:337 + t] for t in range(TT)]
        den = [rout[:, 338 + t:339 + t] for t in range(TT)]
        ixf = [rout[:, 340 + 4 * t:344 + 4 * t] for t in range(TT)]
        cnt, cx, first = (rout[0:E, 348 + j:349 + j] for j in range(3))
        neg = rout[0:E, 352:352 + P]
        oh = rout[0:E, 480:480 + ITEMS + 2]
        ohc = rout[0:E, 530:530 + EXTRA]
        j3 = rout[0:E, 578:626]
        half = rout[0:1, 626:628]
        slT = rout[0:E, 640:640 + SEQ]
        wtT = rout[0:E, 896:896 + SEQ]
        islot = at(rout, 1152, TT, ITEMS + 2)
        iwt = at(rout, 1256, TT, ITEMS + 2)
        slot, wt = ([table[:, t, 0:E] for t in range(TT)] for table in (islot, iwt))
        s = {}
        for n in """consts xload0 xload1 meta rows s5rows bload cload glu_w branch5_w branchh_w out_w expert_rows
                    router_w router_b lastgain win0 win1 out_stored
                    ones_set xs_ready turned_x xnT_ready turned_m
                    rows_turned s5rows_turned s5cols_ready s5r_exp s5r_ang s5r_sin s5r_v
                    bz_ready b_turned b_laid c_turned c_laid
                    proj proj_free bu bu_free ph rounded sines scanned xs5 ysum
                    gelu_in gelu_sig g5_ready glu_mm glu_sig f_sig q_sig og_sig f_ready logf
                    kq_ready decay_in decay_out level_in level_mm level_used diag_mm
                    eb_in eb_out kh_in kh_exp kh_ready kh_turned khT_ready st_mm st1_ready stot_ready
                    qe_ready o_mm o2_ready ms_mm yh_ready y5_ready gate_sig br_mm mrg_ready wo_mm
                    x2_ready logit_mm logits_in exped mask_ready
                    rank_mm slot_ready tr_mm cnt_ready start_mm oh_ready item_mm idx_ready
                    rms_out ohb_used mixed sum_turned sumT_ready wrt_ready inv_ready count_ready og_used xim5 pool_turned parts_mm parts_ready diag_ready inv_mm
                    pick_ready gathered xg_ready gate_in gate_sg h_done
                    ct_mm ct_ready ysl_ready comb0 comb1 added0 added1 piece_used w_last
                    acol dch ach w_gate w_up pad_zero ohb_ready h_turned hT_ready w_pickw var_in root_out""".split():
            s[n] = sem(n)
        landed = [sem(f"landed{i}") for i in range(PIECES)]

        x_d = a["x"].rearrange("b (t p) d -> p (b t) d", p=P)
        win_d = a["w_in"].rearrange("l (k p) n -> p (l k) n", p=P)
        gu_d = a["w_gate_up"].rearrange("l e (k p) n -> p (l e k) n", p=P)
        dn_d = a["w_down"].rearrange("l e (k p) n -> p (l e k) n", p=P)
        GROUPS = [0, 2, 1, 3, 4, 5, 6, 7, 8]
        NG = len(GROUPS)
        V_GROUP = 3
        SUM_PARTS = (NG, 0)
        PROJ = [(n, m) for n in range(NG) for m in range(3 if GROUPS[n] == V_GROUP else 4)]
        PROJ.insert(PROJ.index((V_GROUP + 1, 1)), SUM_PARTS)

        def up_piece(q, e, i):
            q.dma_start(ring[:, i:i + 1, :], gu_d[:, bass.ds(e * KD + i, 1), :]).then_inc(landed[i], 16)

        def down_piece(q, e, j, place):
            q.dma_start(ring[:, bass.ds(place * DOWN + (KD + j), 1), :].rearrange("p a (c n) -> p (a c) n", c=2),
                        dn_d[:, bass.ds(e * KD + 2 * j, 2), :]).then_inc(landed[KD + j], 16)

        block = ctx.enter_context(nc.Block())

        @block.sync
        def _(sp):
            for t in range(TT):
                sp.dma_start(x[:, t, :], x_d[:, t, :]).then_inc(s["xload%d" % t], 16)
            sp.dma_start(xm[:, :], a["meta_tokens"]).then_inc(s["meta"], 16)
            pr = lambda n, k: a[n].rearrange("l (k p) -> (l k) p", p=P)
            sp.dma_start(prow[0:8, :], pr("norm1_gain", 8)).then_inc(s["rows"], 16)
            sp.dma_start(prow[8:16, :], pr("norm2_gain", 8)).then_inc(s["rows"], 16)
            sp.dma_start(prow[16:24, :], pr("hgrn_lb_logits", 8)).then_inc(s["rows"], 16)
            sp.dma_start(prow[24:28, :], pr("hgrn_norm_gain", 4)).then_inc(s["rows"], 16)
            sp.dma_start(prow[28:32, :], a["s5_d"].rearrange("l (k g) h -> (l k) (g h)", k=4)).then_inc(s["rows"], 16)
            for n in range(NG):
                if n >= 2:
                    sp.wait_ge(s["proj"], 1 + max(q for q, tile in enumerate(PROJ) if tile[0] == n - 2))
                g = GROUPS[n]
                sp.dma_start(win[n % 2], win_d[:, :, g * 512:(g + 1) * 512]).then_inc(s["win%d" % (n % 2)], 16)
                if n == 2:
                    sp.dma_start(w_glu, a["s5_w_glu"].rearrange("l (k p) n -> p (l k) n", p=P)).then_inc(s["glu_w"], 16)
                if n == 4:
                    sp.dma_start(w_b5, a["w_branch_s5"].rearrange("l (k p) n -> p (l k) n", p=P)).then_inc(s["branch5_w"], 16)
                if n == 5:
                    sp.dma_start(w_bh, a["w_branch_hgrn"].rearrange("l (k p) n -> p (l k) n", p=P)).then_inc(s["branchh_w"], 16)
            sp.wait_ge(s["proj"], len(PROJ))
            sp.dma_start(w_out, a["w_out"].rearrange("l (k p) n -> p (l k) n", p=P)).then_inc(s["out_w"], 16)
            sp.wait_ge(s["o_mm"], 1)
            for i in (4, 5, 7):
                up_piece(sp, 0, i)
            down_piece(sp, 0, 1, 1)
            down_piece(sp, 0, 3, 1)
            sp.wait_ge(s["og_used"], 1)
            down_piece(sp, 0, 2, 1)
            sp.wait_ge(landed[KD + 3], 16)
            down_piece(sp, 1, 3, 0)
            sp.wait_ge(s["br_mm"], 16)
            sp.dma_start(wrt, a["w_router"].rearrange("l (k p) n -> p (l k) n", p=P)).then_inc(s["router_w"], 16)
            sp.dma_start(brt, a["b_router"].to_broadcast([P, E])).then_inc(s["router_b"], 16)
            up_piece(sp, 0, 6)
            for j in (1, 2):
                sp.wait_ge(landed[KD + j], 16)
                down_piece(sp, 1, j, 0)
            sp.wait_ge(s["mrg_ready"], 4)
            sp.dma_start(bgu[0:E, :], a["b_gate_up"].rearrange("l e n -> (l e) n")).then_inc(s["expert_rows"], 16)
            sp.dma_start(bdn[0:E, :], a["b_down"].rearrange("l e n -> (l e) n")).then_inc(s["expert_rows"], 16)
            sp.dma_start(fgain, a["final_norm_gain"].rearrange("(o n) -> o n", o=1).to_broadcast([P, D])).then_inc(s["lastgain"], 16)
            sp.wait_ge(s["wo_mm"], 4)
            for i in range(4):
                up_piece(sp, 0, i)
            down_piece(sp, 0, 0, 1)
            sp.wait_ge(landed[KD], 16)
            down_piece(sp, 1, 0, 0)
            sp.wait_ge(s["idx_ready"], 1)
            n_early = sp.value_load(idx[0:1, ITEMS + 3:ITEMS + 4], min_val=E - LATE - 2, max_val=ITEMS - LATE - 2)

            def expert_of(w):
                return sp.value_load(idx[0:1, bass.ds(w, 1)], min_val=0, max_val=E - 1)

            def load_up(v, e, landings):
                for i in range(KD):
                    if i < KD - 1:
                        sp.wait_ge(s["piece_used"], v * PIECES + i + (2 if i == KD - 2 else 1))
                    else:
                        sp.wait_ge(landed[KD], landings * 16)
                    up_piece(sp, e, i)

            def load_down(v, e):
                for j in range(DOWN):
                    if j == 0:
                        sp.wait_ge(s["piece_used"], (v + 1) * PIECES)
                    else:
                        sp.wait_ge(landed[KD + j], (v + 2) * 16)
                    down_piece(sp, e, j, (v + 1) % 2)

            with sp.Fori(0, n_early) as v:
                load_up(v, expert_of(v + 1), v + 2)
                load_down(v, expert_of(v + 2))
            load_up(n_early, expert_of(n_early + 1), n_early + 2)
            with sp.Fori(0, LATE) as q:
                v = sp.snap(n_early + q)
                load_up(v + 1, expert_of(v + 2), v + 2)
                load_down(v, expert_of(v + 2))
            for t in range(TT):
                sp.wait_ge(s["w_last"], t + 1)
                sp.dma_start(out.rearrange("b (t p) d -> p (b t) d", p=P)[:, t, :], x2[:, t, :]).then_inc(s["out_stored"], 16)
            sp.wait_ge(s["out_stored"], 16 * TT)

        @block.gpsimd
        def _(pool):
            nc.gpsimd.memset(ones[:, :], 1.0).then_inc(s["ones_set"], 1)
            z = slice(META, TOK)
            for i in range(ST):
                pool.wait_ge(s["scanned"], i + 1)
                if i >= 1:
                    pool.wait_ge(s["xim5"], i)
                if i >= 2:
                    pool.wait_ge(s["ysum"], i - 1)
                nc.gpsimd.tensor_tensor(out=pool_rot[0][:, z], in0=zre[:, z], in1=sinT[i % 2][:, z], op=ALU.mult)
                nc.gpsimd.tensor_tensor(out=pool_rot[1][:, z], in0=zim[:, z], in1=cosT[i % 2][:, z], op=ALU.mult)\
                    .then_inc(s["pool_turned"], 1)
                pool.wait_ge(s["pool_turned"], i + 1)
                nc.gpsimd.tensor_tensor(out=xim[i % 2][:, z], in0=pool_rot[0][:, z], in1=pool_rot[1][:, z], op=ALU.add)\
                    .then_inc(s["xim5"], 1)
            pool.wait_ge(s["mrg_ready"], 4)
            for q in range(1, 4):
                nc.gpsimd.memset(ohb[32 * q:32 * q + 32, :], 0.0)
                nc.gpsimd.memset(bgu[32 * q:32 * q + 32, :], 0.0)
                last = nc.gpsimd.memset(bdn[32 * q:32 * q + 32, :], 0.0)
            last.then_inc(s["pad_zero"], 1)

        @block.scalar
        def _(act):
            n_ach = [0]

            def link(ins):
                n_ach[0] += 1
                ins.then_inc(s["ach"], 1)
                act.wait_ge(s["ach"], n_ach[0])

            def f(o, i, fn, **k):
                return nc.scalar.activation(o, i, fn, **k)

            act.dma_start(cst[:, :], a["shape_consts"]).then_inc(s["consts"], 16)
            act.dma_start(s5r[:, 0, :], a["s5_lambda_re"].rearrange("l (i g) p -> (l i) (g p)", g=2)).then_inc(s["s5rows"], 16)
            act.dma_start(s5r[:, 1, :], a["s5_lambda_im"].rearrange("l (i g) p -> (l i) (g p)", g=2)).then_inc(s["s5rows"], 16)
            act.dma_start(small[0:ST, 0:2], a["s5_log_dt"].rearrange("l (i g) -> (l i) g", g=2)).then_inc(s["s5rows"], 16)
            act.dma_start(bre, a["s5_b_re"].rearrange("l (i g) p h -> (g p) (l i) h", g=2)).then_inc(s["bload"], 16)
            act.dma_start(bim, a["s5_b_im"].rearrange("l (i g) p h -> (g p) (l i) h", g=2)).then_inc(s["bload"], 16)
            act.dma_start(cn[:, 0], a["s5_c_re"].rearrange("l (t g) h p -> (g h) (l t) p", t=4)).then_inc(s["cload"], 16)
            act.dma_start(cn[:, 1], a["s5_c_im"].rearrange("l (t g) h p -> (g h) (l t) p", t=4)).then_inc(s["cload"], 16)

            def root(n, v):
                act.wait_ge(s["var_in"], n)
                f(v, v, ACT.Sqrt).then_inc(s["root_out"], 1)

            for t in range(TT):
                root(1 + t, small[:, 4 + t:5 + t])
            root(3, small[0:META, 8:9])
            act.wait_ge(s["s5rows"], 48)
            f(small[0:ST, 2:4], small[0:ST, 0:2], ACT.Exp).then_inc(s["s5r_exp"], 1)
            act.wait_ge(s["s5r_v"], 1)
            f(s5r[:, 4, :], s5r[:, 2, :], ACT.Exp).then_inc(s["s5r_exp"], 1)
            act.wait_ge(s["s5r_ang"], 1)
            f(s5r[:, 6, :], s5r[:, 5, :], ACT.Sin, scale=TWO_PI).then_inc(s["s5r_sin"], 1)
            f(s5r[:, 7, :], s5r[:, 5, :], ACT.Sin, scale=TWO_PI / 2).then_inc(s["s5r_sin"], 1)

            def turns_of(i):
                if i >= 1:
                    act.wait_ge(s["rounded"], i)
                f(turns, steps, ACT.Identity, scale=s5c[:, 1, i:i + 1]).then_inc(s["ph"], 1)

            def sines_of(i):
                act.wait_ge(s["rounded"], i + 1)
                if i >= 2:
                    act.wait_ge(s["xs5"], i - 1)
                    act.wait_ge(s["xim5"], i - 1)
                f(sinT[i % 2], frac[i % 2], ACT.Sin, scale=-TWO_PI)
                if i >= 1:
                    act.wait_ge(s["sines"], i)
                link(f(absf, frac[i % 2], ACT.Abs))
                f(cosT[i % 2], absf, ACT.Sin, scale=-TWO_PI, bias=zero_c[:, 1:2]).then_inc(s["sines"], 1)

            n_proj = [0]

            def proj_copy(dst, rows=P):
                n = n_proj[0]
                n_proj[0] += 1
                act.wait_ge(s["proj"], n + 1)
                f(dst, ps[n % 2][0:rows, 0:dst.free_size()], ACT.Copy).then_inc(s["proj_free"], 1)

            for m in range(3):
                proj_copy(uT[:, m, :])
            act.wait_ge(s["s5cols_ready"], 1)
            act.wait_ge(s["consts"], 16)
            turns_of(0)
            turns_of(1)
            sines_of(0)
            proj_copy(uT[:, 3, :])
            dsts = [kT[:, m, :] for m in range(4)] + [qT[:, m, :] for m in range(4)]
            dsts += [v_a[:, 0, :], v_a[:, 1, :], v_parts] + [ogT[:, 0, :], (v_m[:, :], META)]
            dsts += [ogT[:, m, :] for m in range(1, 4)]
            dsts += [gates[:, m, :] for m in range(16)]

            def next_proj():
                d = dsts.pop(0)
                proj_copy(*d) if isinstance(d, tuple) else proj_copy(d)

            for i in range(ST):
                if i + 1 < ST:
                    sines_of(i + 1)
                if i + 2 < ST:
                    turns_of(i + 2)
                next_proj()
            act.wait_ge(s["gelu_in"], 1)
            f(yt, yt, ACT.Sigmoid, scale=GELU_C).then_inc(s["gelu_sig"], 1)
            act.wait_ge(s["acol"], 1)
            f(small[:, 20:24], small[:, 16:20], ACT.Sigmoid, scale=-1.0).then_inc(s["acol"], 1)
            f(fT, kT, ACT.Sigmoid).then_inc(s["f_sig"], 1)
            f(sg, qT, ACT.Sigmoid).then_inc(s["q_sig"], 1)
            next_proj()
            next_proj()
            act.wait_ge(s["kq_ready"], 1)
            act.wait_ge(s["glu_mm"], 1)
            for b in range(2):
                last = f(sg[:, 2 * b:2 * b + 2, :], ps[6 + b][:, :].rearrange("p (a n) -> p a n", a=2), ACT.Sigmoid)
            last.then_inc(s["glu_sig"], 1)
            act.wait_ge(s["g5_ready"], 1)
            f(yt, ogT[:, :, :], ACT.Sigmoid).then_inc(s["og_sig"], 1)
            act.wait_ge(s["f_ready"], 1)
            f(bT, fT, ACT.Ln).then_inc(s["logf"], 1)
            next_proj()
            next_proj()
            act.wait_ge(s["kh_in"], 1)
            f(kh, kh, ACT.Exp).then_inc(s["kh_exp"], 1)
            act.wait_ge(s["eb_in"], 1)
            f(eb, bc, ACT.Exp).then_inc(s["eb_out"], 1)
            for n in range(len(LEVELS)):
                act.wait_ge(s["decay_in"], n + 1)
                f(dec, dec, ACT.Exp).then_inc(s["decay_out"], 1)
                next_proj()
            while dsts:
                next_proj()
            act.wait_ge(s["proj_free"], len(PROJ))
            def gate_sigmoids(b):
                f(gates[:, 4 * b:4 * b + 4, :], gates[:, 4 * b:4 * b + 4, :], ACT.Sigmoid).then_inc(s["gate_sig"], 1)

            gate_sigmoids(0)
            gate_sigmoids(1)
            act.wait_ge(s["o_mm"], 1)
            for b in range(2):
                f(o2[:, 512 * b:512 * b + 512], ps[4 + b][:, :], ACT.Square).then_inc(s["o2_ready"], 1)
            act.wait_ge(s["ms_mm"], 1)
            f(rms[:, 0:8], ps[7][:, 0:8], ACT.Sqrt, scale=1.0 / P, bias=zero_c[:, 2:3]).then_inc(s["rms_out"], 1)
            gate_sigmoids(2)
            gate_sigmoids(3)
            for t in range(TT):
                for b in range(2):
                    act.wait_ge(s["sum_turned"], 2 * t + b + 1)
                    f(sumT[:, 4 * b:4 * b + 4, t * P:(t + 1) * P], ps[4 + 2 * t + b][:, :].rearrange("p (a n) -> p a n", a=4),
                      ACT.Copy).then_inc(s["sumT_ready"], 1)
                root(4 + t, small[:, 32 + t:33 + t])
                act.wait_ge(s["inv_ready"], t + 1)
                f(x2[:, t, :], x[:, t, :], ACT.Identity, scale=small[:, 34 + t:35 + t]).then_inc(s["x2_ready"], 1)
            act.wait_ge(s["logits_in"], TT)
            for t in range(TT):
                f(ex[t], lg[t], ACT.Exp, bias=nmx[t]).then_inc(s["exped"], 1)
            act.wait_ge(s["count_ready"], 1)
            n_items = act.value_load(idx[0:1, ITEMS:ITEMS + 1], min_val=E, max_val=ITEMS)

            def combine_parts(w):
                act.wait_ge(s["ct_mm"], w + 1)
                f(ctr, ps[5][:, 0:SEQ], ACT.Copy).then_inc(s["ct_ready"], 1)

            with act.Fori(0, n_items) as w:
                combine_parts(w)
                act.wait_ge(s["gate_in"], w + 1)
                f(sgm, gt, ACT.Sigmoid, scale=1.702).then_inc(s["gate_sg"], 1)
                act.wait_ge(s["piece_used"], (w + 1) * PIECES)
                f(ysl, ps[2][:, :], ACT.Copy).then_inc(s["ysl_ready"], 1)
            combine_parts(n_items)
            root(6, small[:, 40:41])
            root(7, small[:, 41:42])

        @block.tensor
        def _(pe):
            def mm(o, l, r, start, stop):
                return nc.tensor.matmul(o, l, r, start=start, stop=stop, skip_group_check=True)

            def tr(o, i, n=P):
                return nc.tensor.transpose(o, i, ident[0:n, 0:n])

            def keep_warm(n, bank=5):
                for _ in range(n):
                    mm(ps[bank][:, 0:P], ones[:, :], ones[:, :], True, True)

            pe.wait_ge(s["ones_set"], 1)
            keep_warm(30, 7)
            pe.wait_ge(s["consts"], 16)
            pe.wait_ge(s["rows"], 80)
            tr(ps[6][:, 0:32], prow[:, :], 32).then_inc(s["rows_turned"], 1)
            for t in range(TT):
                pe.wait_ge(s["xs_ready"], t + 1)
                for k in range(KD):
                    last = tr(ps[2 * t + k // 4][:, (k % 4) * P:(k % 4 + 1) * P], (xs, xs2)[t][:, k * P:(k + 1) * P])
                last.then_inc(s["turned_x"], 1)
            pe.wait_ge(s["xs_ready"], 3)
            for k in range(KD):
                last = tr(ps[5][:, k * META:(k + 1) * META], xmn[:, k * P:(k + 1) * P], META)
            last.then_inc(s["turned_m"], 1)
            n_proj = [0]

            def proj_tile(n, m):
                q = n_proj[0]
                n_proj[0] += 1
                if (n, m) == SUM_PARTS:
                    pe.wait_ge(s["proj_free"], PROJ.index((V_GROUP, 2)) + 1)
                    mm(ps[q % 2][0:META, :], cst[:, C_SEL:C_SEL + META], v_parts, True, True).then_inc(s["proj"], 1)
                    return
                g = GROUPS[n]
                if m == 0:
                    pe.wait_ge(s["win%d" % (n % 2)], 16 * (n // 2 + 1))
                if q >= 2:
                    pe.wait_ge(s["proj_free"], q - 1)
                for k in range(KD):
                    if g == V_GROUP and m == 2:
                        last = mm(ps[q % 2][32 * (k % 4):32 * (k % 4 + 1), :], xnT[:, k, 0:32], win[n % 2][:, k, :],
                                  k < 4, k >= 4)
                    elif g == V_GROUP:
                        lo, hi = ((META, META + P), (META + P, TOK))[m]
                        last = mm(ps[q % 2][0:hi - lo, :], xnT[:, k, lo:hi], win[n % 2][:, k, :], k == 0, k == KD - 1)
                    else:
                        lo = 0 if g in (0, 2) else META
                        last = mm(ps[q % 2][:, 0:TOK - lo], win[n % 2][:, k, m * P:(m + 1) * P], xnT[:, k, lo:TOK],
                                  k == 0, k == KD - 1)
                last.then_inc(s["proj"], 1)

            def bu(i):
                if i >= 2:
                    pe.wait_ge(s["bu_free"], i - 1)
                r = 32 * (i % 4)
                for c in range(2):
                    last = mm(ps[2 + 2 * (i % 2) + c][:, 0:TOK], blk[r:r + 32, c, i // 4, :], uT[r:r + 32, i // 4, :], True, True)
                last.then_inc(s["bu"], 1)

            def y_of(i):
                pe.wait_ge(s["xs5"], i + 1)
                pe.wait_ge(s["xim5"], i + 1)
                r, t = 32 * (i % 4), i // 4
                o = ps[6 + t // 2][r:r + 32, (t % 2) * SEQ:(t % 2 + 1) * SEQ]
                mm(o, blk[:, 2, t, r:r + 32], xre[i % 2][:, META:TOK], True, False)
                mm(o, blk[:, 3, t, r:r + 32], xim[i % 2][:, META:TOK], False, True).then_inc(s["ysum"], 1)

            keep_warm(5, 7)
            pe.wait_ge(s["xnT_ready"], 1)
            for m in range(3):
                proj_tile(0, m)
            pe.wait_ge(s["s5r_v"], 2)
            for j, row in enumerate((4, 5, 2, 3)):
                last = tr(ps[7][:, j * ST:(j + 1) * ST], s5r[:, row, :], ST)
            last.then_inc(s["s5rows_turned"], 1)
            proj_tile(0, 3)
            pe.wait_ge(s["bz_ready"], 1)
            for c in range(2):
                for t in range(4):
                    last = tr(ps[2 + c][:, t * P:(t + 1) * P], bz[:, c, t, :])
            last.then_inc(s["b_turned"], 1)
            for c in range(2):
                for t in range(4):
                    last = tr(ps[4 + c][:, t * P:(t + 1) * P], cz[:, c, t, :])
            last.then_inc(s["c_turned"], 1)
            tiles = PROJ[4:]
            pe.wait_ge(s["b_laid"], 1)
            pe.wait_ge(s["proj_free"], 4)
            bu(0)
            pe.wait_ge(s["c_laid"], 1)
            bu(1)
            for i in range(ST):
                proj_tile(*tiles.pop(0))
                if i + 2 < ST:
                    bu(i + 2)
                y_of(i)
            for _ in range(2):
                proj_tile(*tiles.pop(0))
            pe.wait_ge(s["glu_w"], 16)
            pe.wait_ge(s["g5_ready"], 1)
            for m in range(KW):
                for k in range(KW):
                    last = mm(ps[6 + m // 2][:, (m % 2) * SEQ:(m % 2 + 1) * SEQ], w_glu[:, k, m * P:(m + 1) * P], g5[:, k, :],
                              k == 0 and m % 2 == 0, k == KW - 1)
            last.then_inc(s["glu_mm"], 1)
            for _ in range(3):
                proj_tile(*tiles.pop(0))
            pe.wait_ge(s["kh_ready"], 1)
            pe.wait_ge(s["glu_sig"], 1)
            for h in range(HEADS):
                tr(ps[6][0:META, h * P:(h + 1) * P], kh[:, h, 0:META])
                last = tr(ps[7][:, h * P:(h + 1) * P], kh[:, h, META:META + P])
            last.then_inc(s["kh_turned"], 1)
            pe.wait_ge(s["kq_ready"], 2)
            for j in range(8):
                last = mm(ps[4 + j // 4][:, (j % 4) * P:(j % 4 + 1) * P], kc[:, j * P:(j + 1) * P],
                          qT.rearrange("p a b -> p (a b)")[:, j * P:(j + 1) * P], j % 4 == 0, j % 4 == 3)
            last.then_inc(s["diag_mm"], 1)
            for n, m in enumerate(LEVELS):
                pe.wait_ge(s["level_in"], n + 1)
                if n >= 2:
                    pe.wait_ge(s["level_used"], n - 1)
                for j in range(8):
                    col = qk[:, j * P:(j + 1) * P]
                    right = col.rearrange("p (b m) -> p b m", m=2 * m)[:, :, m:2 * m]
                    last = mm(ps[2 + n % 2][:, j * 64:(j + 1) * 64], col, right, j == 0, j == 7)
                last.then_inc(s["level_mm"], 1)
                proj_tile(*tiles.pop(0))
                if n == 2:
                    pe.wait_ge(s["khT_ready"], 1)
                    for h in range(HEADS):
                        hs = slice(h * P, (h + 1) * P)
                        mm(ps[6][:, hs], khTm[:, hs], v_m[:, hs], h == 0, h == 3)
                        last = mm(ps[7][:, hs], khT[:, h, :], v_a[:, 0, hs], h == 0, h == 3)
                    last.then_inc(s["st_mm"], 1)
            while tiles:
                proj_tile(*tiles.pop(0))
            pe.wait_ge(s["qe_ready"], 1)
            pe.wait_ge(s["st1_ready"], 1)
            pe.wait_ge(s["stot_ready"], 1)
            for h in range(HEADS):
                for c in range(TT):
                    j = 2 * h + c
                    o = ps[4 + j // 4][:, (j % 4) * P:(j % 4 + 1) * P]
                    mm(o, (st0, st1)[c][:, h, :], qe[:, j * P:(j + 1) * P], j % 4 == 0, False)
                    last = mm(o, v_a[:, c, h * P:(h + 1) * P], stot[:, j, :], False, j % 4 == 3)
            last.then_inc(s["o_mm"], 1)
            def branch(br, b):
                w, y = ((w_b5, y5), (w_bh, yh))[br]
                for j in range(2):
                    m = 2 * b + j
                    for k in range(KW):
                        last = mm(ps[4 * br + b][:, j * SEQ:(j + 1) * SEQ], w[:, k, m * P:(m + 1) * P], y[:, k, :],
                                  k == 0 and j == 0, k == KW - 1)
                    last.then_inc(s["br_mm"], 1)

            pe.wait_ge(s["branch5_w"], 16)
            pe.wait_ge(s["y5_ready"], 1)
            pe.wait_ge(s["proj_free"], len(PROJ))
            pe.wait_ge(s["level_used"], 7)
            branch(0, 0)
            pe.wait_ge(s["o2_ready"], 2)
            for j in range(8):
                last = mm(ps[7][:, j:j + 1], o2[:, j * P:(j + 1) * P], ones[:, 0:1], j == 0, j == 7)
            last.then_inc(s["ms_mm"], 1)
            branch(0, 1)
            pe.wait_ge(s["diag_ready"], 1)
            for b in range(2):
                last = mm(ps[6 + b][:, :], ones[:, :], dgs[:, 512 * b:512 * b + 512], True, True)
            last.then_inc(s["inv_mm"], 1)
            branch(0, 2)
            branch(0, 3)
            pe.wait_ge(s["branchh_w"], 16)
            pe.wait_ge(s["yh_ready"], 2)
            for b in range(4):
                branch(1, b)
            def times_w_out(t, b):
                for k in range(KD):
                    if t == 0 and b == 0 and k % 2 == 0:
                        pe.wait_ge(s["mrg_ready"], k // 2 + 1)
                    last = mm(ps[2 * t + b][:, :], mrg[:, k, t * P:(t + 1) * P], w_out[:, k, 512 * b:512 * b + 512],
                              k == 0, k == KD - 1)
                last.then_inc(s["wo_mm"], 1)

            def turn_sum(t, b):
                pe.wait_ge(s["mixed"], 2 * t + b + 1)
                for k in range(4):
                    last = tr(ps[4 + 2 * t + b][:, k * P:(k + 1) * P], x[:, t, (4 * b + k) * P:(4 * b + k + 1) * P])
                last.then_inc(s["sum_turned"], 1)

            def logit_parts(t):
                pe.wait_ge(s["sumT_ready"], 2 * t + 2)
                o = [ps[t][E * q:E * (q + 1), 0:P] for q in range(4)]
                for k in range(KD):
                    last = mm(o[k % 4], wrt[:, k, :], sumT[:, k, t * P:(t + 1) * P], k < 4, k >= 4)
                last.then_inc(s["parts_mm"], 1)

            def turn_logits(t):
                pe.wait_ge(s["parts_ready"], t + 1)
                tr(ps[4 + 2 * t][:, 0:P], lgq[:, t, :]).then_inc(s["logit_mm"], 1)

            pe.wait_ge(s["out_w"], 16)
            times_w_out(0, 0)
            times_w_out(0, 1)
            turn_sum(0, 0)
            times_w_out(1, 0)
            turn_sum(0, 1)
            times_w_out(1, 1)
            turn_sum(1, 0)
            pe.wait_ge(s["wrt_ready"], 1)
            logit_parts(0)
            turn_sum(1, 1)
            turn_logits(0)
            logit_parts(1)
            turn_logits(1)
            keep_warm(12)
            pe.wait_ge(s["mask_ready"], 1)
            mm(ps[0][:, 0:E], tri, mask[0], True, True)
            mm(ps[1][:, 0:E], tri, mask[1], True, False)
            mm(ps[1][:, 0:E], ones[:, :], mask[0], False, True)
            for t in range(TT):
                last = mm(ps[2][0:E, 0:1], mask[t], ones[:, 0:1], t == 0, t == TT - 1)
            last.then_inc(s["rank_mm"], 1)
            keep_warm(3)
            pe.wait_ge(s["slot_ready"], 1)
            for t in range(TT):
                tr(ps[7][0:E, t * P:(t + 1) * P], slot[t])
                last = tr(ps[7][0:E, (2 + t) * P:(3 + t) * P], wt[t])
            last.then_inc(s["tr_mm"], 1)
            pe.wait_ge(s["cnt_ready"], 1)
            mm(ps[2][0:E, 1:2], tri[0:E, 0:E], cx, True, True)
            mm(ps[2][0:1, 2:3], ones[0:E, 0:1], cx, True, True).then_inc(s["start_mm"], 1)

            def gather(w):
                pe.wait_ge(s["pick_ready"], w + 1)
                for k in range(KD):
                    for t in range(TT):
                        last = mm(ps[3][:, k * SLOTS:(k + 1) * SLOTS], x2[:, t, k * P:(k + 1) * P], pick[:, t, :],
                                  k == 0 and t == 0, t == TT - 1)
                last.then_inc(s["gathered"], 1)

            def turn_last(w1):
                pe.wait_ge(s["w_pickw"], w1)
                pe.wait_ge(s["added1"], w1)
                for t in range(TT):
                    last = tr(ps[5][:, t * P:(t + 1) * P], pickw[:, t, :, :].rearrange("p a b -> p (a b)"))
                last.then_inc(s["ct_mm"], 1)

            def add_last(w):
                pe.wait_ge(s["ct_ready"], w + 1)
                pe.wait_ge(s["ysl_ready"], w + 1)
                pe.wait_ge(s["added0"], w + 1)
                for t, sm in ((0, "comb0"), (1, "comb1")):
                    for b in range(2):
                        hs = slice(SLOTS * b, SLOTS * (b + 1))
                        last = mm(ps[(6, 4)[t] + b][:, :], ctr[hs, t * P:(t + 1) * P], ysl[hs, :], True, True)
                    last.then_inc(s[sm], 1)

            pe.wait_ge(s["x2_ready"], TT)
            gather(0)
            pe.wait_ge(s["oh_ready"], 1)
            further = oh[:, E:ITEMS]
            for t in range(TT):
                o = ps[6][:, P * t:P * (t + 1)]
                mm(o[:, 0:EXTRA], slT[:, t * P:(t + 1) * P], further, True, False)
                mm(o[:, 0:EXTRA], neg, ohc, False, True)
                mm(o[:, 64:64 + EXTRA], wtT[:, t * P:(t + 1) * P], further, True, True)
            mm(ps[7][0:1, 0:EXTRA], cst[0:E, C_PI:C_PI + 1], further, True, True).then_inc(s["item_mm"], 1)
            pe.wait_ge(s["expert_rows"], 32)
            turn_last(1)
            pe.wait_ge(s["count_ready"], 1)
            n_items = pe.value_load(idx[0:1, ITEMS:ITEMS + 1], min_val=E, max_val=ITEMS)
            n_pairs = pe.value_load(idx[0:1, ITEMS + 2:ITEMS + 3], min_val=E // 2, max_val=ITEMS // 2)
            def item(w, odd):
                pe.wait_ge(s["h_done"], w + 1)
                pe.wait_ge(s["ohb_ready"], w + 1)
                for k in range(-1, KD):
                    if k == 0:
                        pe.wait_ge(s["xg_ready"], w + 1)
                    if k >= 0:
                        pe.wait_ge(landed[k], 16 * (w + 1))
                    lhs, wk = (ohb, bgu) if k < 0 else (xgT[:, k, :], ring[:, k, :])
                    wv = wk.rearrange("p (h f g) -> p g h f", h=2, g=2)
                    for g in range(2):
                        for h in range(2):
                            last = mm(ps[g][SLOTS * h:SLOTS * (h + 1), :], lhs, wv[:, g, h, :], k < 0, k == KD - 1)
                    if k >= 0:
                        last.then_inc(s["piece_used"], 1)
                add_last(w)
                pe.wait_ge(s["h_done"], w + 2)
                for c in range(4):
                    last = tr(ps[3][:, c * P:(c + 1) * P], up[:, c * P:(c + 1) * P])
                last.then_inc(s["h_turned"], 1)
                for h in range(2):
                    last = mm(ps[2][SLOTS * h:SLOTS * (h + 1), :], ohb, bdn[:, 512 * h:512 * h + 512], True, False)
                last.then_inc(s["ohb_used"], 1)
                pe.wait_ge(s["hT_ready"], w + 1)
                for k in range(KD):
                    if k % 2 == 0:
                        pe.wait_ge(landed[KD + k // 2], 16 * (w + 1))
                    wv = ring[:, KD + (1 - odd) * DOWN + k // 2, (k % 2) * D:(k % 2 + 1) * D]
                    for h in range(2):
                        last = mm(ps[2][SLOTS * h:SLOTS * (h + 1), :], hT[:, k % 4, k // 4, :],
                                  wv[:, 512 * h:512 * h + 512],
                                  False, k == KD - 1)
                    if k % 2 == 1:
                        last.then_inc(s["piece_used"], 1)
                turn_last(pe.snap(w + 2))
                gather(w + 1)
            with pe.Fori(0, n_pairs) as pair:
                for odd in range(2):
                    item(pe.snap(pair * 2 + odd), odd)
            add_last(n_items)

        @block.vector
        def _(dve):
            n_dch = [0]
            V = nc.vector

            def link(ins):
                n_dch[0] += 1
                ins.then_inc(s["dch"], 1)
                dve.wait_ge(s["dch"], n_dch[0])

            def tt(o, i0, i1, op):
                return V.tensor_tensor(out=o, in0=i0, in1=i1, op=op)

            def ts(o, i, s1, s2, op0, op1=None):
                return V.tensor_scalar(o, i, s1, s2, op0, op1) if op1 is not None else V.tensor_scalar(o, i, s1, None, op0)

            def stt(o, i0, sc, i1, op0, op1):
                return V.scalar_tensor_tensor(out=o, in0=i0, scalar=sc, in1=i1, op0=op0, op1=op1)

            def wide(col, n):
                return col.unsqueeze(2).to_broadcast([col.shape[0], col.shape[1], n])

            MU, AD, SU = ALU.mult, ALU.add, ALU.subtract
            V.memset(zero_c[:, 0:1], 0.0)
            V.memset(zero_c[:, 2:3], EPS)
            link(V.memset(zero_c[:, 1:2], float(np.float32(np.pi / 2))))
            for t in range(TT):
                dve.wait_ge(s["xload%d" % t], 16)
                link(V.tensor_tensor_reduce((xs, xs2)[t], x[:, t, :], x[:, t, :], 1.0, 0.0, MU, AD, small[:, 4 + t:5 + t]))
                ts(small[:, 4 + t:5 + t], small[:, 4 + t:5 + t], 1.0 / D, EPS, MU, AD).then_inc(s["var_in"], 1)
            for t in range(TT):
                dve.wait_ge(s["root_out"], t + 1)
                link(V.reciprocal(small[:, 6 + t:7 + t], small[:, 4 + t:5 + t]))
                ts((xs, xs2)[t], x[:, t, :], small[:, 6 + t:7 + t], None, MU).then_inc(s["xs_ready"], 1)
            dve.wait_ge(s["meta"], 16)
            link(V.tensor_tensor_reduce(xmn, xm[:, :], xm[:, :], 1.0, 0.0, MU, AD, small[0:META, 8:9]))
            ts(small[0:META, 8:9], small[0:META, 8:9], 1.0 / D, EPS, MU, AD).then_inc(s["var_in"], 1)
            dve.wait_ge(s["root_out"], 3)
            link(V.reciprocal(small[0:META, 9:10], small[0:META, 8:9]))
            ts(xmn, xm[:, :], small[0:META, 9:10], None, MU).then_inc(s["xs_ready"], 1)
            dve.wait_ge(s["rows_turned"], 1)
            link(V.tensor_copy(pcol[:, :], ps[6][:, 0:32]))
            gain1, gain2 = pcol[:, 0:8], pcol[:, 8:16]
            for t in range(TT):
                dve.wait_ge(s["turned_x"], t + 1)
                for b in range(2):
                    tt(xnT[:, 4 * b:4 * b + 4, META + t * P:META + (t + 1) * P],
                       ps[2 * t + b][:, :].rearrange("p (a n) -> p a n", a=4), wide(gain1[:, 4 * b:4 * b + 4], P), MU)
            dve.wait_ge(s["turned_m"], 1)
            tt(xnT[:, :, 0:META], ps[5][:, 0:KD * META].rearrange("p (a n) -> p a n", a=KD), wide(gain1, META), MU)\
                .then_inc(s["xnT_ready"], 1)
            R = lambda j: s5r[:, j, :]
            R2 = lambda j: s5r[:, j, :].rearrange("p (g n) -> p g n", g=2)
            dt2 = wide(small[0:ST, 2:4], 64)
            dve.wait_ge(s["s5r_exp"], 1)
            tt(R2(2), R2(0), dt2, MU).then_inc(s["s5r_v"], 1)
            link(tt(R2(3), R2(1), dt2, MU))
            link(ts(R(6), R(3), float(1 / (2 * np.pi)), MAGIC, MU, AD))
            link(ts(R(6), R(6), MAGIC, None, SU))
            c1 = 6.28125
            c2 = float(np.float32(2 * np.pi - c1) // 2 ** -19 * 2 ** -19)
            c3 = float(2 * np.pi - c1 - c2)
            for c in (c1, c2, c3):
                link(stt(R(3), R(6), -c, R(3), MU, AD))
            link(ts(R(5), R(3), float(1 / (2 * np.pi)), 0.5, MU, ALU.min))
            ts(R(5), R(5), -0.5, None, ALU.max).then_inc(s["s5r_ang"], 1)
            dve.wait_ge(s["s5r_exp"], 2)
            dve.wait_ge(s["s5r_sin"], 2)
            link(tt(R(7), R(7), R(7), MU))
            link(tt(R(7), R(7), R(4), MU))
            link(stt(R(7), R(7), -2.0, R(4), MU, AD))
            link(ts(R(7), R(7), -1.0, None, AD))
            link(tt(R(6), R(6), R(4), MU))
            q1, q2, q3 = s5q[:, 0, :], s5q[:, 1, :], s5q[:, 2, :]
            tt(q1, R(0), R(0), MU)
            link(tt(q2, R(1), R(1), MU))
            link(tt(q1, q1, q2, AD))
            link(V.reciprocal(q1, q1))
            tt(q2, R(7), R(0), MU)
            link(tt(q3, R(6), R(1), MU))
            link(tt(q2, q2, q3, AD))
            link(tt(R(2), q2, q1, MU))
            tt(q2, R(6), R(0), MU)
            link(tt(q3, R(7), R(1), MU))
            link(tt(q2, q2, q3, SU))
            tt(R(3), q2, q1, MU).then_inc(s["s5r_v"], 1)

            dve.wait_ge(s["s5rows_turned"], 1)
            V.tensor_copy(s5c[:, :, :], ps[7][:, 0:4 * ST].rearrange("p (a n) -> p a n", a=4)).then_inc(s["s5cols_ready"], 1)
            dve.wait_ge(s["s5cols_ready"], 1)
            dve.wait_ge(s["bload"], 32)
            dve.wait_ge(s["consts"], 16)
            cr, ci = wide(s5c[:, 2, :], 16), wide(s5c[:, 3, :], 16)
            tt(bb[0], bre, cr, MU)
            tt(bb[1], bim, ci, MU)
            tt(bb[2], bre, ci, MU)
            link(tt(bb[3], bim, cr, MU))
            tt(bb[0], bb[0], bb[1], SU)
            link(tt(bb[2], bb[2], bb[3], AD))
            for c in range(2):
                for g in range(2):
                    o = bz[:, c, :, :].rearrange("p t (i g h) -> p (t i) g h", i=4, g=2)[:, :, g, :]
                    last = ts(o, bb[2 * c], cst[:, C_GB + g:C_GB + g + 1], None, MU)
            dve.wait_ge(s["cload"], 32)
            for c in range(2):
                for g in range(2):
                    last = ts(cz[:, c, :, g * 64:(g + 1) * 64], cn[:, c], cst[:, C_GC + g:C_GC + g + 1], (1.0, -1.0)[c], MU, MU)
            last.then_inc(s["bz_ready"], 1)

            def fraction(i):
                dve.wait_ge(s["ph"], i + 1)
                if i >= 2:
                    dve.wait_ge(s["sines"], i - 1)
                link(ts(rnd, turns, MAGIC, None, AD))
                stt(frac[i % 2], rnd, MAGIC, turns, SU, SU).then_inc(s["rounded"], 1)

            fraction(0)
            dve.wait_ge(s["b_turned"], 1)
            for c in range(2):
                last = V.tensor_copy(blk[:, c, :, :], ps[2 + c][:, :].rearrange("p (a n) -> p a n", a=4))
            last.then_inc(s["b_laid"], 1)
            dve.wait_ge(s["c_turned"], 1)
            for c in range(2):
                last = V.tensor_copy(blk[:, 2 + c, :, :], ps[4 + c][:, :].rearrange("p (a n) -> p a n", a=4))
            last.then_inc(s["c_laid"], 1)
            fraction(1)
            for i in range(ST):
                re, im = ps[2 + 2 * (i % 2)][:, 0:TOK], ps[3 + 2 * (i % 2)][:, 0:TOK]
                sn, co = sinT[i % 2], cosT[i % 2]
                if i >= 1:
                    dve.wait_ge(s["xs5"], i)
                dve.wait_ge(s["bu"], i + 1)
                dve.wait_ge(s["sines"], i + 1)
                tt(rot[0], re, co, MU)
                tt(rot[1], im, sn, MU)
                tt(rot[2], im, co, MU)
                link(tt(rot[3], re, sn, MU))
                tt(rot[0], rot[0], rot[1], AD).then_inc(s["bu_free"], 1)
                link(tt(rot[2], rot[2], rot[3], SU))
                r = s5c[:, 0, i:i + 1].to_broadcast([P, TOK])
                if i >= 1:
                    dve.wait_ge(s["xim5"], i)
                V.tensor_tensor_scan(zre, r, rot[0], 0.0, MU, AD)
                V.tensor_tensor_scan(zim, r, rot[2], 0.0, MU, AD).then_inc(s["scanned"], 1)
                dve.wait_ge(s["scanned"], i + 1)
                z = slice(META, TOK)
                if i >= 2:
                    dve.wait_ge(s["ysum"], i - 1)
                tt(rot[0][:, z], zre[:, z], co[:, z], MU)
                link(tt(rot[1][:, z], zim[:, z], sn[:, z], MU))
                tt(xre[i % 2][:, z], rot[0][:, z], rot[1][:, z], SU).then_inc(s["xs5"], 1)
                if i + 2 < ST:
                    fraction(i + 2)
            dve.wait_ge(s["ysum"], ST)
            for t in range(KW):
                last = stt(y5[:, t, :], uT[:, t, META:TOK], pcol[:, 28 + t:29 + t],
                           ps[6 + t // 2][:, (t % 2) * SEQ:(t % 2 + 1) * SEQ], MU, AD)
            link(last)
            link(tt(yt, y5, y5, MU))
            link(ts(yt, yt, 0.044715, 1.0, MU, AD))
            tt(yt, yt, y5, MU).then_inc(s["gelu_in"], 1)
            tt(small[:, 16:20], pcol[:, 20:24], pcol[:, 16:20], SU).then_inc(s["acol"], 1)
            dve.wait_ge(s["gelu_sig"], 1)
            tt(g5, y5, yt, MU).then_inc(s["g5_ready"], 1)
            dve.wait_ge(s["q_sig"], 1)
            tt(qT, qT, sg, MU).then_inc(s["kq_ready"], 1)
            dve.wait_ge(s["acol"], 2)
            link(ts(small[:, 24:28], small[:, 20:24], -1.0, 1.0, MU, AD))
            dve.wait_ge(s["f_sig"], 1)
            for h in range(HEADS):
                last = ts(fT[:, h, :], fT[:, h, :], small[:, 24 + h:25 + h], small[:, 20 + h:21 + h], MU, AD)
            last.then_inc(s["f_ready"], 1)
            dve.wait_ge(s["f_ready"], 1)
            link(ts(kT, fT, -1.0, 1.0, MU, AD))
            dve.wait_ge(s["glu_sig"], 1)
            tt(y5, g5, sg, MU).then_inc(s["y5_ready"], 1)
            V.tensor_copy(kc.rearrange("p (a n) -> p a n", a=KW), kT[:, :, META:TOK]).then_inc(s["kq_ready"], 1)
            dve.wait_ge(s["og_sig"], 1)
            for h in range(HEADS):
                link(stt(ogT[:, h, :], ogT[:, h, :], pcol[:, 24 + h:25 + h], yt[:, h, :], MU, MU))
            dve.wait_ge(s["logf"], 1)
            chunk = ((0, META), (META, META + P), (META + P, TOK))
            one = ones[:, 0:1]
            dve.wait_ge(s["ones_set"], 1)
            for h in range(HEADS):
                for lo, hi in chunk:
                    last = V.tensor_tensor_scan(bT[:, h, lo:hi], one.to_broadcast([P, hi - lo]), bT[:, h, lo:hi], 0.0, MU, AD)
            link(last)
            for lo, hi in chunk[:2]:
                last = tt(kh[:, :, lo:hi], bT[:, :, hi - 1:hi].to_broadcast([P, HEADS, hi - lo]), bT[:, :, lo:hi], SU)
            last.then_inc(s["kh_in"], 1)
            V.tensor_copy(bc.rearrange("p (a n) -> p a n", a=KW), bT[:, :, META:TOK]).then_inc(s["eb_in"], 1)

            def level_decay(n):
                m = LEVELS[n]
                if n >= 1:
                    dve.wait_ge(s["level_in"], n)
                b = bc.rearrange("p (c m) -> p c m", m=2 * m)
                d = dec.rearrange("p (c m) -> p c m", m=2 * m)
                mid = b[:, :, m - 1:m].to_broadcast([P, 1024 // (2 * m), m])
                tt(d[:, :, 0:m], mid, b[:, :, 0:m], SU)
                tt(d[:, :, m:2 * m], b[:, :, m:2 * m], mid, SU).then_inc(s["decay_in"], 1)

            dve.wait_ge(s["eb_in"], 1)
            level_decay(0)
            dve.wait_ge(s["kh_exp"], 1)
            tt(kh, kh, kT[:, :, 0:META + P], MU).then_inc(s["kh_ready"], 1)
            dve.wait_ge(s["eb_out"], 1)
            tt(qe, eb, qT.rearrange("p a b -> p (a b)"), MU).then_inc(s["qe_ready"], 1)
            dve.wait_ge(s["diag_mm"], 1)
            for b in range(2):
                last = tt(stot[:, 4 * b:4 * b + 4, :], ps[4 + b][:, :].rearrange("p (a n) -> p a n", a=4),
                          ident.unsqueeze(1).to_broadcast([P, 4, P]), MU)
            link(last)
            qf = qT.rearrange("p a b -> p (a b)")
            stf = stot.rearrange("p a b -> p (a b)")

            def level_sum(n):
                m = LEVELS[n]
                dve.wait_ge(s["level_mm"], n + 1)
                mk = cst[:, C_MASK + 64 * n:C_MASK + 64 * (n + 1)].unsqueeze(1).to_broadcast([P, 8, 64])
                ins = tt(tmpl, ps[2 + n % 2][:, :].rearrange("p (a n) -> p a n", a=8), mk, MU)
                ins.then_inc(s["level_used"], 1)
                dve.wait_ge(s["level_used"], n + 1)
                so = stf.rearrange("p (c m) -> p c m", m=2 * m)[:, :, m:2 * m]
                ins = tt(so, so, tmpl.rearrange("p a b -> p (a b)").rearrange("p (c m) -> p c m", m=m), AD)
                if n == len(LEVELS) - 1:
                    ins.then_inc(s["stot_ready"], 1)
                else:
                    link(ins)

            for n, m in enumerate(LEVELS):
                dve.wait_ge(s["decay_out"], n + 1)
                if n >= 1:
                    dve.wait_ge(s["level_mm"], n)
                g3 = lambda t: t.rearrange("p (c m) -> p c m", m=2 * m)
                tt(g3(qk)[:, :, 0:m], g3(dec)[:, :, 0:m], g3(kc)[:, :, 0:m], MU)
                tt(g3(qk)[:, :, m:2 * m], g3(dec)[:, :, m:2 * m], g3(qf)[:, :, m:2 * m], MU).then_inc(s["level_in"], 1)
                if n + 1 < len(LEVELS):
                    level_decay(n + 1)
                if n == 1:
                    dve.wait_ge(s["kh_turned"], 1)
                    V.tensor_copy(khTm, ps[6][0:META, :])
                    V.tensor_copy(khT, ps[7][:, :].rearrange("p (a n) -> p a n", a=4)).then_inc(s["khT_ready"], 1)
                if n >= 1:
                    level_sum(n - 1)
            level_sum(len(LEVELS) - 1)
            dve.wait_ge(s["st_mm"], 1)
            link(V.tensor_copy(st0, ps[6][:, :].rearrange("p (a n) -> p a n", a=4)))
            for h in range(HEADS):
                last = stt(st1[:, h, :], st0[:, h, :], eb[:, h * SEQ + P - 1:h * SEQ + P], ps[7][:, h * P:(h + 1) * P], MU, AD)
            last.then_inc(s["st1_ready"], 1)
            for b in range(2):
                dve.wait_ge(s["o2_ready"], b + 1)
                last = tt(orn[:, 512 * b:512 * b + 512], ps[4 + b][:, :],
                          ogT[:, 2 * b:2 * b + 2, :].rearrange("p a b -> p (a b)"), MU)
            last.then_inc(s["og_used"], 1)
            def merge(br, b):
                dve.wait_ge(s["gate_sig"], 2 * br + 2)
                dve.wait_ge(s["br_mm"], 8 * br + 2 * b + 2)
                return tt((mrg[:, 2 * b:2 * b + 2, :], gates[:, KD + 2 * b:KD + 2 * b + 2, :])[br],
                          ps[4 * br + b][:, :].rearrange("p (a n) -> p a n", a=2),
                          gates[:, br * KD + 2 * b:br * KD + 2 * b + 2, :], MU)

            link(merge(0, 0))
            dve.wait_ge(s["rms_out"], 1)
            link(V.reciprocal(rms[:, 8:16], rms[:, 0:8]))
            tt(dgs.rearrange("p (a n) -> p a n", a=8), wide(rms[:, 8:16], P), ident.unsqueeze(1).to_broadcast([P, 8, P]), MU)\
                .then_inc(s["diag_ready"], 1)
            merge(0, 1)
            dve.wait_ge(s["inv_mm"], 1)
            for b in range(2):
                tt(yh[:, 2 * b:2 * b + 2, :], orn[:, 512 * b:512 * b + 512].rearrange("p (a n) -> p a n", a=2),
                   ps[6 + b][:, :].rearrange("p (a n) -> p a n", a=2), MU).then_inc(s["yh_ready"], 1)
            for b in range(2, 4):
                merge(0, b)
            for b in range(4):
                link(merge(1, b))
                tt(mrg[:, 2 * b:2 * b + 2, :], mrg[:, 2 * b:2 * b + 2, :], gates[:, KD + 2 * b:KD + 2 * b + 2, :], AD)\
                    .then_inc(s["mrg_ready"], 1)
            def add_mixers(t, b):
                dve.wait_ge(s["wo_mm"], 2 * t + b + 1)
                return tt(x[:, t, 512 * b:512 * b + 512], ps[2 * t + b][:, :], x[:, t, 512 * b:512 * b + 512], AD)

            def second_norm(t):
                link(V.tensor_tensor_reduce(x2[:, t, :], x[:, t, :], x[:, t, :], 1.0, 0.0, MU, AD, small[:, 32 + t:33 + t]))
                ts(small[:, 32 + t:33 + t], small[:, 32 + t:33 + t], 1.0 / D, EPS, MU, AD).then_inc(s["var_in"], 1)
                dve.wait_ge(s["root_out"], 4 + t)
                V.reciprocal(small[:, 34 + t:35 + t], small[:, 32 + t:33 + t]).then_inc(s["inv_ready"], 1)

            def take_parts(t):
                dve.wait_ge(s["parts_mm"], t + 1)
                V.tensor_copy(lgq[:, t, :], ps[t][:, 0:P]).then_inc(s["parts_ready"], 1)

            def sum_parts(t):
                dve.wait_ge(s["logit_mm"], t + 1)
                return V.tensor_reduce(ex[t], ps[4 + 2 * t][:, 0:P].rearrange("p (q e) -> p e q", q=4), AX, AD)

            dve.wait_ge(s["router_w"], 16)
            tt(wrt, wrt, wide(gain2, E), MU).then_inc(s["wrt_ready"], 1)
            for t in range(TT):
                for b in range(2):
                    add_mixers(t, b).then_inc(s["mixed"], 1)
                dve.wait_ge(s["mixed"], 2 * t + 2)
                if t == 1:
                    take_parts(0)
                second_norm(t)
            sum_parts(0)
            take_parts(1)
            dve.wait_ge(s["inv_ready"], TT)
            dve.wait_ge(s["router_b"], 16)
            link(sum_parts(1))
            both = range(TT)
            link([stt(lg[t], ex[t], small[:, 34 + t:35 + t], brt, MU, AD) for t in both][-1])
            def picks(w):
                for t in range(TT):
                    last = ts(pick[:, t, :], iota_s, islot[:, t, bass.ds(w, 1)], None, ALU.is_equal)
                return last

            link([V.max(mx[t], lg[t]) for t in both][-1])
            for t in both:
                ts(nmx[t], mx[t][:, 0:1], -1.0, None, MU).then_inc(s["logits_in"], 1)
            link([V.max_index(ix[:, t, :], mx[t], lg[t]) for t in both][-1])
            link([V.tensor_copy(ixf[t], ix[:, t, 0:TOPK]) for t in both][-1])
            link([ts(mask[t], iota_e, ixf[t][:, 0:1], None, ALU.is_equal) for t in both][-1])
            for k in range(1, TOPK):
                last = [stt(mask[t], iota_e, ixf[t][:, k:k + 1], mask[t], ALU.is_equal, AD) for t in both][-1]
                if k < TOPK - 1:
                    link(last)
            last.then_inc(s["mask_ready"], 1)
            dve.wait_ge(s["mask_ready"], 1)
            dve.wait_ge(s["exped"], TT)
            link([tt(ex[t], ex[t], mask[t], MU) for t in both][-1])
            link([V.tensor_reduce(den[t], ex[t], AX, AD) for t in both][-1])
            link([V.reciprocal(den[t], den[t]) for t in both][-1])
            for t in both:
                ts(wt[t], ex[t], den[t], None, MU)
            dve.wait_ge(s["rank_mm"], 1)
            link([stt(slot[t], mask[t], 4096.0, ps[t][:, 0:E], MU, AD) for t in both][-1])
            for t in both:
                last = ts(slot[t], slot[t], -4096.0, None, AD)
            last.then_inc(s["slot_ready"], 1)
            dve.wait_ge(s["slot_ready"], 1)
            picks(0).then_inc(s["pick_ready"], 1)
            link(V.tensor_copy(cnt, ps[2][0:E, 0:1]))
            link(ts(cx, cnt, float(SLOTS), None, ALU.is_gt))
            for j in (2, 3):
                ins = stt(cx, cnt, float(SLOTS * j), cx, ALU.is_gt, AD)
                if j == 2:
                    link(ins)
            ins.then_inc(s["cnt_ready"], 1)
            V.memset(neg, -float(SLOTS))
            V.memset(oh[:, ITEMS:ITEMS + 2], 0.0)
            V.memset(islot[:, :, ITEMS:ITEMS + 2], 0.0)
            V.memset(iwt[:, :, ITEMS:ITEMS + 2], 0.0)
            V.tensor_copy(oh[:, 0:E], ident[0:E, 0:E]).then_inc(s["h_done"], 1)
            V.tensor_copy(idx[0:1, 0:E], iota_e[0:1, :]).then_inc(s["added1"], 1)
            dve.wait_ge(s["start_mm"], 1)
            V.tensor_copy(first, ps[2][0:E, 1:2])
            link(ts(half[:, 0:1], ps[2][0:1, 2:3], 0.5, 0.25, MU, AD))
            link(ts(half[:, 0:1], half[:, 0:1], MAGIC, None, AD))
            link(ts(half[:, 0:1], half[:, 0:1], MAGIC, None, SU))
            ts(idx[0:1, ITEMS + 2:ITEMS + 3], half[:, 0:1], float(E // 2), None, AD)
            ts(idx[0:1, ITEMS + 3:ITEMS + 4], half[:, 0:1], 2.0, float(E - LATE - 2), MU, AD)
            ts(idx[0:1, ITEMS:ITEMS + 1], half[:, 0:1], 2.0, float(E), MU, AD).then_inc(s["count_ready"], 1)
            js, ja, jb = j3[:, 0:EXTRA], j3[:, 16:32], j3[:, 32:48]
            link(ts(js, iota_e[0:E, 0:EXTRA], first, None, SU))
            ts(ja, js, 0.0, None, ALU.is_ge)
            link(ts(jb, js, cx, None, ALU.is_lt))
            link(tt(oh[:, E:ITEMS], ja, jb, MU))
            link(ts(js, js, 1.0, None, AD))
            tt(ohc, js, oh[:, E:ITEMS], MU)
            dve.wait_ge(s["tr_mm"], 1)
            V.tensor_copy(slT, ps[7][0:E, 0:SEQ])
            V.tensor_copy(wtT, ps[7][0:E, SEQ:2 * SEQ]).then_inc(s["oh_ready"], 1)
            V.memset(pickw, 0.0).then_inc(s["w_pickw"], 1)
            V.memset(ysl, 0.0).then_inc(s["ysl_ready"], 1)

            def take_gathered(w):
                dve.wait_ge(s["gathered"], w + 1)
                tt(xgT, ps[3][:, :].rearrange("p (a n) -> p a n", a=KD), wide(gain2, SLOTS), MU).then_inc(s["xg_ready"], 1)

            def add_item(w, t):
                dve.wait_ge(s[("comb0", "comb1")[t]], w + 1)
                for b in range(2):
                    last = tt(x[:, t, 512 * b:512 * b + 512], ps[(6, 4)[t] + b][:, :], x[:, t, 512 * b:512 * b + 512], AD)
                last.then_inc(s[("added0", "added1")[t]], 1)

            def expert_of(w):
                return V.tensor_copy(ohb[0:E, :], oh[:, bass.ds(w, 1)].to_broadcast([E, SLOTS]))

            dve.wait_ge(s["pad_zero"], 1)
            expert_of(0).then_inc(s["ohb_ready"], 1)
            take_gathered(0)
            dve.wait_ge(s["item_mm"], 1)
            V.tensor_copy(idx[0:1, E:ITEMS], ps[7][0:1, 0:EXTRA]).then_inc(s["idx_ready"], 1)
            for t in range(TT):
                V.tensor_copy(islot[:, t, E:ITEMS], ps[6][:, P * t:P * t + EXTRA])
                last = V.tensor_copy(iwt[:, t, E:ITEMS], ps[6][:, P * t + 64:P * t + 64 + EXTRA])
            last.then_inc(s["added0"], 1)
            dve.wait_ge(s["added0"], 1)
            n_items = dve.value_load(idx[0:1, ITEMS:ITEMS + 1], min_val=E, max_val=ITEMS)
            with dve.Fori(0, n_items) as w:
                picks(w + 1).then_inc(s["pick_ready"], 1)
                dve.wait_ge(s["piece_used"], w * PIECES + KD)
                ts(gt, ps[0][:, :], LIMIT, None, ALU.min).then_inc(s["gate_in"], 1)
                ts(up, ps[1][:, :], LIMIT, -LIMIT, ALU.min, ALU.max).then_inc(s["w_gate"], 1)
                dve.wait_ge(s["w_gate"], w + 1)
                stt(up, up, 1.0, gt, AD, MU).then_inc(s["w_up"], 1)
                dve.wait_ge(s["w_up"], w + 1)
                dve.wait_ge(s["gate_sg"], w + 1)
                tt(up, up, sgm, MU).then_inc(s["h_done"], 1)
                dve.wait_ge(s["h_turned"], w + 1)
                V.tensor_copy(hT, ps[3][:, :].rearrange("p (a b c) -> p a b c", a=4, b=2)).then_inc(s["hT_ready"], 1)
                add_item(w, 0)
                add_item(w, 1)
                dve.wait_ge(s["ct_mm"], w + 1)
                for t in range(TT):
                    for h in range(2):
                        last = ts(pickw[:, t, h, :], iota_s, islot[:, t, bass.ds(w, 1)], iwt[:, t, bass.ds(w, 1)],
                                  ALU.is_equal, MU)
                last.then_inc(s["w_pickw"], 1)
                dve.wait_ge(s["ohb_used"], w + 1)
                expert_of(w + 1).then_inc(s["ohb_ready"], 1)
                take_gathered(w + 1)
            add_item(n_items, 0)
            add_item(n_items, 1)
            dve.wait_ge(s["added1"], n_items + 2)
            dve.wait_ge(s["lastgain"], 16)
            for t in range(TT):
                link(V.tensor_tensor_reduce(x2[:, t, :], x[:, t, :], x[:, t, :], 1.0, 0.0, MU, AD, small[:, 40 + t:41 + t]))
                ts(small[:, 40 + t:41 + t], small[:, 40 + t:41 + t], 1.0 / D, EPS, MU, AD).then_inc(s["var_in"], 1)
                dve.wait_ge(s["root_out"], 6 + t)
                link(V.reciprocal(small[:, 42 + t:43 + t], small[:, 40 + t:41 + t]))
                stt(x2[:, t, :], x[:, t, :], small[:, 42 + t:43 + t], fgain, MU, MU).then_inc(s["w_last"], 1)


_INS = ["x", "meta_tokens", "norm1_gain", "w_in", "s5_lambda_re", "s5_lambda_im", "s5_log_dt", "s5_b_re",
        "s5_b_im", "s5_c_re", "s5_c_im", "s5_d", "s5_w_glu", "hgrn_lb_logits", "hgrn_norm_gain", "w_branch_s5",
        "w_branch_hgrn", "w_out", "norm2_gain", "w_router", "b_router", "w_gate_up", "b_gate_up", "w_down",
        "b_down", "final_norm_gain"]


def kernel(**inputs):
    import concourse.bacc as bacc
    from concourse.bass_utils import run_bass_kernel_spmd

    nc = bacc.Bacc("TRN2", target_bir_lowering=False, num_devices=1)
    arrays = {n: np.ascontiguousarray(inputs[n]) for n in _INS}
    arrays["shape_consts"] = shape_constants()
    feeds, views = {}, {}
    for n, v in arrays.items():
        feeds[f"in_{n}"] = v
        views[n] = nc.dram_tensor(f"in_{n}", v.shape, mybir.dt.from_np(v.dtype), kind="ExternalInput").ap()
    out = nc.dram_tensor("out_0", (1, SEQ, D), F32, kind="ExternalOutput").ap()
    build(nc, views, out)
    r = run_bass_kernel_spmd(nc, [feeds], core_ids=[0])
    return r.results[0]["out_0"]
```
